# Optimizing a Trainium2 kernel written in Bass

```python
import math
import jax
import jax.numpy as jnp
from jax import lax
import numpy as np
import jax, jax.numpy as jnp

D_MODEL = 1024
BATCH = 1
SEQ = 1024
DEPTH = 2

CHUNK = 64
N_MIXERS = 2
CONV_WIDTH = 4
EPS = 1e-6

D_RNN = D_MODEL
LRU_BLOCKS = 8
LRU_BLOCK_W = D_RNN // LRU_BLOCKS
RG_C = 8.0

GDN_HEAD_DIM = 128
GDN_HEADS = max(4, D_MODEL // GDN_HEAD_DIM)
GDN_DK = GDN_HEAD_DIM
GDN_DV = GDN_HEAD_DIM
GDN_HK = GDN_HEADS * GDN_DK
GDN_HV = GDN_HEADS * GDN_DV
GDN_PROJ = 2 * GDN_HK + 2 * GDN_HV + 2 * GDN_HEADS


def rmsnorm(x, g):
    xf = x.astype(jnp.float32)
    y = xf * lax.rsqrt(jnp.mean(xf * xf, axis=-1, keepdims=True) + EPS)
    return (y * g.astype(jnp.float32)).astype(x.dtype)

def l2norm(x):
    return x * lax.rsqrt(jnp.sum(x * x, axis=-1, keepdims=True) + EPS)

def causal_dwconv(x, w):
    k = w.shape[0]
    s = x.shape[1]
    xp = jnp.pad(x, ((0, 0), (k - 1, 0), (0, 0)))
    out = xp[:, 0:s] * w[0]
    for j in range(1, k):
        out = out + xp[:, j:j + s] * w[j]
    return out

def _lin_combine(e1, e2):
    a1, b1 = e1
    a2, b2 = e2
    return a1 * a2, a2 * b1 + b2

def rglru_block(h, in_w, conv_w, conv_b, gate_w, gate_b, lam, out_w):
    bsz, s, _ = h.shape
    proj = h @ in_w
    xb, zg = proj[..., :D_RNN], proj[..., D_RNN:]
    xb = causal_dwconv(xb, conv_w) + conv_b
    xf = xb.astype(jnp.float32)
    xg = xf.reshape(bsz, s, LRU_BLOCKS, LRU_BLOCK_W)
    pre = jnp.einsum('bsni,knij->kbsnj', xg, gate_w.astype(jnp.float32))
    pre = pre.reshape(2, bsz, s, D_RNN) + gate_b.astype(jnp.float32)[:, None, None, :]
    gates = jax.nn.sigmoid(pre)
    r_t, i_t = gates[0], gates[1]
    log_a = -RG_C * r_t * jax.nn.softplus(-lam.astype(jnp.float32))
    a_t = jnp.exp(log_a)
    mult = jnp.sqrt(-jnp.expm1(2.0 * log_a))
    b_t = mult * (i_t * xf)
    _, hseq = lax.associative_scan(_lin_combine, (a_t, b_t), axis=1)
    y = hseq.astype(h.dtype) * jax.nn.silu(zg)
    return y @ out_w

def chunk_gated_delta_rule(q, k, v, g, beta):
    bsz, s, nh, dk = q.shape
    dv = v.shape[-1]
    n = s // CHUNK

    def to_chunks(t):
        return t.reshape(bsz, n, CHUNK, nh, -1).transpose(0, 3, 1, 2, 4)

    q, k, v = to_chunks(q), to_chunks(k), to_chunks(v)
    g = g.reshape(bsz, n, CHUNK, nh).transpose(0, 3, 1, 2)
    beta = beta.reshape(bsz, n, CHUNK, nh).transpose(0, 3, 1, 2)
    g = jnp.cumsum(g, axis=-1)
    idx = jnp.arange(CHUNK)
    causal = idx[:, None] >= idx[None, :]
    strict = idx[:, None] > idx[None, :]
    diff = g[..., :, None] - g[..., None, :]
    decay_mask = jnp.exp(jnp.where(causal, diff, -jnp.inf))
    k_beta = k * beta[..., None]
    v_beta = v * beta[..., None]
    a_mat = jnp.where(strict, jnp.einsum('bhncd,bhnmd->bhncm', k_beta, k) * decay_mask, 0.0)
    eye = jnp.eye(CHUNK, dtype=jnp.float32)
    t_mat = lax.linalg.triangular_solve(a_mat + eye, jnp.broadcast_to(eye, a_mat.shape),
                                        left_side=True, lower=True)
    w = jnp.einsum('bhncm,bhnmd->bhncd', t_mat, k_beta * jnp.exp(g)[..., None])
    u = jnp.einsum('bhncm,bhnmd->bhncd', t_mat, v_beta)
    attn = jnp.where(causal, jnp.einsum('bhncd,bhnmd->bhncm', q, k) * decay_mask, 0.0)
    g_last = g[..., -1]
    q_dec = q * jnp.exp(g)[..., None]
    k_dec = k * jnp.exp(g_last[..., None] - g)[..., None]
    e_last = jnp.exp(g_last)

    def step(state, inp):
        w_c, u_c, attn_c, q_c, k_c, e_c = inp
        v_new = u_c - jnp.einsum('bhcd,bhde->bhce', w_c, state)
        o_c = jnp.einsum('bhcd,bhde->bhce', q_c, state) + jnp.einsum('bhcm,bhme->bhce', attn_c, v_new)
        state = state * e_c[..., None, None] + jnp.einsum('bhcd,bhce->bhde', k_c, v_new)
        return state, o_c

    def lead(t):
        return jnp.moveaxis(t, 2, 0)

    s0 = jnp.zeros((bsz, nh, dk, dv), jnp.float32)
    _, o = lax.scan(step, s0, (lead(w), lead(u), lead(attn), lead(q_dec), lead(k_dec), lead(e_last)))
    return o.transpose(1, 0, 3, 2, 4).reshape(bsz, s, nh, dv)

def gated_deltanet_block(h, in_w, conv_w, a_log, dt_bias, onorm_g, out_w):
    bsz, s, _ = h.shape
    proj = h @ in_w
    o1 = 2 * GDN_HK + GDN_HV
    o2 = o1 + GDN_HV
    qkv = jax.nn.silu(causal_dwconv(proj[..., :o1], conv_w))
    z = proj[..., o1:o2]
    a_in = proj[..., o2:o2 + GDN_HEADS]
    b_in = proj[..., o2 + GDN_HEADS:]
    qkv = qkv.astype(jnp.float32)
    q = qkv[..., :GDN_HK].reshape(bsz, s, GDN_HEADS, GDN_DK)
    k = qkv[..., GDN_HK:2 * GDN_HK].reshape(bsz, s, GDN_HEADS, GDN_DK)
    v = qkv[..., 2 * GDN_HK:].reshape(bsz, s, GDN_HEADS, GDN_DV)
    q = l2norm(q) * (GDN_DK ** -0.5)
    k = l2norm(k)
    beta = jax.nn.sigmoid(b_in.astype(jnp.float32))
    g = -jnp.exp(a_log.astype(jnp.float32)) * jax.nn.softplus(
        a_in.astype(jnp.float32) + dt_bias.astype(jnp.float32))
    o = chunk_gated_delta_rule(q, k, v, g, beta)
    o = o * lax.rsqrt(jnp.mean(o * o, axis=-1, keepdims=True) + EPS) * onorm_g.astype(jnp.float32)
    o = o.astype(h.dtype) * jax.nn.silu(z.reshape(bsz, s, GDN_HEADS, GDN_DV))
    return o.reshape(bsz, s, GDN_HV) @ out_w

def first_inputs(seed: int = 0) -> dict:
    key = jax.random.key(seed)
    ks = jax.random.split(key, 24)
    n_a = (DEPTH + 1) // 2
    n_b = DEPTH // 2
    f32 = jnp.float32
    nrm = lambda k, shp, sc: jax.random.normal(k, shp, f32) * sc
    x = jax.random.normal(ks[0], (BATCH, SEQ, D_MODEL), f32)
    c = jax.random.normal(ks[1], (BATCH, D_MODEL), f32)
    ada_w = nrm(ks[2], (DEPTH, D_MODEL, 3 * D_MODEL), 0.5 * D_MODEL ** -0.5)
    ada_b = nrm(ks[3], (DEPTH, 3 * D_MODEL), 0.02)
    norm_g = 1.0 + nrm(ks[4], (DEPTH, D_MODEL), 0.02)
    final_g = 1.0 + nrm(ks[5], (D_MODEL,), 0.02)
    lru_in_w = nrm(ks[6], (n_a, D_MODEL, 2 * D_RNN), D_MODEL ** -0.5)
    lru_conv_w = nrm(ks[7], (n_a, CONV_WIDTH, D_RNN), CONV_WIDTH ** -0.5)
    lru_conv_b = nrm(ks[8], (n_a, D_RNN), 0.01)
    lru_gate_w = nrm(ks[9], (n_a, 2, LRU_BLOCKS, LRU_BLOCK_W, LRU_BLOCK_W), LRU_BLOCK_W ** -0.5)
    lru_gate_b = nrm(ks[10], (n_a, 2, D_RNN), 0.01)
    a_target = jax.random.uniform(ks[11], (n_a, D_RNN), f32, 0.9, 0.999)
    s_lam = a_target ** (1.0 / RG_C)
    lru_lambda = jnp.log(s_lam) - jnp.log1p(-s_lam)
    lru_out_w = nrm(ks[12], (n_a, D_RNN, D_MODEL), D_RNN ** -0.5)
    gdn_in_w = nrm(ks[13], (n_b, D_MODEL, GDN_PROJ), D_MODEL ** -0.5)
    gdn_conv_w = nrm(ks[14], (n_b, CONV_WIDTH, 2 * GDN_HK + GDN_HV), CONV_WIDTH ** -0.5)
    gdn_a_log = jnp.log(jax.random.uniform(ks[15], (n_b, GDN_HEADS), f32, 1.0, 16.0))
    dt = jnp.exp(jax.random.uniform(ks[16], (n_b, GDN_HEADS), f32, math.log(1e-3), math.log(1e-1)))
    gdn_dt_bias = dt + jnp.log(-jnp.expm1(-dt))
    gdn_onorm_g = 1.0 + nrm(ks[17], (n_b, GDN_DV), 0.02)
    gdn_out_w = nrm(ks[18], (n_b, GDN_HV, D_MODEL), GDN_HV ** -0.5)
    return {"x": x, "c": c, "ada_w": ada_w, "ada_b": ada_b, "norm_g": norm_g, "final_g": final_g,
            "lru_in_w": lru_in_w, "lru_conv_w": lru_conv_w, "lru_conv_b": lru_conv_b,
            "lru_gate_w": lru_gate_w, "lru_gate_b": lru_gate_b, "lru_lambda": lru_lambda,
            "lru_out_w": lru_out_w,
            "gdn_in_w": gdn_in_w, "gdn_conv_w": gdn_conv_w, "gdn_a_log": gdn_a_log,
            "gdn_dt_bias": gdn_dt_bias, "gdn_onorm_g": gdn_onorm_g, "gdn_out_w": gdn_out_w}

def first_block(x, c, ada_w, ada_b, norm_g, final_g,
              lru_in_w, lru_conv_w, lru_conv_b, lru_gate_w, lru_gate_b, lru_lambda, lru_out_w,
              gdn_in_w, gdn_conv_w, gdn_a_log, gdn_dt_bias, gdn_onorm_g, gdn_out_w):
    c_act = jax.nn.silu(c)
    for i in range(DEPTH):
        cond = c_act @ ada_w[i] + ada_b[i]
        shift = cond[:, None, :D_MODEL]
        scale = cond[:, None, D_MODEL:2 * D_MODEL]
        gate = cond[:, None, 2 * D_MODEL:]
        h = rmsnorm(x, norm_g[i]) * (1.0 + scale) + shift
        j = i // N_MIXERS
        if i % N_MIXERS == 0:
            out = rglru_block(h, lru_in_w[j], lru_conv_w[j], lru_conv_b[j], lru_gate_w[j],
                              lru_gate_b[j], lru_lambda[j], lru_out_w[j])
        else:
            out = gated_deltanet_block(h, gdn_in_w[j], gdn_conv_w[j], gdn_a_log[j],
                                       gdn_dt_bias[j], gdn_onorm_g[j], gdn_out_w[j])
        x = x + gate * out
    return rmsnorm(x, final_g)


DEPTH_2 = 1

CONV_WIDTH_2 = D_MODEL
CONV_SIZE = 31
SSM_WIDTH = D_MODEL // 2
SSM_GROUP = 16
SSM_GROUPS = SSM_WIDTH // SSM_GROUP
SSM_STATE = 64
DT_MIN = 0.001
DT_MAX = 0.1
RMS_EPS = 1e-6
LN_EPS = 1e-5
IN_SPLITS = (2 * CONV_WIDTH_2, CONV_WIDTH_2, SSM_WIDTH, SSM_WIDTH, D_MODEL, D_MODEL)
IN_WIDTH = sum(IN_SPLITS)
IN_OFFSETS = [int(v) for v in np.cumsum(IN_SPLITS)[:-1]]


def rms_norm(x, g):
    xf = x.astype(jnp.float32)
    y = xf * lax.rsqrt(jnp.mean(xf * xf, axis=-1, keepdims=True) + RMS_EPS)
    return (y * g.astype(jnp.float32)).astype(x.dtype)

def layer_norm(x, g, b):
    xf = x.astype(jnp.float32)
    mu = jnp.mean(xf, axis=-1, keepdims=True)
    xc = xf - mu
    var = jnp.mean(xc * xc, axis=-1, keepdims=True)
    y = xc * lax.rsqrt(var + LN_EPS) * g.astype(jnp.float32) + b.astype(jnp.float32)
    return y.astype(x.dtype)

def causal_depthwise_conv(u, w, b):
    c = u.shape[-1]
    y = lax.conv_general_dilated(
        u, w[:, None, :].astype(u.dtype), window_strides=(1,),
        padding=[(CONV_SIZE - 1, 0)],
        dimension_numbers=("NWC", "WIO", "NWC"),
        feature_group_count=c)
    return y + b

def s5_mimo(u, lam_re, lam_im, log_dt, b_re, b_im, c_re, c_im, d):
    bsz, length, _ = u.shape
    f32 = jnp.float32
    uf = u.astype(f32).reshape(bsz, length, SSM_GROUPS, SSM_GROUP)
    dt = jnp.exp(log_dt.astype(f32))[:, None]
    lr = lam_re.astype(f32)
    li = lam_im.astype(f32)
    mag = jnp.exp(lr * dt)
    ar = mag * jnp.cos(li * dt)
    ai = mag * jnp.sin(li * dt)
    den = lr * lr + li * li
    zr = ((ar - 1.0) * lr + ai * li) / den
    zi = (ai * lr - (ar - 1.0) * li) / den
    br = b_re.astype(f32)
    bi = b_im.astype(f32)
    bbar_re = zr[..., None] * br - zi[..., None] * bi
    bbar_im = zr[..., None] * bi + zi[..., None] * br
    bu_re = jnp.einsum("blgh,gph->blgp", uf, bbar_re)
    bu_im = jnp.einsum("blgh,gph->blgp", uf, bbar_im)
    a_re = jnp.broadcast_to(ar, bu_re.shape)
    a_im = jnp.broadcast_to(ai, bu_re.shape)

    def combine(e1, e2):
        a1r, a1i, b1r, b1i = e1
        a2r, a2i, b2r, b2i = e2
        return (a2r * a1r - a2i * a1i,
                a2r * a1i + a2i * a1r,
                a2r * b1r - a2i * b1i + b2r,
                a2r * b1i + a2i * b1r + b2i)

    _, _, s_re, s_im = lax.associative_scan(combine, (a_re, a_im, bu_re, bu_im), axis=1)
    y = (jnp.einsum("blgp,ghp->blgh", s_re, c_re.astype(f32))
         - jnp.einsum("blgp,ghp->blgh", s_im, c_im.astype(f32))
         + d.astype(f32) * uf)
    return y.reshape(bsz, length, SSM_WIDTH).astype(u.dtype)

def hybrid_layer(x, pre_g, w_in, conv_w, conv_b, conv_ln_g, conv_ln_b, w_conv_out,
                 lam_re, lam_im, log_dt, b_re, b_im, c_re, c_im, d,
                 w_glu, b_glu, w_ssm_out, w_out, post_g):
    h = rms_norm(x, pre_g)
    proj = jnp.einsum("bld,de->ble", h, w_in)
    conv_in, z_c, u_s, z_s, g_c, g_s = jnp.split(proj, IN_OFFSETS, axis=-1)
    ca, cb = jnp.split(conv_in, 2, axis=-1)
    cu = ca * jax.nn.sigmoid(cb)
    cu = causal_depthwise_conv(cu, conv_w, conv_b)
    cu = jax.nn.silu(layer_norm(cu, conv_ln_g, conv_ln_b))
    conv_out = jnp.einsum("blc,cd->bld", cu * jax.nn.silu(z_c), w_conv_out)
    y = jax.nn.gelu(s5_mimo(u_s, lam_re, lam_im, log_dt, b_re, b_im, c_re, c_im, d))
    y = y * jax.nn.sigmoid(jnp.einsum("blc,ce->ble", y, w_glu) + b_glu)
    ssm_out = jnp.einsum("blc,cd->bld", y * jax.nn.silu(z_s), w_ssm_out)
    merged = jax.nn.sigmoid(g_c) * conv_out + jax.nn.sigmoid(g_s) * ssm_out
    out = jnp.einsum("bld,de->ble", merged, w_out)
    return x + rms_norm(out, post_g)

def second_inputs(seed: int = 0) -> dict:
    key = jax.random.key(seed)
    ks = jax.random.split(key, 24)
    f32 = jnp.float32
    nrm = lambda k, shape, scale: jax.random.normal(k, shape, f32) * scale
    L, G, P, H = DEPTH_2, SSM_GROUPS, SSM_STATE, SSM_GROUP
    n = jnp.arange(P, dtype=f32)
    log_dt = (jnp.log(DT_MIN) + jax.random.uniform(ks[11], (L, G), f32)
              * (jnp.log(DT_MAX) - jnp.log(DT_MIN)))
    return {
        "x": jax.random.normal(ks[0], (BATCH, SEQ, D_MODEL), f32),
        "pre_norm_gain": 1.0 + nrm(ks[1], (L, D_MODEL), 0.05),
        "w_in": nrm(ks[2], (L, D_MODEL, IN_WIDTH), D_MODEL ** -0.5),
        "conv_w": nrm(ks[3], (L, CONV_SIZE, CONV_WIDTH_2), CONV_SIZE ** -0.5),
        "conv_b": nrm(ks[4], (L, CONV_WIDTH_2), 0.02),
        "conv_ln_gain": 1.0 + nrm(ks[5], (L, CONV_WIDTH_2), 0.05),
        "conv_ln_bias": nrm(ks[6], (L, CONV_WIDTH_2), 0.02),
        "w_conv_out": nrm(ks[7], (L, CONV_WIDTH_2, D_MODEL), CONV_WIDTH_2 ** -0.5),
        "ssm_lambda_re": -0.5 + nrm(ks[8], (L, G, P), 0.01),
        "ssm_lambda_im": jnp.pi * n + nrm(ks[9], (L, G, P), 0.01),
        "ssm_log_dt": log_dt,
        "ssm_b_re": nrm(ks[12], (L, G, P, H), (2.0 * H) ** -0.5),
        "ssm_b_im": nrm(ks[13], (L, G, P, H), (2.0 * H) ** -0.5),
        "ssm_c_re": nrm(ks[14], (L, G, H, P), (2.0 * P) ** -0.5),
        "ssm_c_im": nrm(ks[15], (L, G, H, P), (2.0 * P) ** -0.5),
        "ssm_d": nrm(ks[16], (L, G, H), 1.0),
        "w_ssm_glu": nrm(ks[17], (L, SSM_WIDTH, SSM_WIDTH), SSM_WIDTH ** -0.5),
        "b_ssm_glu": nrm(ks[18], (L, SSM_WIDTH), 0.02),
        "w_ssm_out": nrm(ks[19], (L, SSM_WIDTH, D_MODEL), SSM_WIDTH ** -0.5),
        "w_out": nrm(ks[20], (L, D_MODEL, D_MODEL), D_MODEL ** -0.5),
        "post_norm_gain": 1.0 + nrm(ks[21], (L, D_MODEL), 0.05),
    }

def second_block(x, pre_norm_gain, w_in, conv_w, conv_b, conv_ln_gain, conv_ln_bias, w_conv_out,
              ssm_lambda_re, ssm_lambda_im, ssm_log_dt, ssm_b_re, ssm_b_im, ssm_c_re, ssm_c_im,
              ssm_d, w_ssm_glu, b_ssm_glu, w_ssm_out, w_out, post_norm_gain):
    for l in range(DEPTH_2):
        x = hybrid_layer(x, pre_norm_gain[l], w_in[l], conv_w[l], conv_b[l], conv_ln_gain[l],
                         conv_ln_bias[l], w_conv_out[l], ssm_lambda_re[l], ssm_lambda_im[l],
                         ssm_log_dt[l], ssm_b_re[l], ssm_b_im[l], ssm_c_re[l], ssm_c_im[l],
                         ssm_d[l], w_ssm_glu[l], b_ssm_glu[l], w_ssm_out[l], w_out[l],
                         post_norm_gain[l])
    return x


def setup_inputs(seed=0):
    out = dict(first_inputs(seed))
    for name, value in second_inputs(seed + 1).items():
        if name != "x":
            out[name + "_2"] = value
    return out


def reference(
    x, c, ada_w, ada_b, norm_g, final_g, lru_in_w, lru_conv_w, lru_conv_b, lru_gate_w,
    lru_gate_b, lru_lambda, lru_out_w, gdn_in_w, gdn_conv_w, gdn_a_log, gdn_dt_bias,
    gdn_onorm_g, gdn_out_w, pre_norm_gain_2, w_in_2, conv_w_2, conv_b_2, conv_ln_gain_2,
    conv_ln_bias_2, w_conv_out_2, ssm_lambda_re_2, ssm_lambda_im_2, ssm_log_dt_2, ssm_b_re_2,
    ssm_b_im_2, ssm_c_re_2, ssm_c_im_2, ssm_d_2, w_ssm_glu_2, b_ssm_glu_2, w_ssm_out_2, w_out_2,
    post_norm_gain_2,
):
    x = first_block(
        x, c, ada_w, ada_b, norm_g, final_g, lru_in_w, lru_conv_w, lru_conv_b, lru_gate_w,
        lru_gate_b, lru_lambda, lru_out_w, gdn_in_w, gdn_conv_w, gdn_a_log, gdn_dt_bias,
        gdn_onorm_g, gdn_out_w,
    )
    return second_block(
        x, pre_norm_gain_2, w_in_2, conv_w_2, conv_b_2, conv_ln_gain_2, conv_ln_bias_2,
        w_conv_out_2, ssm_lambda_re_2, ssm_lambda_im_2, ssm_log_dt_2, ssm_b_re_2, ssm_b_im_2,
        ssm_c_re_2, ssm_c_im_2, ssm_d_2, w_ssm_glu_2, b_ssm_glu_2, w_ssm_out_2, w_out_2,
        post_norm_gain_2,
    )


_drawn_inputs = setup_inputs


def setup_inputs(seed=0):
    import zlib

    import numpy as np

    out = dict(_drawn_inputs(seed))
    spreads = {}
    factors = {'norm_g': 4.73,
     'lru_conv_b': 4.232,
     'lru_gate_b': 8.0,
     'gdn_a_log': 3.14,
     'gdn_onorm_g': 8.0,
     'conv_ln_bias_2': 4.792,
     'ssm_lambda_re_2': 8.0,
     'ssm_b_re_2': 3.293,
     'ssm_b_im_2': 3.282,
     'ssm_c_re_2': 3.234,
     'ssm_c_im_2': 3.263,
     'b_ssm_glu_2': 8.0}
    for name, (base, spread) in spreads.items():
        noise = np.random.default_rng([zlib.crc32(name.encode()), seed]).standard_normal(out[name].shape)
        drawn = base * np.exp(spread * noise) if base else spread * noise
        out[name] = jnp.asarray(drawn.astype(out[name].dtype))
    for name, factor in factors.items():
        out[name] = (out[name] * factor).astype(out[name].dtype)
    return out
```

```python
import math
from contextlib import ExitStack

import concourse.bass as bass
import numpy as np
from concourse import mybir
from concourse.alu_op_type import AluOpType as ALU

ACT = mybir.ActivationFunctionType
AX = mybir.AxisListType
F32 = mybir.dt.float32

P = 128
D = 1024
S = 1024
KT = D // P
TT = S // P
HALF = 512
HEADS = 8
CH = P
NCH = S // CH
TAPS4 = 4
TAPS31 = 31
EPS = 1e-6
LN_EPS = 1e-5
RG_C = 8.0
GDN_Z = 4 * D
GROUPS = 32
PAIRS = GROUPS // 2
NS = 64
GH = 16
BLK = P // GH
NBLK = S // BLK
MASKED = -1.0e30


class Steps:

    def __init__(self, sem, names):
        self.sem, self.names = sem, names
        self.at = {n: k + 1 for k, n in enumerate(names)}
        assert len(self.at) == len(names)
        self.next = 0

    def ready(self, eng):
        eng.sem_inc(self.sem, len(self.names))

    def mark(self, ins, name):
        assert self.names[self.next] == name, (name, self.names[self.next])
        self.next = (self.next + 1) % len(self.names)
        ins.then_inc(self.sem, 1)

    def wait(self, eng, name, body=0, back=0):
        eng.wait_ge(self.sem, (body + 1 - back) * len(self.names) + self.at[name])


def block_program(nc, a, out):
    ctx = ExitStack()

    with ctx:
        def sem(name):
            return ctx.enter_context(nc.semaphore(name))

        def sb(name, shape, scope=ctx):
            return scope.enter_context(nc.sbuf_tensor(name, shape, F32))

        bank = ctx.enter_context(nc.psum_tensor("bank", [P, 8, HALF], F32))
        ident = sb("ident", [P, P])
        ones = sb("ones", [P, P])
        resid = sb("resid", [P, TT, D])
        hT = sb("hT", [P, KT, S])
        yT = sb("yT", [P, KT, S])
        ring = sb("ring", [P, 4, KT, P])
        vecs = sb("vecs", [P, 5, P])
        cond = sb("cond", [P, 2, 2 * KT])
        layers = ctx.enter_context(ExitStack())
        gate_b = sb("gate_b", [P, 2, D], layers)
        w_loaded = [sem(f"w_loaded{b}") for b in range(4)]
        quads = [0]

        def pair(n):
            return bank[:, 2 * n:2 * n + 2, :].rearrange("p a c -> p (a c)")

        VEC = {}

        def vec(name, k, n=1):
            tile, at = VEC[name]
            return vecs[:, tile, bass.ds(at + k, n)]

        def load_quad(sp, pe, body, tiles):
            for b, (dst, src) in enumerate(tiles):
                pe.wait(sp, f"tile{b}", body, back=1)
                sp.dma_start(dst, src).then_inc(w_loaded[b], 16)

        def columns(w, n, kt=KT):
            return w.rearrange("(k p) c -> p k c", p=P)[:, :, bass.ts(n, P)]

        def project(b, src, kt=KT):
            for h in range(2):
                for k in range(kt):
                    last = nc.tensor.matmul(bank[:, 2 * (b % 2) + h, :], ring[:, b, k, :],
                                            src[:, k, h * HALF:(h + 1) * HALF],
                                            start=(k == 0), stop=(k == kt - 1))
            return last

        def linker(eng, s):
            count = [0]

            def link(ins):
                count[0] += 1
                ins.then_inc(s, 1)
                eng.wait_ge(s, count[0])
            return link

        rows = [
            [("norm_g0", a["norm_g"][0]), ("norm_g1", a["norm_g"][1]), ("conv_b", a["lru_conv_b"][0]),
             ("gate_b0", a["lru_gate_b"][0, 0]), ("gate_b1", a["lru_gate_b"][0, 1]), ("lam", a["lru_lambda"][0]),
             ("ada_b0", a["ada_b"][0, 0:2 * D]), ("ada_b1", a["ada_b"][1, 0:2 * D])],
            [("conv_b2", a["conv_b_2"][0]), ("ln_g", a["conv_ln_gain_2"][0]), ("ln_b", a["conv_ln_bias_2"][0]),
             ("glu_b", a["b_ssm_glu_2"][0]), ("pre_g", a["pre_norm_gain_2"][0]), ("c", a["c"][0]),
             ("onorm", a["gdn_onorm_g"][0])] + [(f"lru_conv{j}", a["lru_conv_w"][0, j]) for j in range(TAPS4)],
            [(f"gdn_conv{j}", a["gdn_conv_w"][0, j]) for j in range(TAPS4)],
            [(f"conv31_{j}", a["conv_w_2"][0, j]) for j in range(16)],
            [(f"conv31_{j}", a["conv_w_2"][0, j]) for j in range(16, TAPS31)],
        ]
        with ExitStack() as scope:
            row_tiles = sb("row_tiles", [P, 5, P], scope)
            c_act = sb("c_act", [P, KT], scope)
            c_wide = sb("c_wide", [P, KT, P], scope)
            ada = sb("ada", [P, 2, KT, HALF], scope)
            gate_bias = sb("gate_bias", [P, 2, D], scope)
            rows_loaded, biases_loaded = sem("rows_loaded"), sem("biases_loaded")
            ada_loaded = [sem("ada_loaded0"), sem("ada_loaded1")]
            x_loaded = sem("x_loaded")
            pool = Steps(sem("setup_pool"), ["ident0", "ident", "ones", "row0"])
            pe_s = Steps(sem("setup_pe"), ["rows_flipped"])
            act_s = Steps(sem("setup_act"), ["vecs", "c_act"])
            dve_s = Steps(sem("setup_dve"), ["c_wide", "cond0"])
            pe_c = Steps(sem("cond_pe"), [f"chunk{q}" for q in range(6)])
            dve_c = Steps(sem("cond_dve"), ["gate0", "gate1", "cond"])

            counts = []
            for tile, vectors in enumerate(rows):
                at = 0
                for name, v in vectors:
                    VEC[name] = (tile, at)
                    at += v.shape[0] // P
                assert at <= P
                counts.append(at)
            n_rows = sum(len(r) for r in rows)

            with nc.Block() as block:
                @block.sync
                def _(sp):
                    sp.dma_start(resid[:, :, :], a["x"][0].rearrange("(t p) c -> p t c", p=P)).then_inc(x_loaded, 16)
                    with sp.Fori(0, 2) as layer:
                        for q in range(6):
                            pe_c.wait(sp, f"chunk{q - 2}" if q >= 2 else f"chunk{q + 4}", layer, back=int(q < 2))
                            src = a["ada_w"][layer].rearrange("(k p) c -> p k c", p=P)
                            sp.dma_start(ada[:, q % 2, :, :], src[:, :, q * HALF:(q + 1) * HALF]) \
                                .then_inc(ada_loaded[q % 2], 16)
                    sp.wait_ge(x_loaded, 16)

                @block.gpsimd
                def _(g):
                    pool.ready(g)
                    pool.mark(g.memset(ident[:, :], 0.0), "ident0")
                    pool.wait(g, "ident0")
                    pool.mark(g.affine_select(out=ident[:, :], in_=ident[:, :], compare_op=ALU.not_equal, fill=1.0,
                                              base=0, pattern=[[-1, P]], channel_multiplier=1), "ident")
                    pool.mark(g.memset(ones[:, :], 1.0), "ones")
                    pool.mark(g.memset(row_tiles[:, :, :], 0.0), "row0")

                @block.scalar
                def _(act):
                    act_s.ready(act)
                    pool.wait(act, "row0")
                    for tile, vectors in enumerate(rows):
                        for name, v in vectors:
                            at = VEC[name][1]
                            act.dma_start(row_tiles[at:at + v.shape[0] // P, tile, :],
                                          v.rearrange("(k p) -> k p", p=P)).then_inc(rows_loaded, 16)
                    for layer in range(2):
                        act.dma_start(gate_bias[:, layer, :],
                                      a["ada_b"][layer, 2 * D:3 * D].partition_broadcast(P)).then_inc(biases_loaded, 16)
                    pe_s.wait(act, "rows_flipped")
                    act.activation(vecs[:, 4, :], bank[:, 1, 0:P], ACT.Copy)
                    act_s.mark(act.activation(vecs[:, 0:4, :].rearrange("p t c -> p (t c)"), bank[:, 0, :], ACT.Copy),
                               "vecs")
                    act_s.wait(act, "vecs")
                    act_s.mark(act.activation(c_act[:, :], vec("c", 0, KT), ACT.Silu), "c_act")

                @block.tensor
                def _(pe):
                    pe_s.ready(pe)
                    pe_c.ready(pe)
                    pool.wait(pe, "row0")
                    pe.wait_ge(rows_loaded, 16 * n_rows)
                    for tile in range(5):
                        last = nc.tensor.transpose(bank[:, tile // 4, (tile % 4) * P:(tile % 4 + 1) * P],
                                                   row_tiles[:, tile, :], ident[:, :])
                    pe_s.mark(last, "rows_flipped")
                    dve_s.wait(pe, "c_wide")
                    with pe.Fori(0, 2) as layer:
                        for q in range(6):
                            pe.wait_ge(ada_loaded[q % 2], (layer * 3 + q // 2 + 1) * 16)
                            if q == 0:
                                dve_c.wait(pe, "cond", layer, back=1)
                            if q < 4:
                                for m in range(4):
                                    for k in range(KT):
                                        last = nc.tensor.matmul(bank[:, 2, 4 * q + m:4 * q + m + 1],
                                                                ada[:, q % 2, k, m * P:(m + 1) * P], c_act[:, k:k + 1],
                                                                start=(k == 0), stop=(k == KT - 1))
                            else:
                                for k in range(KT):
                                    last = nc.tensor.matmul(bank[:, q, :], c_wide[:, k, :], ada[:, q % 2, k, :],
                                                            start=(k == 0), stop=(k == KT - 1))
                            pe_c.mark(last, f"chunk{q}")

                @block.vector
                def _(dve):
                    dve_s.ready(dve)
                    dve_c.ready(dve)
                    act_s.wait(dve, "c_act")
                    dve_s.mark(dve.tensor_copy(c_wide[:, :, :], c_act[:, :].unsqueeze(2).broadcast_to([P, KT, P])), "c_wide")
                    dve.wait_ge(biases_loaded, 32)
                    with dve.Fori(0, 2) as layer:
                        for q in range(2):
                            pe_c.wait(dve, f"chunk{4 + q}", layer)
                            dve_c.mark(dve.tensor_tensor(gate_b[:, layer, q * HALF:(q + 1) * HALF], bank[:, 4 + q, :],
                                                         gate_bias[:, layer, q * HALF:(q + 1) * HALF], ALU.add), f"gate{q}")
                        dve_c.mark(dve.tensor_copy(cond[:, layer, :], bank[:, 2, 0:2 * KT]), "cond")
                    dve_c.wait(dve, "cond", 1)
                    for layer in range(2):
                        ins = dve.tensor_tensor(cond[:, layer, :], cond[:, layer, :], vec(f"ada_b{layer}", 0, 2 * KT), ALU.add)
                    dve_s.mark(ins, "cond0")
                    dve_s.wait(dve, "cond0")
                    for layer in range(2):
                        dve.scalar_tensor_tensor(out=cond[:, layer, KT:2 * KT], in0=cond[:, layer, KT:2 * KT], scalar=1.0,
                                                 in1=vec(f"norm_g{layer}", 0, KT), op0=ALU.add, op1=ALU.mult)

        def norm_transpose(name, scale, shift, before=None):
            with ExitStack() as scope:
                junk = sb(f"{name}_junk", [P, D], scope)
                normed = sb(f"{name}_normed", [P, 2, D], scope)
                stat = sb(f"{name}_stat", [P, 2, 4], scope)
                eps = sb(f"{name}_eps", [P, 1], scope)
                gain = sb(f"{name}_gain", [P, D], scope) if before is not None else None
                gain_loaded = sem(f"{name}_gain_loaded") if before is not None else None
                first = ["sq0_", "rms0_"] if before is not None else []
                act_n = Steps(sem(f"{name}_act"), [s + str(p) for p in range(2) for s in first + ["sq", "rms", "low"]])
                firstd = ["inv0_", "res", "kept"] if before is not None else []
                dve_n = Steps(sem(f"{name}_dve"), [s + str(p) for p in range(2) for s in firstd + ["inv", "normed", "high"]])
                pe_n = Steps(sem(f"{name}_pe"), ["flip0", "flip1"])
                pool_n = Steps(sem(f"{name}_pool"), ["eps"])
                with nc.Block() as block:
                    @block.gpsimd
                    def _(g):
                        pool_n.ready(g)
                        pool_n.mark(g.memset(eps[:, :], EPS), "eps")
                        if before is not None:
                            g.dma_start(gain[:, :], before.partition_broadcast(P)).then_inc(gain_loaded, 16)
                            g.wait_ge(gain_loaded, 16)

                    @block.scalar
                    def _(act):
                        act_n.ready(act)
                        pool_n.wait(act, "eps")
                        with act.Fori(0, TT // 2) as i:
                            for p in range(2):
                                x_t = resid[:, i * 2 + p, :]
                                if before is not None:
                                    act_n.mark(act.activation(junk[:, :], x_t, ACT.Square, accum_out=stat[:, p, 0:1]), f"sq0_{p}")
                                    act_n.wait(act, f"sq0_{p}", i)
                                    act_n.mark(act.activation(stat[:, p, 1:2], stat[:, p, 0:1], ACT.Sqrt, bias=eps[:, 0:1],
                                                              scale=1.0 / D), f"rms0_{p}")
                                    dve_n.wait(act, f"res{p}", i)
                                    x_t = normed[:, p, :]
                                else:
                                    dve_n.wait(act, f"inv{p}", i, back=1)
                                act_n.mark(act.activation(junk[:, :], x_t, ACT.Square, accum_out=stat[:, p, 2:3]), f"sq{p}")
                                act_n.wait(act, f"sq{p}", i)
                                act_n.mark(act.activation(stat[:, p, 3:4], stat[:, p, 2:3], ACT.Sqrt, bias=eps[:, 0:1],
                                                          scale=1.0 / D), f"rms{p}")
                                pe_n.wait(act, f"flip{p}", i)
                                for k in range(KT // 2):
                                    ins = act.activation(hT[:, k, bass.ts(i * 2 + p, P)], bank[:, 2 * p, k * P:(k + 1) * P],
                                                         ACT.Identity, scale=scale(k), bias=shift(k))
                                act_n.mark(ins, f"low{p}")

                    @block.vector
                    def _(dve):
                        dve_n.ready(dve)
                        if before is not None:
                            dve.wait_ge(gain_loaded, 16)
                        with dve.Fori(0, TT // 2) as i:
                            for p in range(2):
                                x_t = resid[:, i * 2 + p, :]
                                if before is not None:
                                    act_n.wait(dve, f"rms0_{p}", i)
                                    dve_n.mark(dve.reciprocal(stat[:, p, 1:2], stat[:, p, 1:2]), f"inv0_{p}")
                                    dve_n.wait(dve, f"inv0_{p}", i)
                                    pe_n.wait(dve, f"flip{p}", i, back=1)
                                    dve_n.mark(dve.scalar_tensor_tensor(out=normed[:, p, :], in0=x_t, scalar=stat[:, p, 1:2], in1=gain[:, :],
                                                                        op0=ALU.mult, op1=ALU.mult), f"res{p}")
                                    dve_n.wait(dve, f"res{p}", i)
                                    dve_n.mark(dve.tensor_scalar(x_t, normed[:, p, :], 1.0, None, ALU.mult), f"kept{p}")
                                    x_t = normed[:, p, :]
                                act_n.wait(dve, f"rms{p}", i)
                                dve_n.mark(dve.reciprocal(stat[:, p, 3:4], stat[:, p, 3:4]), f"inv{p}")
                                dve_n.wait(dve, f"inv{p}", i)
                                pe_n.wait(dve, f"flip{p}", i, back=1)
                                dve_n.mark(dve.tensor_scalar(normed[:, p, :], x_t, stat[:, p, 3:4], None, ALU.mult), f"normed{p}")
                                pe_n.wait(dve, f"flip{p}", i)
                                for k in range(KT // 2):
                                    ins = dve.tensor_scalar(hT[:, KT // 2 + k, bass.ts(i * 2 + p, P)],
                                                            bank[:, 2 * p + 1, k * P:(k + 1) * P],
                                                            scale(KT // 2 + k), shift(KT // 2 + k), ALU.mult, ALU.add)
                                dve_n.mark(ins, f"high{p}")

                    @block.tensor
                    def _(pe):
                        pe_n.ready(pe)
                        with pe.Fori(0, TT // 2) as i:
                            for p in range(2):
                                dve_n.wait(pe, f"normed{p}", i)
                                act_n.wait(pe, f"low{p}", i, back=1)
                                dve_n.wait(pe, f"high{p}", i, back=1)
                                for k in range(KT):
                                    last = nc.tensor.transpose(bank[:, 2 * p + k // 4, (k % 4) * P:(k % 4 + 1) * P],
                                                               normed[:, p, k * P:(k + 1) * P], ident[:, :])
                                pe_n.mark(last, f"flip{p}")

        def project_out(name, w, layer):
            with ExitStack() as scope:
                w_out = sb(f"{name}_w", [P, KT, 2, HALF], scope)
                gated = sb(f"{name}_gated", [P, 2, HALF], scope)
                loaded = [sem(f"{name}_loaded0"), sem(f"{name}_loaded1")]
                pe_o = Steps(sem(f"{name}_pe"), [f"tok{t}" for t in range(TT)])
                dve_o = Steps(sem(f"{name}_dve"), [f"{s}{t}" for t in range(TT) for s in ("gated", "added")])
                with nc.Block() as block:
                    @block.sync
                    def _(sp):
                        for c in range(2):
                            sp.dma_start(w_out[:, :, c, :], w.rearrange("(k p) (h c) -> p k h c", p=P, h=2)[:, :, c, :]) \
                                .then_inc(loaded[c], 16)

                    @block.tensor
                    def _(pe):
                        pe_o.ready(pe)
                        for c in range(2):
                            pe.wait_ge(loaded[c], 16)
                        with pe.Fori(0, 2) as c:
                            for t in range(TT):
                                dve_o.wait(pe, f"gated{t}", c, back=1)
                                for k in range(KT):
                                    last = nc.tensor.matmul(bank[:, t, :], yT[:, k, t * P:(t + 1) * P], w_out[:, k, c, :],
                                                            start=(k == 0), stop=(k == KT - 1))
                                pe_o.mark(last, f"tok{t}")

                    @block.vector
                    def _(dve):
                        dve_o.ready(dve)
                        with dve.Fori(0, 2) as c:
                            for t in range(TT):
                                pe_o.wait(dve, f"tok{t}", c)
                                x_t = resid[:, t, bass.ts(c, HALF)]
                                dve_o.mark(dve.tensor_tensor(gated[:, t % 2, :], bank[:, t, :], gate_b[:, layer, bass.ts(c, HALF)],
                                                             ALU.mult), f"gated{t}")
                                dve_o.wait(dve, f"gated{t}", c)
                                dve_o.mark(dve.tensor_tensor(x_t, x_t, gated[:, t % 2, :], ALU.add), f"added{t}")

        def log1p_steps(dve, link, p, e, z, z2):
            link(dve.tensor_scalar(z, e, 2.0, None, ALU.add))
            link(dve.reciprocal(z, z))
            link(dve.tensor_tensor(z, z, e, ALU.mult))
            link(dve.tensor_tensor(z2, z, z, ALU.mult))
            link(dve.tensor_scalar(p, z2, 1.0 / 19.0, None, ALU.mult))
            for n in range(17, 1, -2):
                link(dve.scalar_tensor_tensor(out=p, in0=p, scalar=1.0 / n, in1=z2, op0=ALU.add, op1=ALU.mult))
            link(dve.scalar_tensor_tensor(out=p, in0=p, scalar=1.0, in1=z, op0=ALU.add, op1=ALU.mult))
            link(dve.tensor_scalar(p, p, 2.0, None, ALU.mult))

        norm_transpose("norm0", lambda k: cond[:, 0, KT + k:KT + k + 1], lambda k: cond[:, 0, k:k + 1])

        with ExitStack() as scope:
            PAD = TAPS4 - 1
            rate = sb("rate", [P, KT], scope)
            nrate = sb("nrate", [P, KT], scope)
            small = sb("lru_small", [P, 5, KT], scope)
            padded = sb("padded", [P, 2, PAD + S], scope)
            conv = sb("conv", [P, 2, S], scope)
            gw = sb("gw", [P, 2, 2, P], scope)
            gate_r = sb("gate_r", [P, S], scope)
            gate_i = sb("gate_i", [P, S], scope)
            sig_z = sb("sig_z", [P, 2, S], scope)
            tau = sb("tau", [P, S], scope)
            decay = sb("decay", [P, S], scope)
            mult = sb("mult", [P, S], scope)
            inp = sb("inp", [P, S], scope)
            state = sb("state", [P, S], scope)
            gw_loaded = [sem("gw_loaded0"), sem("gw_loaded1")]
            pe_l = Steps(sem("lru_pe"), ["tile0", "tile1", "gates0", "tile2", "tile3", "gates1"])
            act_names = ["x_in", "sig_z", "gate_r", "gate_i", "tau", "decay", "decay2", "mult"]
            act_l = Steps(sem("lru_act"), [s + str(p) for p in range(2) for s in act_names])
            dve_names = ["c0_", "c1_", "c2_", "conv", "sz", "ix", "m2", "b", "scan", "y"]
            dve_l = Steps(sem("lru_dve"), [s + str(p) for p in range(2) for s in dve_names])
            chain, e_ready = sem("lru_chain"), sem("lru_e_ready")
            pad_zero = sem("lru_pad_zero")
            q0 = quads[0]
            quads[0] += KT // 2

            with nc.Block() as block:
                @block.sync
                def _(sp):
                    w = a["lru_in_w"][0]
                    with sp.Fori(0, KT // 2) as i:
                        load_quad(sp, pe_l, i, [(ring[:, 2 * p + z, :, :], columns(w, i * 2 + (z * KT + p)))
                                                for p in range(2) for z in range(2)])

                @block.gpsimd
                def _(g):
                    g.memset(padded[:, :, 0:PAD], 0.0).then_inc(pad_zero, 1)
                    with g.Fori(0, KT // 2) as i:
                        for p in range(2):
                            pe_l.wait(g, f"gates{p}", i, back=1)
                            g.dma_start(gw[:, p, :, :], a["lru_gate_w"][0].rearrange("g n i j -> n i g j")[i * 2 + p]) \
                                .then_inc(gw_loaded[p], 16)

                @block.tensor
                def _(pe):
                    pe_l.ready(pe)

                    def gates(i, p):
                        pe.wait_ge(gw_loaded[p], (i + 1) * 16)
                        dve_l.wait(pe, f"conv{p}", i)
                        act_l.wait(pe, f"gate_i{1 - p}", i, back=int(p == 0))
                        for g in range(2):
                            for h in range(2):
                                last = nc.tensor.matmul(bank[:, 4 + 2 * g + h, :], gw[:, p, g, :],
                                                        conv[:, p, h * HALF:(h + 1) * HALF], start=True, stop=True)
                        pe_l.mark(last, f"gates{p}")

                    with pe.Fori(0, KT // 2) as i:
                        for b in range(4):
                            pe.wait_ge(w_loaded[b], (i + (q0 + 1)) * 16)
                            if b % 2 == 0:
                                act_l.wait(pe, f"x_in{1 - b // 2}", i, back=int(b == 0))
                            else:
                                dve_l.wait(pe, f"sz{1 - b // 2}", i, back=int(b == 1))
                            pe_l.mark(project(b, hT), f"tile{b}")
                            if b % 2 == 1:
                                gates(i, b // 2)

                @block.scalar
                def _(act):
                    act_l.ready(act)
                    act.activation(small[:, 0, :], vec("lam", 0, KT), ACT.Abs).then_inc(e_ready, 1)
                    act.wait_ge(e_ready, 1)
                    act.activation(small[:, 1, :], small[:, 0, :], ACT.Exp, scale=-1.0).then_inc(e_ready, 1)
                    act.wait_ge(pad_zero, 1)
                    act.wait_ge(chain, 17)
                    with act.Fori(0, KT // 2) as i:
                        for p in range(2):
                            n = i * 2 + p
                            pe_l.wait(act, f"tile{2 * p}", i)
                            dve_l.wait(act, f"conv{p}", i, back=1)
                            act_l.mark(act.activation(padded[:, p, PAD:], pair(0), ACT.Copy), f"x_in{p}")
                            pe_l.wait(act, f"tile{2 * p + 1}", i)
                            act_l.mark(act.activation(sig_z[:, p, :], pair(1), ACT.Sigmoid), f"sig_z{p}")
                            pe_l.wait(act, f"gates{p}", i)
                            act_l.mark(act.activation(gate_r[:, :], pair(2), ACT.Sigmoid, bias=vec("gate_b0", n)), f"gate_r{p}")
                            dve_l.wait(act, f"ix{1 - p}", i, back=int(p == 0))
                            act_l.mark(act.activation(gate_i[:, :], pair(3), ACT.Sigmoid, bias=vec("gate_b1", n)), f"gate_i{p}")
                            act_l.wait(act, f"gate_r{p}", i)
                            dve_l.wait(act, f"m2{1 - p}", i, back=int(p == 0))
                            act_l.mark(act.activation(tau[:, :], gate_r[:, :], ACT.Tanh, scale=nrate[:, bass.ds(n, 1)]), f"tau{p}")
                            dve_l.wait(act, f"scan{1 - p}", i, back=int(p == 0))
                            act_l.mark(act.activation(decay[:, :], gate_r[:, :], ACT.Exp, scale=rate[:, bass.ds(n, 1)]), f"decay{p}")
                            act_l.wait(act, f"decay{p}", i)
                            act_l.mark(act.activation(mult[:, :], decay[:, :], ACT.Square), f"decay2{p}")
                            dve_l.wait(act, f"m2{p}", i)
                            act_l.mark(act.activation(mult[:, :], mult[:, :], ACT.Sqrt), f"mult{p}")

                @block.vector
                def _(dve):
                    dve_l.ready(dve)
                    link = linker(dve, chain)
                    dve.wait_ge(e_ready, 2)
                    log1p_steps(dve, link, small[:, 2, :], small[:, 1, :], small[:, 3, :], small[:, 4, :])
                    link(dve.tensor_scalar(small[:, 0, :], vec("lam", 0, KT), -1.0, 0.0, ALU.mult, ALU.max))
                    link(dve.tensor_tensor(small[:, 2, :], small[:, 2, :], small[:, 0, :], ALU.add))
                    dve.tensor_scalar(rate[:, :], small[:, 2, :], -RG_C, None, ALU.mult)
                    link(dve.tensor_scalar(nrate[:, :], small[:, 2, :], RG_C, None, ALU.mult))
                    with dve.Fori(0, KT // 2) as i:
                        for p in range(2):
                            n = i * 2 + p
                            acc = conv[:, p, :]
                            act_l.wait(dve, f"x_in{p}", i)
                            pe_l.wait(dve, f"gates{p}", i, back=1)
                            dve_l.mark(dve.tensor_scalar(acc, padded[:, p, 0:S], vec("lru_conv0", n), vec("conv_b", n),
                                                         ALU.mult, ALU.add), f"c0_{p}")
                            for j in range(1, TAPS4):
                                dve_l.wait(dve, f"c{j - 1}_{p}", i)
                                dve_l.mark(dve.scalar_tensor_tensor(out=acc, in0=padded[:, p, j:j + S], scalar=vec(f"lru_conv{j}", n),
                                                                    in1=acc, op0=ALU.mult, op1=ALU.add),
                                           f"c{j}_{p}" if j < TAPS4 - 1 else f"conv{p}")
                            act_l.wait(dve, f"sig_z{p}", i)
                            dve_l.mark(dve.tensor_tensor(sig_z[:, p, :], pair(1), sig_z[:, p, :], ALU.mult), f"sz{p}")
                            act_l.wait(dve, f"gate_i{p}", i)
                            dve_l.mark(dve.tensor_tensor(inp[:, :], gate_i[:, :], acc, ALU.mult), f"ix{p}")
                            act_l.wait(dve, f"decay2{p}", i)
                            dve_l.mark(dve.scalar_tensor_tensor(out=mult[:, :], in0=mult[:, :], scalar=1.0, in1=tau[:, :],
                                                                op0=ALU.add, op1=ALU.mult), f"m2{p}")
                            act_l.wait(dve, f"mult{p}", i)
                            dve_l.mark(dve.tensor_tensor(inp[:, :], inp[:, :], mult[:, :], ALU.mult), f"b{p}")
                            dve_l.wait(dve, f"b{p}", i)
                            dve_l.mark(dve.tensor_tensor_scan(state[:, :], decay[:, :], inp[:, :], 0.0, ALU.mult, ALU.add), f"scan{p}")
                            dve_l.wait(dve, f"scan{p}", i)
                            dve_l.mark(dve.tensor_tensor(yT[:, n, :], state[:, :], sig_z[:, p, :], ALU.mult), f"y{p}")
        project_out("out0", a["lru_out_w"][0], 0)
        norm_transpose("norm1", lambda k: cond[:, 1, KT + k:KT + k + 1], lambda k: cond[:, 1, k:k + 1])

        with ExitStack() as scope:
            levels = [1 << s for s in range(7)]
            cols = {n: sb(f"col_{n}", [P, HEADS, NCH], scope)
                    for n in ("g", "beta", "exp_g", "exp_rest", "exp_last", "neg_beta_exp_g")}
            level_mask = sb("level_mask", [P, len(levels), P], scope)
            causal = sb("causal", [P, P], scope)

            with ExitStack() as inner:
                w_ab = sb("w_ab", [P, KT, 2 * HEADS], inner)
                tri = sb("tri", [P, P], inner)
                last_row = sb("last_row", [P, P], inner)
                dt_bias = sb("dt_bias", [P, HEADS], inner)
                neg_a = sb("neg_a", [P, HEADS], inner)
                a_in = sb("a_in", [P, HEADS, NCH], inner)
                step = sb("step", [P, HEADS, NCH], inner)
                tmp = [sb(f"ab_tmp{n}", [P, HEADS, NCH], inner) for n in range(5)]
                ab_loaded, row_loaded = sem("ab_loaded"), sem("ab_row_loaded")
                pe_a = Steps(sem("ab_pe"), ["ab", "cum", "last"])
                act_a = Steps(sem("ab_act"), ["neg_a", "beta", "abs", "exp", "exp_g", "exp_last", "exp_rest"])
                dve_a = Steps(sem("ab_dve"), ["a_in", "g_step", "g", "rest", "neg"])
                pool_a = Steps(sem("ab_pool"), ["fill", "masks"])
                chain = sem("ab_chain")
                pool_chain = sem("ab_pool_chain")
                with nc.Block() as block:
                    @block.sync
                    def _(sp):
                        sp.dma_start(w_ab[:, :, :], a["gdn_in_w"][0].rearrange("(k p) c -> p k c", p=P)[:, :, GDN_Z:]) \
                            .then_inc(ab_loaded, 16)
                        sp.dma_start(dt_bias[:, :], a["gdn_dt_bias"][0].partition_broadcast(P)).then_inc(row_loaded, 16)
                        sp.dma_start(neg_a[:, :], a["gdn_a_log"][0].partition_broadcast(P)).then_inc(row_loaded, 16)

                    @block.gpsimd
                    def _(g):
                        pool_a.ready(g)
                        link = linker(g, pool_chain)

                        def select(m, pattern, base, mult, fill, op=ALU.is_ge):
                            link(g.affine_select(out=m, in_=m, compare_op=op, fill=fill, base=base, pattern=pattern,
                                                 channel_multiplier=mult))

                        g.memset(tri[:, :], 1.0)
                        g.memset(causal[:, :], 0.0)
                        g.memset(last_row[:, :], 1.0)
                        pool_a.mark(g.memset(level_mask[:, :, :], 1.0), "fill")
                        pool_a.wait(g, "fill")
                        select(tri[:, :], [[1, P]], 0, -1, 0.0)
                        select(causal[:, :], [[1, P]], 0, -1, MASKED)
                        select(last_row[:, :], [[0, P]], -(P - 1), 1, 0.0)
                        for n, s in enumerate(levels):
                            nb = P // (2 * s)
                            m = level_mask[:, n, :].rearrange("p (b r e) -> p b r e", r=2, e=s)
                            select(m, [[0, nb], [1, 2], [0, s]], -1, 0, 0.0)
                            select(m, [[-2 * s, nb], [0, 2], [0, s]], 0, 1, 0.0)
                            select(m, [[2 * s, nb], [0, 2], [0, s]], s - 1, -1, 0.0)
                        pool_a.mark(g.memset(a_in[:, :, :], 0.0), "masks")

                    @block.tensor
                    def _(pe):
                        pe_a.ready(pe)
                        pe.wait_ge(ab_loaded, 16)
                        for t in range(TT):
                            for k in range(KT):
                                last = nc.tensor.matmul(bank[:, 4, t * 16:t * 16 + 16], hT[:, k, t * P:(t + 1) * P], w_ab[:, k, :],
                                                        start=(k == 0), stop=(k == KT - 1))
                        pe_a.mark(last, "ab")
                        pool_a.wait(pe, "masks")
                        dve_a.wait(pe, "g_step")
                        pe_a.mark(nc.tensor.matmul(bank[:, 5, 0:HEADS * NCH], tri[:, :], step[:, :, :].rearrange("p h c -> p (h c)"),
                                                   start=True, stop=True), "cum")
                        dve_a.wait(pe, "g")
                        pe_a.mark(nc.tensor.matmul(bank[:, 6, 0:HEADS * NCH], last_row[:, :],
                                                   cols["g"][:, :, :].rearrange("p h c -> p (h c)"), start=True, stop=True), "last")

                    @block.scalar
                    def _(act):
                        act_a.ready(act)
                        ab = bank[:, 4, 0:P].rearrange("p (t x h) -> p x h t", x=2, h=HEADS)
                        act.wait_ge(row_loaded, 32)
                        act_a.mark(act.activation(neg_a[:, :], neg_a[:, :], ACT.Exp), "neg_a")
                        pe_a.wait(act, "ab")
                        act_a.mark(act.activation(cols["beta"][:, :, :], ab[:, 1], ACT.Sigmoid), "beta")
                        dve_a.wait(act, "a_in")
                        act_a.mark(act.activation(tmp[0][:, :, :], a_in[:, :, :], ACT.Abs), "abs")
                        act_a.wait(act, "abs")
                        act_a.mark(act.activation(tmp[1][:, :, :], tmp[0][:, :, :], ACT.Exp, scale=-1.0), "exp")
                        dve_a.wait(act, "g")
                        act_a.mark(act.activation(cols["exp_g"][:, :, :], cols["g"][:, :, :], ACT.Exp), "exp_g")
                        pe_a.wait(act, "last")
                        act_a.mark(act.activation(cols["exp_last"][:, :, :],
                                                  bank[:, 6, 0:HEADS * NCH].rearrange("p (h c) -> p h c", h=HEADS), ACT.Exp), "exp_last")
                        dve_a.wait(act, "rest")
                        act_a.mark(act.activation(cols["exp_rest"][:, :, :], tmp[2][:, :, :], ACT.Exp), "exp_rest")

                    @block.vector
                    def _(dve):
                        dve_a.ready(dve)
                        link = linker(dve, chain)
                        ab = bank[:, 4, 0:P].rearrange("p (t x h) -> p x h t", x=2, h=HEADS)
                        dve.wait_ge(row_loaded, 32)
                        pool_a.wait(dve, "masks")
                        pe_a.wait(dve, "ab")
                        act_a.wait(dve, "beta")
                        dve_a.mark(dve.tensor_tensor(a_in[:, :, :], ab[:, 0], dt_bias[:, :].unsqueeze(2).broadcast_to([P, HEADS, NCH]),
                                                     ALU.add), "a_in")
                        act_a.wait(dve, "exp")
                        log1p_steps(dve, link, tmp[2][:, :, :], tmp[1][:, :, :], tmp[3][:, :, :], tmp[4][:, :, :])
                        link(dve.scalar_tensor_tensor(out=tmp[2][:, :, :], in0=a_in[:, :, :], scalar=0.0, in1=tmp[2][:, :, :],
                                                      op0=ALU.max, op1=ALU.add))
                        act_a.wait(dve, "neg_a")
                        dve_a.mark(dve.scalar_tensor_tensor(out=step[:, :, :], in0=tmp[2][:, :, :], scalar=-1.0,
                                                            in1=neg_a[:, :].unsqueeze(2).broadcast_to([P, HEADS, NCH]),
                                                            op0=ALU.mult, op1=ALU.mult), "g_step")
                        pe_a.wait(dve, "cum")
                        dve_a.mark(dve.tensor_copy(cols["g"][:, :, :], bank[:, 5, 0:HEADS * NCH].rearrange("p (h c) -> p h c", h=HEADS)), "g")
                        pe_a.wait(dve, "last")
                        act_a.wait(dve, "exp_last")
                        dve_a.wait(dve, "g")
                        dve_a.mark(dve.tensor_tensor(tmp[2][:, :, :], bank[:, 6, 0:HEADS * NCH].rearrange("p (h c) -> p h c", h=HEADS),
                                                     cols["g"][:, :, :], ALU.subtract), "rest")
                        act_a.wait(dve, "exp_g")
                        dve_a.mark(dve.scalar_tensor_tensor(out=cols["neg_beta_exp_g"][:, :, :], in0=cols["beta"][:, :, :], scalar=-1.0,
                                                            in1=cols["exp_g"][:, :, :], op0=ALU.mult, op1=ALU.mult), "neg")

            PAD = TAPS4 - 1
            padded = sb("qkv_padded", [P, 3, PAD + S], scope)
            tok_shape = [P, NCH, P]
            cq, ck, cv = (sb(n, [P, S], scope) for n in ("cq", "ck", "cv"))
            silu_z = sb("silu_z", [P, S], scope)
            k_tok, k_rest, v_tok, buf_a, buf_b, buf_c = (sb(n, tok_shape, scope) for n in ("k_tok", "k_rest", "v_tok", "buf_a", "buf_b", "buf_c"))
            kT, kbT, qT, qdT = (sb(n, tok_shape, scope) for n in ("kT", "kbT", "qT", "qdT"))
            decayT, attnT = (sb(n, tok_shape, scope) for n in ("decayT", "attnT"))
            q_tok = cq[:, :].rearrange("p (c d) -> p c d", c=NCH)
            kb_tok = ck[:, :].rearrange("p (c d) -> p c d", c=NCH)
            qd_tok = cv[:, :].rearrange("p (c d) -> p c d", c=NCH)
            AT, inv, invT = buf_a, buf_b, buf_c
            part = [qT, k_tok]
            prod = kbT
            o_tok, o_normed = kb_tok, q_tok
            memory = sb("memory", [P, P], scope)
            delta = sb("delta", [P, 2, P], scope)
            g_col = sb("g_col", [P, NCH], scope)
            stat = sb("gdn_stat", [P, 3, NCH], scope)
            eps2 = sb("gdn_eps", [P, 2], scope)
            hd_pe = Steps(sem("gdn_pe"), ["q", "k", "v", "z", "k_flip", "q_flip", "v_flip", "kT", "kbT", "qT", "qdT", "g_row", "kk", "qk", "Y1"]
                          + [f"{n}{s}" for s in levels[1:] for n in (("Y", "TY", "YT") if s < 64 else ("Y", "YT"))]
                          + [f"{n}{c}" for c in range(NCH) for n in ("read", "new", "mem", "o")] + ["o_flip"])
            hd_act = Steps(sem("gdn_act"), ["q_in", "k_in", "v_in", "z", "k_silu", "q_silu", "v_silu", "k_sq", "k_rms", "q_sq", "q_rms",
                                            "kT", "kbT", "qT", "decay"]
                           + [f"prod{s}" for s in levels[1:]] + [f"{n}{c}" for c in range(NCH) for n in ("new", "o")] + ["o_sq", "o_rms"])
            hd_dve = Steps(sem("gdn_dve"), ["g_col"] + [f"{n}{j}" for n in ("kc", "qc", "vc") for j in range(TAPS4)]
                           + ["k_ss", "k_inv", "k_tok", "q_ss", "q_inv", "q_tok", "v_tok", "qdT", "rel", "AT", "attn", "inv1", "invT1"]
                           + [f"{n}{s}" for s in levels[1:] for n in (("inv", "invT") if s < 64 else ("invT",))]
                           + ["mem_zero"] + [f"{n}{c}" for c in range(NCH) for n in ("delta", "mem")] + ["o_ss", "o_inv", "o_tok", "y"])
            hd_pool = Steps(sem("gdn_pool"), ["kb_tok", "qd_tok", "k_rest", "rel"] + [f"part{s}" for s in levels])
            gdn_zero = sem("gdn_zero")
            q0 = quads[0]
            quads[0] += HEADS
            R4, R5 = pair(2).rearrange("p (c d) -> p c d", c=NCH), pair(3).rearrange("p (c d) -> p c d", c=NCH)

            def per_tok(name, h):
                return cols[name][:, h, :].unsqueeze(2).broadcast_to(tok_shape)

            def along(m):
                return m.unsqueeze(1).broadcast_to(tok_shape)

            with nc.Block() as block:
                @block.sync
                def _(sp):
                    w = a["gdn_in_w"][0].rearrange("(k p) c -> p k c", p=P)
                    with sp.Fori(0, HEADS) as h:
                        for b, name in enumerate(("q", "k", "v", "z")):
                            hd_pe.wait(sp, name, h, back=1)
                            sp.dma_start(ring[:, b, :, :], w[:, :, bass.ts(h + b * HEADS, P)]).then_inc(w_loaded[b], 16)

                @block.gpsimd
                def _(g):
                    hd_pool.ready(g)
                    g.memset(padded[:, :, 0:PAD], 0.0).then_inc(gdn_zero, 1)
                    g.memset(eps2[:, 0:1], EPS).then_inc(gdn_zero, 1)
                    g.memset(eps2[:, 1:2], EPS * P).then_inc(gdn_zero, 1)
                    with g.Fori(0, HEADS) as h:
                        hd_dve.wait(g, "k_tok", h)
                        hd_pe.wait(g, "k_flip", h)
                        hd_pool.mark(g.tensor_tensor(kb_tok, k_tok[:, :, :], per_tok("beta", h), ALU.mult), "kb_tok")
                        hd_dve.wait(g, "q_tok", h)
                        hd_dve.wait(g, "v_tok", h)
                        hd_pe.wait(g, "v_flip", h)
                        hd_pool.mark(g.tensor_tensor(qd_tok, q_tok, per_tok("exp_g", h), ALU.mult), "qd_tok")
                        hd_pool.mark(g.tensor_tensor(k_rest[:, :, :], k_tok[:, :, :], per_tok("exp_rest", h), ALU.mult), "k_rest")
                        hd_dve.wait(g, "rel", h)
                        hd_pool.mark(g.tensor_tensor(decayT[:, :, :], decayT[:, :, :], along(causal[:, :]), ALU.add), "rel")
                        hd_dve.wait(g, "AT", h)
                        hd_pe.wait(g, "kT", h)
                        hd_pe.wait(g, "qk", h)
                        hd_pool.wait(g, "k_rest", h)
                        for n, s in enumerate(levels):
                            if n >= 2:
                                hd_pe.wait(g, f"Y{levels[n - 2]}", h)
                            if n == 2:
                                hd_dve.wait(g, "invT1", h)
                            hd_pool.mark(g.tensor_tensor(part[n % 2][:, :, :], AT[:, :, :], along(level_mask[:, n, :]), ALU.mult), f"part{s}")

                @block.tensor
                def _(pe):
                    hd_pe.ready(pe)

                    def each(dst, lhs, rhs, name):
                        for c in range(NCH):
                            last = nc.tensor.matmul(dst[:, c, :], lhs(c), rhs(c), start=True, stop=True)
                        hd_pe.mark(last, name)

                    def flip(dst, src, name):
                        for c in range(NCH):
                            last = nc.tensor.transpose(dst[:, c, :], src(c), ident[:, :])
                        hd_pe.mark(last, name)

                    with pe.Fori(0, HEADS) as h:
                        for b, name in enumerate(("q", "k", "v", "z")):
                            pe.wait_ge(w_loaded[b], (h + (q0 + 1)) * 16)
                            if b < 2:
                                hd_act.wait(pe, ("v_in", "z")[b], h, back=1)
                            else:
                                hd_act.wait(pe, ("q_in", "k_in")[b - 2], h)
                            hd_pe.mark(project(b, hT), name)
                        hd_act.wait(pe, "k_silu", h)
                        hd_dve.wait(pe, "y", h, back=1)
                        flip(R4, lambda c: ck[:, c * P:(c + 1) * P], "k_flip")
                        hd_act.wait(pe, "q_silu", h)
                        hd_act.wait(pe, f"o{NCH - 1}", h, back=1)
                        flip(R5, lambda c: cq[:, c * P:(c + 1) * P], "q_flip")
                        hd_act.wait(pe, "v_silu", h)
                        hd_dve.wait(pe, "k_tok", h)
                        hd_act.wait(pe, "k_sq", h)
                        flip(R4, lambda c: cv[:, c * P:(c + 1) * P], "v_flip")
                        hd_dve.wait(pe, "q_tok", h)
                        flip(R5, lambda c: k_tok[:, c, :], "kT")
                        hd_dve.wait(pe, "v_tok", h)
                        hd_pool.wait(pe, "kb_tok", h)
                        flip(R4, lambda c: kb_tok[:, c, :], "kbT")
                        hd_act.wait(pe, "kT", h)
                        flip(R5, lambda c: q_tok[:, c, :], "qT")
                        hd_act.wait(pe, "kbT", h)
                        hd_pool.wait(pe, "qd_tok", h)
                        flip(R4, lambda c: qd_tok[:, c, :], "qdT")
                        hd_act.wait(pe, "qT", h)
                        hd_dve.wait(pe, "g_col", h)
                        for c in range(NCH):
                            last = nc.tensor.matmul(R5[:, c, :], g_col[:, c:c + 1].broadcast_to([P, P]),
                                                    ident[:, :], start=True, stop=True)
                        hd_pe.mark(last, "g_row")
                        hd_dve.wait(pe, "qdT", h)
                        each(R4, lambda c: kT[:, c, :], lambda c: kbT[:, c, :], "kk")
                        hd_dve.wait(pe, "rel", h)
                        each(R5, lambda c: kT[:, c, :], lambda c: qT[:, c, :], "qk")
                        hd_dve.wait(pe, "AT", h)
                        hd_pool.wait(pe, "part1", h)
                        each(R4, lambda c: part[0][:, c, :], lambda c: ident[:, :], "Y1")
                        for n, s in enumerate(levels):
                            if n == 0:
                                continue
                            hd_pool.wait(pe, f"part{s}", h)
                            hd_dve.wait(pe, f"inv{levels[n - 1]}", h)
                            hd_dve.wait(pe, f"invT{levels[n - 1]}", h)
                            each(R4, lambda c: part[n % 2][:, c, :], lambda c: inv[:, c, :], f"Y{s}")
                            hd_act.wait(pe, f"prod{s}", h)
                            if s < 64:
                                if n == 1:
                                    hd_dve.wait(pe, "attn", h)
                                each(R5, lambda c: invT[:, c, :], lambda c: prod[:, c, :], f"TY{s}")
                            each(R4, lambda c: prod[:, c, :], lambda c: invT[:, c, :], f"YT{s}")
                        for c in range(NCH):
                            if c == 0:
                                hd_dve.wait(pe, "invT64", h)
                                hd_dve.wait(pe, "mem_zero", h)
                                hd_dve.wait(pe, "inv32", h)
                            else:
                                hd_dve.wait(pe, f"mem{c - 1}", h)
                            hd_pe.mark(nc.tensor.matmul(R4[:, 0, :], kT[:, c, :], memory[:, :], start=True, stop=True), f"read{c}")
                            hd_dve.wait(pe, f"delta{c}", h)
                            hd_pe.mark(nc.tensor.matmul(R4[:, 4, :], invT[:, c, :], delta[:, 0, :], start=True, stop=True), f"new{c}")
                            hd_act.wait(pe, f"new{c}", h)
                            hd_pool.wait(pe, "k_rest", h)
                            hd_pe.mark(nc.tensor.matmul(R5[:, 0, :], k_rest[:, c, :], delta[:, 1, :], start=True, stop=True), f"mem{c}")
                            if c:
                                hd_act.wait(pe, f"o{c - 1}", h)
                            nc.tensor.matmul(R5[:, 4, :], attnT[:, c, :], delta[:, 1, :], start=True, stop=False)
                            hd_pe.mark(nc.tensor.matmul(R5[:, 4, :], qdT[:, c, :], memory[:, :], start=False, stop=True), f"o{c}")
                        hd_dve.wait(pe, "o_tok", h)
                        flip(R4, lambda c: o_normed[:, c, :], "o_flip")

                @block.scalar
                def _(act):
                    hd_act.ready(act)
                    act.wait_ge(gdn_zero, 3)
                    with act.Fori(0, HEADS) as h:
                        for n, name in enumerate(("q", "k", "v")):
                            hd_pe.wait(act, name, h)
                            hd_dve.wait(act, f"{name}c{TAPS4 - 1}", h, back=1)
                            hd_act.mark(act.activation(padded[:, n, PAD:], pair(n % 2), ACT.Copy), f"{name}_in")
                        hd_pe.wait(act, "z", h)
                        hd_dve.wait(act, "y", h, back=1)
                        hd_act.mark(act.activation(silu_z[:, :], pair(1), ACT.Silu), "z")
                        for name, x in (("k", ck), ("q", cq), ("v", cv)):
                            hd_dve.wait(act, f"{name}c{TAPS4 - 1}", h)
                            hd_act.mark(act.activation(x[:, :], x[:, :], ACT.Silu), f"{name}_silu")
                        for n, (name, r) in enumerate((("k", R4), ("q", R5))):
                            hd_pe.wait(act, f"{name}_flip", h)
                            if n:
                                hd_dve.wait(act, "k_ss", h)
                            else:
                                hd_pe.wait(act, f"o{NCH - 1}", h, back=1)
                            hd_act.mark(act.activation(inv[:, :, :], r, ACT.Square), f"{name}_sq")
                            hd_dve.wait(act, f"{name}_ss", h)
                            hd_act.mark(act.activation(stat[:, n, :], stat[:, n, :], ACT.Sqrt, bias=eps2[:, n:n + 1],
                                                       scale=1.0 if n == 0 else float(P)), f"{name}_rms")
                        for name, r, dst in (("kT", R5, kT), ("kbT", R4, kbT), ("qT", R5, qT)):
                            hd_pe.wait(act, name, h)
                            hd_act.mark(act.activation(dst[:, :, :], r, ACT.Copy), name)
                        hd_pool.wait(act, "rel", h)
                        hd_act.mark(act.activation(decayT[:, :, :], decayT[:, :, :], ACT.Exp), "decay")
                        for n, s in enumerate(levels[1:]):
                            hd_pe.wait(act, f"Y{s}", h)
                            hd_act.mark(act.activation(prod[:, :, :], R4, ACT.Copy), f"prod{s}")
                        for c in range(NCH):
                            hd_pe.wait(act, f"new{c}", h)
                            hd_act.mark(act.activation(delta[:, 1, :], R4[:, 4, :], ACT.Copy), f"new{c}")
                            hd_pe.wait(act, f"o{c}", h)
                            hd_act.mark(act.activation(o_tok[:, c, :], R5[:, 4, :], ACT.Copy), f"o{c}")
                        hd_act.wait(act, f"o{NCH - 1}", h)
                        hd_act.mark(act.activation(inv[:, :, :], o_tok, ACT.Square), "o_sq")
                        hd_dve.wait(act, "o_ss", h)
                        hd_act.mark(act.activation(stat[:, 2, :], stat[:, 2, :], ACT.Sqrt, bias=eps2[:, 0:1], scale=1.0 / P), "o_rms")

                @block.vector
                def _(dve):
                    hd_dve.ready(dve)
                    dve.wait_ge(gdn_zero, 3)

                    def conv4(h, n, name, dst):
                        hd_act.wait(dve, f"{name}_in", h)
                        w = [vec(f"gdn_conv{j}", h + n * HEADS) for j in range(TAPS4)]
                        hd_dve.mark(dve.tensor_scalar(dst[:, :], padded[:, n, 0:S], w[0], None, ALU.mult), f"{name}c0")
                        for j in range(1, TAPS4):
                            hd_dve.wait(dve, f"{name}c{j - 1}", h)
                            hd_dve.mark(dve.scalar_tensor_tensor(out=dst[:, :], in0=padded[:, n, j:j + S], scalar=w[j], in1=dst[:, :],
                                                                 op0=ALU.mult, op1=ALU.add), f"{name}c{j}")

                    def inverse_root(h, n, name):
                        hd_act.wait(dve, f"{name}_sq", h)
                        hd_dve.mark(dve.tensor_reduce(out=stat[:, n, :], in_=inv[:, :, :], op=ALU.add, axis=AX.X), f"{name}_ss")
                        hd_act.wait(dve, f"{name}_rms", h)
                        hd_dve.mark(dve.reciprocal(stat[:, n, :], stat[:, n, :]), f"{name}_inv")
                        hd_dve.wait(dve, f"{name}_inv", h)
                        return stat[:, n, :].unsqueeze(2).broadcast_to(tok_shape)

                    with dve.Fori(0, HEADS) as h:
                        hd_pe.wait(dve, "g_row", h, back=1)
                        hd_dve.mark(dve.tensor_copy(g_col[:, :], cols["g"][:, h, :]), "g_col")
                        conv4(h, 1, "k", ck)
                        conv4(h, 0, "q", cq)
                        conv4(h, 2, "v", cv)
                        by = inverse_root(h, 0, "k")
                        hd_dve.mark(dve.tensor_tensor(k_tok[:, :, :], R4, by, ALU.mult), "k_tok")
                        by = inverse_root(h, 1, "q")
                        hd_dve.mark(dve.tensor_tensor(q_tok, R5, by, ALU.mult), "q_tok")
                        hd_pe.wait(dve, "v_flip", h)
                        hd_dve.mark(dve.tensor_tensor(v_tok[:, :, :], R4, per_tok("beta", h), ALU.mult), "v_tok")
                        hd_pe.wait(dve, "qdT", h)
                        hd_dve.mark(dve.tensor_copy(qdT[:, :, :], R4), "qdT")
                        hd_pe.wait(dve, "g_row", h)
                        hd_dve.mark(dve.tensor_tensor(decayT[:, :, :], R5, per_tok("g", h), ALU.subtract), "rel")
                        hd_act.wait(dve, "decay", h)
                        hd_pe.wait(dve, "kk", h)
                        hd_dve.mark(dve.tensor_tensor(AT[:, :, :], R4, decayT[:, :, :], ALU.mult), "AT")
                        hd_pe.wait(dve, "qk", h)
                        hd_dve.mark(dve.tensor_tensor(attnT[:, :, :], R5, decayT[:, :, :], ALU.mult), "attn")
                        hd_pe.wait(dve, "Y1", h)
                        hd_dve.mark(dve.scalar_tensor_tensor(out=inv[:, :, :], in0=R4, scalar=-1.0, in1=along(ident[:, :]),
                                                             op0=ALU.mult, op1=ALU.add), "inv1")
                        hd_dve.mark(dve.scalar_tensor_tensor(out=invT[:, :, :], in0=part[0][:, :, :], scalar=-1.0, in1=along(ident[:, :]),
                                                             op0=ALU.mult, op1=ALU.add), "invT1")
                        for n, s in enumerate(levels):
                            if n == 0:
                                continue
                            if s < 64:
                                hd_dve.wait(dve, f"inv{levels[n - 1]}", h)
                                hd_pe.wait(dve, f"TY{s}", h)
                                hd_dve.mark(dve.tensor_tensor(inv[:, :, :], inv[:, :, :], R5, ALU.subtract), f"inv{s}")
                            hd_pe.wait(dve, f"YT{s}", h)
                            hd_dve.wait(dve, f"invT{levels[n - 1]}", h)
                            hd_dve.mark(dve.tensor_tensor(invT[:, :, :], invT[:, :, :], R4, ALU.subtract), f"invT{s}")
                        hd_pe.wait(dve, f"o{NCH - 1}", h, back=1)
                        hd_dve.mark(dve.memset(memory[:, :], 0.0), "mem_zero")
                        for c in range(NCH):
                            hd_pe.wait(dve, f"read{c}", h)
                            hd_dve.mark(dve.scalar_tensor_tensor(out=delta[:, 0, :], in0=R4[:, 0, :],
                                                                 scalar=cols["neg_beta_exp_g"][:, h, c:c + 1],
                                                                 in1=v_tok[:, c, :], op0=ALU.mult, op1=ALU.add), f"delta{c}")
                            hd_pe.wait(dve, f"o{c}", h)
                            hd_dve.mark(dve.scalar_tensor_tensor(out=memory[:, :], in0=memory[:, :], scalar=cols["exp_last"][:, h, c:c + 1],
                                                                 in1=R5[:, 0, :], op0=ALU.mult, op1=ALU.add), f"mem{c}")
                        by = inverse_root(h, 2, "o")
                        hd_dve.mark(dve.tensor_tensor(o_normed, o_tok, by, ALU.mult), "o_tok")
                        hd_pe.wait(dve, "o_flip", h)
                        hd_dve.mark(dve.scalar_tensor_tensor(out=yT[:, h, :], in0=pair(2), scalar=vec("onorm", 0), in1=silu_z[:, :],
                                                             op0=ALU.mult, op1=ALU.mult), "y")
        project_out("out1", a["gdn_out_w"][0], 1)

        layers.close()
        norm_transpose("norm2", lambda k: vec("pre_g", k), lambda k: 0.0, before=a["final_g"])
        w_in = a["w_in_2"][0]
        CA, CB, ZC, US, ZS, GC, GS = (c // P for c in (0, D, 2 * D, 3 * D, 3 * D + 512, 4 * D, 5 * D))
        ST = GROUPS * GH // P
        u_dram = nc.dram_tensor("u_scratch", (ST * P, BLK, NBLK), F32, kind="Internal").ap()
        y_dram = nc.dram_tensor("y_scratch", (ST * P, BLK, NBLK), F32, kind="Internal").ap()
        ssm_y = sb("ssm_y", [P, ST, S])

        with ExitStack() as scope:
            u_perm = sb("u_perm", [P, 2, BLK, NBLK], scope)
            pe_u = Steps(sem("u_pe"), [f"tile{b}" for b in range(4)])
            act_u = Steps(sem("u_act"), [f"u{b}" for b in range(4)])
            u_stored = [sem("u_stored0"), sem("u_stored1")]
            q0 = quads[0]
            quads[0] += 1
            with nc.Block() as block:
                @block.sync
                def _(sp):
                    load_quad(sp, pe_u, 0, [(ring[:, b, :, :], columns(w_in, US + b)) for b in range(4)])
                    for b in range(4):
                        act_u.wait(sp, f"u{b}")
                        sp.dma_start(u_dram[b * P:(b + 1) * P], u_perm[:, b % 2, :, :]).then_inc(u_stored[b % 2], 16)
                    for p in range(2):
                        sp.wait_ge(u_stored[p], 32)

                @block.tensor
                def _(pe):
                    pe_u.ready(pe)
                    for b in range(4):
                        pe.wait_ge(w_loaded[b], (q0 + 1) * 16)
                        if b >= 2:
                            act_u.wait(pe, f"u{b - 2}")
                        pe_u.mark(project(b, hT), f"tile{b}")

                @block.scalar
                def _(act):
                    act_u.ready(act)
                    for b in range(4):
                        pe_u.wait(act, f"tile{b}")
                        if b >= 2:
                            act.wait_ge(u_stored[b % 2], 16)
                        act_u.mark(act.activation(u_perm[:, b % 2, :, :], pair(b % 2).rearrange("p (k t) -> p t k", t=BLK), ACT.Copy), f"u{b}")

        with ExitStack() as scope:
            flat = yT[:, :, :].rearrange("p k s -> p (k s)")
            lift = flat[:, 0:4096].rearrange("p (x j t h) -> p x j t h", x=2, j=PAIRS, t=BLK)
            kernel16 = flat[0:GH, 4096:8192].rearrange("p (g c) -> p g c", g=GROUPS)
            u_blk = flat[:, 0:4096].rearrange("p (g k) -> p g k", g=GROUPS)
            HP = PAIRS // 2
            w1, w2, w3, z_re = (flat[:, 4096 + n * 1024:5120 + n * 1024].rearrange("p (j k) -> p j k", j=HP) for n in range(4))
            turn = ring[:, :, :, :].rearrange("p b k c -> p (b k c)").rearrange("p (x j k) -> p x j k", x=2, j=PAIRS)
            turn_re, turn_im = turn[:, 0], turn[:, 1]
            B_lift = sb("B_lift", [P, 2, PAIRS, P], scope)
            C_pow = sb("C_pow", [P, 2, PAIRS, BLK + 1, GH], scope)
            K_lift = sb("K_lift", [P, GROUPS, P], scope)
            shrink = sb("shrink", [P, PAIRS, NBLK], scope)
            z_im = ssm_y[:, 2, :].rearrange("p (j k) -> p j k", j=HP)
            y_blk = ssm_y[:, 0:2, :].rearrange("p c (g k) -> p (c g) k", k=NBLK)
            st_re, st_im = (sb(n, [P, HP, NBLK + 2], scope) for n in ("st_re", "st_im"))
            par = sb("s5_par", [P, 24, PAIRS], scope)
            (lr, li, dt, mag, th, nn, red, co, si, ar, ai, den, zr, zi, x1, x2, c8, s8, rho, ab, ph) = (par[:, n, :] for n in range(21))
            pw = sb("s5_pow", [P, 2, BLK + 1, PAIRS], scope)
            bb = sb("s5_b", [P, 4, PAIRS, GH], scope)
            cc = sb("s5_c", [P, 2, PAIRS, GH], scope)
            c_rows = ssm_y[:, 3, :].rearrange("p (x t g s) -> p x t g s", x=2, t=ST, g=2)
            d16 = sb("s5_d", [GH, 2, PAIRS], scope)
            half_pi = sb("half_pi", [P, 1], scope)
            par_loaded, c_loaded, d_loaded, u_loaded = sem("par_loaded"), sem("c_loaded"), sem("d_loaded"), sem("u_loaded")
            K_placed, y_stored, y_loaded = sem("K_placed"), sem("y_stored"), sem("y_loaded")
            pe_s = Steps(sem("s5_pe"), ["c_flip", "kernel", "B_flip"] + [f"{n}{h}" for h in range(2) for n in ("w", "y")])
            act_s = Steps(sem("s5_act"), ["dt", "mag", "rho", "sin", "cos_abs", "cos", "kernel", "B", "y0", "y1"]
                          + [f"gelu{n}" for n in range(ST)])
            dve_s = Steps(sem("s5_dve"), ["rates", "reduced", "c", "b", "C", "lift", "kernel", "s0", "s1"])
            pool_s = Steps(sem("s5_pool"), ["zero"])
            chain = sem("s5_chain")
            with nc.Block() as block:
                @block.sync
                def _(sp):
                    for g in range(2):
                        half = slice(g * NS, (g + 1) * NS)
                        sp.dma_start(lr[half], a["ssm_lambda_re_2"][0].rearrange("(j g) p -> g p j", g=2)[g], allow_slow_non_contiguous=True).then_inc(par_loaded, 16)
                        sp.dma_start(li[half], a["ssm_lambda_im_2"][0].rearrange("(j g) p -> g p j", g=2)[g], allow_slow_non_contiguous=True).then_inc(par_loaded, 16)
                        sp.dma_start(dt[half], a["ssm_log_dt_2"][0].rearrange("(j g) -> g j", g=2)[g].partition_broadcast(NS), allow_slow_non_contiguous=True).then_inc(par_loaded, 16)
                        for x, n in enumerate(("ssm_b_re_2", "ssm_b_im_2")):
                            sp.dma_start(bb[half, x], a[n][0].rearrange("(j g) p h -> g p j h", g=2)[g]).then_inc(par_loaded, 16)
                        for x, n in enumerate(("ssm_c_re_2", "ssm_c_im_2")):
                            sp.dma_start(c_rows[:, x, :, g, :], a[n][0].rearrange("(t r) h p -> (r h) t p", t=ST)).then_inc(c_loaded, 16)
                        sp.dma_start(d16[:, g, :], a["ssm_d_2"][0].rearrange("(j g) h -> g h j", g=2)[g],
                                     allow_slow_non_contiguous=True).then_inc(d_loaded, 16)
                    dve_s.wait(sp, "kernel")
                    pool_s.wait(sp, "zero")
                    for r in range(BLK):
                        sp.dma_start(K_lift[r * GH:(r + 1) * GH, :, (BLK - 1 - r) * GH:], kernel16[:, :, 0:(r + 1) * GH]).then_inc(K_placed, 16)
                    pe_s.wait(sp, "B_flip")
                    for t in range(BLK):
                        sp.dma_start(u_blk[(BLK - 1 - t) * GH:(BLK - t) * GH, :, :],
                                     u_dram.rearrange("(g h) t k -> t h g k", h=GH)[t]).then_inc(u_loaded, 16)
                    for h in range(2):
                        act_s.wait(sp, f"y{h}")
                        for t in range(BLK):
                            for g in range(2):
                                sp.dma_start(y_dram.rearrange("(j g h) t k -> t g h j k", h=GH, g=2)[t, g][:, h * HP:(h + 1) * HP, :],
                                             y_blk[t * GH:(t + 1) * GH, g * HP:(g + 1) * HP, :]).then_inc(y_stored, 16)
                        sp.wait_ge(y_stored, (h + 1) * 2 * BLK * 16)
                    sp.dma_start(flat[:, 4096:8192].rearrange("p (c x) -> p c x", c=ST),
                                 y_dram.rearrange("(c p) t k -> p c (t k)", p=P)).then_inc(y_loaded, 16)
                    sp.wait_ge(y_loaded, 16)

                @block.gpsimd
                def _(g):
                    pool_s.ready(g)
                    g.memset(half_pi[:, :], math.pi / 2)
                    g.memset(st_re[:, :, 0:1], 0.0)
                    g.memset(st_im[:, :, 0:1], 0.0)
                    pool_s.mark(g.memset(K_lift[:, :, :], 0.0), "zero")

                @block.tensor
                def _(pe):
                    pe_s.ready(pe)
                    pe.wait_ge(c_loaded, 64)
                    for x in range(2):
                        for t in range(ST):
                            last = nc.tensor.transpose(bank[:, x, t * P:(t + 1) * P], c_rows[:, x, t, :, :].rearrange("p g s -> p (g s)"), ident[:, :])
                    pe_s.mark(last, "c_flip")
                    dve_s.wait(pe, "C")
                    dve_s.wait(pe, "b")
                    for n in range(GROUPS):
                        g, j = n % 2, n // 2
                        half = slice(g * NS, (g + 1) * NS)
                        dst = bank[0:GH, 4 * g + j // 4, (j % 4) * P:(j % 4 + 1) * P]
                        for x in range(2):
                            last = nc.tensor.matmul(dst, bb[half, 2 + x, j, :], C_pow[half, x, j, 0:BLK, :].rearrange("p t h -> p (t h)"),
                                                    start=(x == 0), stop=(x == 1))
                    pe_s.mark(last, "kernel")
                    dve_s.wait(pe, "lift")
                    act_s.wait(pe, "kernel")
                    for x in range(2):
                        for j in range(PAIRS):
                            last = nc.tensor.transpose(bank[:, 4 * x + j // 4, (j % 4) * P:(j % 4 + 1) * P],
                                                       lift[:, x, j].rearrange("p t h -> p (t h)"), ident[:, :])
                    pe_s.mark(last, "B_flip")
                    act_s.wait(pe, "B")
                    pe.wait_ge(u_loaded, BLK * 16)
                    pe.wait_ge(K_placed, BLK * 16)
                    for h in range(2):
                        if h:
                            dve_s.wait(pe, "s0")
                        for x in range(2):
                            for jl in range(HP):
                                for g in range(2):
                                    j = h * HP + jl
                                    last = nc.tensor.matmul(bank[g * NS:(g + 1) * NS, 2 * x + jl // 4, (jl % 4) * P:(jl % 4 + 1) * P],
                                                            B_lift[:, x, j, g * NS:(g + 1) * NS], u_blk[:, 2 * j + g, :], start=True, stop=True)
                        pe_s.mark(last, f"w{h}")
                        dve_s.wait(pe, f"s{h}")
                        if h:
                            act_s.wait(pe, "y0")
                        for n in range(2 * HP):
                            g, jl = n % 2, n // 2
                            half, j = slice(g * NS, (g + 1) * NS), h * HP + jl
                            dst = bank[:, 4 + 2 * g + jl // 4, (jl % 4) * P:(jl % 4 + 1) * P]
                            nc.tensor.matmul(dst, K_lift[:, g * PAIRS + j, :], u_blk[:, 2 * j + g, :], start=True, stop=False)
                            nc.tensor.matmul(dst, C_pow[half, 0, j, 1:, :].rearrange("p t h -> p (t h)"), st_re[half, jl, 0:NBLK], start=False, stop=False)
                            last = nc.tensor.matmul(dst, C_pow[half, 1, j, 1:, :].rearrange("p t h -> p (t h)"), st_im[half, jl, 0:NBLK],
                                                    start=False, stop=True)
                        pe_s.mark(last, f"y{h}")

                @block.scalar
                def _(act):
                    act_s.ready(act)
                    act.wait_ge(par_loaded, 160)
                    act_s.mark(act.activation(dt, dt, ACT.Exp), "dt")
                    dve_s.wait(act, "rates")
                    act_s.mark(act.activation(mag, x1, ACT.Exp), "mag")
                    act_s.mark(act.activation(rho, x1, ACT.Exp, scale=float(BLK)), "rho")
                    pool_s.wait(act, "zero")
                    dve_s.wait(act, "reduced")
                    act_s.mark(act.activation(si, red, ACT.Sin), "sin")
                    act_s.mark(act.activation(ab, red, ACT.Abs), "cos_abs")
                    act_s.wait(act, "cos_abs")
                    act_s.mark(act.activation(co, ab, ACT.Sin, scale=-1.0, bias=half_pi[:, 0:1]), "cos")
                    pe_s.wait(act, "kernel")
                    dve_s.wait(act, "lift")
                    act_s.mark(act.activation(kernel16.rearrange("p g c -> p (g c)"), bank[0:GH, :, :].rearrange("p b c -> p (b c)"), ACT.Copy), "kernel")
                    pe_s.wait(act, "B_flip")
                    act_s.mark(act.activation(B_lift[:, :, :, :].rearrange("p x j c -> p (x j c)"), bank[:, :, :].rearrange("p b c -> p (b c)"), ACT.Copy), "B")
                    for h in range(2):
                        pe_s.wait(act, f"y{h}")
                        if h:
                            act.wait_ge(y_stored, 2 * BLK * 16)
                        act_s.mark(act.activation(y_blk[:, :, :].rearrange("p g k -> p (g k)"), bank[:, 4:8, :].rearrange("p b c -> p (b c)"), ACT.Copy), f"y{h}")
                    act.wait_ge(y_loaded, 16)
                    for n in range(ST):
                        act_s.mark(act.activation(ssm_y[:, n, :].rearrange("p (k t) -> p t k", t=BLK),
                                                  flat[:, 4096 + n * S:4096 + (n + 1) * S].rearrange("p (t k) -> p t k", t=BLK),
                                                  ACT.Gelu_apprx_tanh), f"gelu{n}")

                @block.vector
                def _(dve):
                    dve_s.ready(dve)
                    link = linker(dve, chain)
                    TT_, TS, STT = dve.tensor_tensor, dve.tensor_scalar, dve.scalar_tensor_tensor

                    def cmul(out_re, out_im, xr, xi, yr, yi, t):
                        TT_(t[0], xr, yr, ALU.mult)
                        link(TT_(t[1], xi, yi, ALU.mult))
                        link(TT_(out_re, t[0], t[1], ALU.subtract))
                        TT_(t[0], xr, yi, ALU.mult)
                        link(TT_(t[1], xi, yr, ALU.mult))
                        link(TT_(out_im, t[0], t[1], ALU.add))

                    act_s.wait(dve, "dt")
                    link(TT_(th, li, dt, ALU.mult))
                    dve_s.mark(TT_(x1, lr, dt, ALU.mult), "rates")
                    MAGIC = 1.5 * 2.0 ** 23
                    link(TS(nn, th, 1.0 / (2 * math.pi), MAGIC, ALU.mult, ALU.add))
                    link(TS(nn, nn, -MAGIC, None, ALU.add))
                    two_pi = [6.28125, float(np.float32(2 * math.pi - 6.28125) - np.float32(2 * math.pi - 6.28125) % np.float32(2.0 ** -21))]
                    two_pi.append(2 * math.pi - sum(two_pi))
                    link(STT(out=red, in0=nn, scalar=-two_pi[0], in1=th, op0=ALU.mult, op1=ALU.add))
                    link(STT(out=red, in0=nn, scalar=-two_pi[1], in1=red, op0=ALU.mult, op1=ALU.add))
                    link(STT(out=red, in0=nn, scalar=-two_pi[2], in1=red, op0=ALU.mult, op1=ALU.add))
                    dve_s.mark(TS(red, red, 3.1415925, -3.1415925, ALU.min, ALU.max), "reduced")
                    pe_s.wait(dve, "c_flip")
                    for g in range(2):
                        half = slice(g * NS, (g + 1) * NS)
                        ins = dve.tensor_copy(cc[half, :, :, :].rearrange("p x (t j) h -> p (x t) j h", t=ST),
                                              bank[half, 0:2, :].rearrange("p x (t j g h) -> p (x t) j g h", t=ST, g=2, h=GH)[:, :, :, g, :])
                    dve_s.mark(ins, "c")
                    act_s.wait(dve, "cos")
                    TT_(ar, mag, co, ALU.mult)
                    TT_(ai, mag, si, ALU.mult)
                    TT_(x2, lr, lr, ALU.mult)
                    link(TT_(den, li, li, ALU.mult))
                    link(TT_(den, den, x2, ALU.add))
                    link(dve.reciprocal(den, den))
                    link(TS(x2, ar, -1.0, None, ALU.add))
                    TT_(zr, x2, lr, ALU.mult)
                    TT_(zi, ai, lr, ALU.mult)
                    link(TT_(nn, ai, li, ALU.mult))
                    link(TT_(zr, zr, nn, ALU.add))
                    link(TT_(nn, x2, li, ALU.mult))
                    link(TT_(zi, zi, nn, ALU.subtract))
                    link(TT_(zr, zr, den, ALU.mult))
                    link(TT_(zi, zi, den, ALU.mult))
                    wide = [P, PAIRS, GH]
                    f1, f2 = (w.rearrange("p j k -> p (j k)") for w in (w1, w2))
                    by_h = lambda v: v.unsqueeze(2).broadcast_to(wide)
                    small = [f[:, 0:256].rearrange("p (j h) -> p j h", j=PAIRS) for f in (f1, f2)]
                    cmul(bb[:, 2], bb[:, 3], bb[:, 0], bb[:, 1], by_h(zr), by_h(zi), small)
                    TS(pw[:, 0, 0, :], lr, 0.0, 1.0, ALU.mult, ALU.add)
                    TS(pw[:, 1, 0, :], lr, 0.0, None, ALU.mult)
                    dve.tensor_copy(pw[:, 0, 1, :], ar)
                    dve_s.mark(dve.tensor_copy(pw[:, 1, 1, :], ai), "b")
                    dve_s.wait(dve, "b")
                    for n in (1, 2, 4):
                        shape = [P, n, PAIRS]
                        t = [f[:, 0:n * PAIRS].rearrange("p (n j) -> p n j", n=n) for f in (f1, f2)]
                        cmul(pw[:, 0, n + 1:2 * n + 1, :], pw[:, 1, n + 1:2 * n + 1, :], pw[:, 0, 1:n + 1, :], pw[:, 1, 1:n + 1, :],
                             pw[:, 0, n:n + 1, :].broadcast_to(shape), pw[:, 1, n:n + 1, :].broadcast_to(shape), t)
                    for n in range(BLK + 1):
                        pr, pi = by_h(pw[:, 0, n, :]), by_h(pw[:, 1, n, :])
                        TT_(small[0], cc[:, 0], pr, ALU.mult)
                        link(TT_(small[1], cc[:, 1], pi, ALU.mult))
                        link(TT_(C_pow[:, 0, :, n, :], small[0], small[1], ALU.subtract))
                        TT_(small[0], cc[:, 0], pi, ALU.mult)
                        link(TT_(small[1], cc[:, 1], pr, ALU.mult))
                        ins = STT(out=C_pow[:, 1, :, n, :], in0=small[0], scalar=-1.0, in1=small[1], op0=ALU.mult, op1=ALU.subtract)
                        if n < BLK:
                            link(ins)
                    dve_s.mark(ins, "C")
                    dve_s.wait(dve, "C")
                    for n in range(BLK):
                        cmul(lift[:, 0, :, n, :], lift[:, 1, :, n, :], bb[:, 2], bb[:, 3], by_h(pw[:, 0, n, :]), by_h(pw[:, 1, n, :]), small)
                    dve_s.mark(TS(c8, co, 1.0, None, ALU.mult), "lift")
                    act_s.wait(dve, "kernel")
                    dve.wait_ge(d_loaded, 32)
                    diag = [GH, GROUPS, GH]
                    dI = bb[0:GH, 0:2, :, :].rearrange("p x j h -> p (x j) h")
                    link(TT_(dI, d16[:, :, :].rearrange("p g j -> p (g j)").unsqueeze(2).broadcast_to(diag), ident[0:GH, 0:GH].unsqueeze(1).broadcast_to(diag), ALU.mult))
                    dve_s.mark(TT_(kernel16[:, :, 0:GH], kernel16[:, :, 0:GH], dI, ALU.add), "kernel")
                    link(dve.tensor_copy(s8, si))
                    t = [ab, ph]
                    for _ in range(3):
                        cmul(x2, nn, c8, s8, c8, s8, t)
                        dve.tensor_copy(c8, x2)
                        link(dve.tensor_copy(s8, nn))
                    for r in range(1):
                        dve.wait_ge(K_placed, BLK * 16)
                    TS(turn_re[:, :, 0:1], lr.unsqueeze(2), 0.0, 1.0, ALU.mult, ALU.add)
                    link(TS(turn_im[:, :, 0:1], lr.unsqueeze(2), 0.0, None, ALU.mult))
                    n = 1
                    while n < NBLK:
                        shape = [P, PAIRS, n]
                        t = [f.rearrange("p (j k) -> p j k", j=PAIRS)[:, :, 0:n] for f in (f1, f2)]
                        cmul(turn_re[:, :, n:2 * n], turn_im[:, :, n:2 * n], turn_re[:, :, 0:n], turn_im[:, :, 0:n],
                             c8.unsqueeze(2).broadcast_to(shape), s8.unsqueeze(2).broadcast_to(shape), t)
                        n *= 2
                        if n < NBLK:
                            cmul(x2, nn, c8, s8, c8, s8, [ab, ph])
                            dve.tensor_copy(c8, x2)
                            link(dve.tensor_copy(s8, nn))
                    act_s.wait(dve, "rho")
                    link(dve.tensor_copy(shrink[:, :, :], rho.unsqueeze(2).broadcast_to([P, PAIRS, NBLK])))
                    link(dve.memset(shrink[:, :, 0:1], 0.0))
                    pool_s.wait(dve, "zero")
                    for h in range(2):
                        rows_ = slice(h * HP, (h + 1) * HP)
                        tr, ti = turn_re[:, rows_, :], turn_im[:, rows_, :]
                        w_re, w_im = (bank[:, 2 * x:2 * x + 2, :].rearrange("p b (j k) -> p (b j) k", k=NBLK) for x in range(2))
                        one = lambda v: v.rearrange("p j k -> p (j k)")
                        if h:
                            pe_s.wait(dve, "y0")
                        pe_s.wait(dve, f"w{h}")
                        TT_(w1, w_re, tr, ALU.mult)
                        link(TT_(w2, w_im, ti, ALU.mult))
                        link(TT_(w1, w1, w2, ALU.add))
                        TT_(w3, w_re, ti, ALU.mult)
                        link(TT_(w2, w_im, tr, ALU.mult))
                        link(TT_(w2, w2, w3, ALU.subtract))
                        sh = one(shrink[:, rows_, :])
                        dve.tensor_tensor_scan(one(z_re), sh, one(w1), 0.0, ALU.mult, ALU.add)
                        link(dve.tensor_tensor_scan(one(z_im[:, :, :]), sh, one(w2), 0.0, ALU.mult, ALU.add))
                        TT_(w1, z_re, tr, ALU.mult)
                        link(TT_(w2, z_im[:, :, :], ti, ALU.mult))
                        link(TT_(st_re[:, :, 1:NBLK + 1], w1, w2, ALU.subtract))
                        TT_(w1, z_re, ti, ALU.mult)
                        link(TT_(w2, z_im[:, :, :], tr, ALU.mult))
                        dve_s.mark(TT_(st_im[:, :, 1:NBLK + 1], w1, w2, ALU.add), f"s{h}")

        with ExitStack() as scope:
            sig = sb("glu_sig", [P, 2, S], scope)
            glu = sb("glu", [P, ST, S], scope)
            pe_g = Steps(sem("glu_pe"), [f"{n}{b}" for n in ("glu", "z") for b in range(4)])
            act_g = Steps(sem("glu_act"), [f"{n}{b}" for n in ("glu", "z") for b in range(4)])
            dve_g = Steps(sem("glu_dve"), [f"{n}{b}" for n in ("glu", "z") for b in range(4)])
            q0 = quads[0]
            quads[0] += 2
            with nc.Block() as block:
                @block.sync
                def _(sp):
                    for b in range(4):
                        sp.dma_start(ring[:, b, 0:ST, :], columns(a["w_ssm_glu_2"][0], b)).then_inc(w_loaded[b], 16)
                    for b in range(4):
                        pe_g.wait(sp, f"glu{b}")
                        sp.dma_start(ring[:, b, :, :], columns(w_in, ZS + b)).then_inc(w_loaded[b], 16)

                @block.tensor
                def _(pe):
                    pe_g.ready(pe)
                    for n, (name, src, kt) in enumerate((("glu", ssm_y, ST), ("z", hT, KT))):
                        for b in range(4):
                            pe.wait_ge(w_loaded[b], (q0 + n + 1) * 16)
                            if b >= 2:
                                act_g.wait(pe, f"{name}{b - 2}")
                            elif n:
                                act_g.wait(pe, f"glu{b + 2}")
                            pe_g.mark(project(b, src, kt), f"{name}{b}")

                @block.scalar
                def _(act):
                    act_g.ready(act)
                    for n, (name, f) in enumerate((("glu", ACT.Sigmoid), ("z", ACT.Silu))):
                        for b in range(4):
                            pe_g.wait(act, f"{name}{b}")
                            if b >= 2 or n:
                                dve_g.wait(act, f"{name}{b - 2}" if b >= 2 else f"glu{b + 2}")
                            act_g.mark(act.activation(sig[:, b % 2, :], pair(b % 2), f, bias=vec("glu_b", b) if n == 0 else 0.0), f"{name}{b}")

                @block.vector
                def _(dve):
                    dve_g.ready(dve)
                    for b in range(4):
                        act_g.wait(dve, f"glu{b}")
                        dve_g.mark(dve.tensor_tensor(glu[:, b, :], ssm_y[:, b, :], sig[:, b % 2, :], ALU.mult), f"glu{b}")
                    pe_g.wait(dve, "glu3")
                    for b in range(4):
                        act_g.wait(dve, f"z{b}")
                        dve_g.wait(dve, f"glu{b}")
                        dve_g.mark(dve.tensor_tensor(ssm_y[:, b, :], glu[:, b, :], sig[:, b % 2, :], ALU.mult), f"z{b}")

        with ExitStack() as scope:
            PAD = TAPS31 - 1
            sig = sb("conv_sig", [P, S], scope)
            padded = sb("conv_padded", [P, 2, PAD + S], scope)
            acc = sb("conv_acc", [P, 2, S], scope)
            taps = sb("conv_taps", [P, 2, 32], scope)
            pe_v = Steps(sem("conv_pe"), [f"tile{b}" for b in range(4)])
            act_v = Steps(sem("conv_act"), [f"sig{p}" for p in range(2)])
            dve_v = Steps(sem("conv_dve"), [s + str(p) for p in range(2) for s in ["taps", "cu"] + [f"t{j}_" for j in range(TAPS31)]])
            pad_zero = sem("conv_pad_zero")
            q0 = quads[0]
            quads[0] += KT // 2
            with nc.Block() as block:
                @block.sync
                def _(sp):
                    with sp.Fori(0, KT // 2) as i:
                        load_quad(sp, pe_v, i, [(ring[:, 2 * p + z, :, :], columns(w_in, i * 2 + (p + z * CB)))
                                                for p in range(2) for z in range(2)])

                @block.gpsimd
                def _(g):
                    g.memset(padded[:, :, 0:PAD], 0.0).then_inc(pad_zero, 1)

                @block.tensor
                def _(pe):
                    pe_v.ready(pe)
                    with pe.Fori(0, KT // 2) as i:
                        for b in range(4):
                            pe.wait_ge(w_loaded[b], (i + (q0 + 1)) * 16)
                            if b % 2 == 0:
                                dve_v.wait(pe, f"cu{1 - b // 2}", i, back=int(b == 0))
                            else:
                                act_v.wait(pe, f"sig{1 - b // 2}", i, back=int(b == 1))
                            pe_v.mark(project(b, hT), f"tile{b}")

                @block.scalar
                def _(act):
                    act_v.ready(act)
                    with act.Fori(0, KT // 2) as i:
                        for p in range(2):
                            pe_v.wait(act, f"tile{2 * p + 1}", i)
                            dve_v.wait(act, f"cu{1 - p}", i, back=int(p == 0))
                            act_v.mark(act.activation(sig[:, :], pair(1), ACT.Sigmoid), f"sig{p}")

                @block.vector
                def _(dve):
                    dve_v.ready(dve)
                    dve.wait_ge(pad_zero, 1)
                    with dve.Fori(0, KT // 2) as i:
                        for p in range(2):
                            n = i * 2 + p
                            dve.tensor_copy(taps[:, p, 0:16], vecs[:, 3, :].rearrange("p (j k) -> p k j", k=KT)[:, n, :])
                            dve_v.mark(dve.tensor_copy(taps[:, p, 16:TAPS31], vecs[:, 4, 0:15 * KT].rearrange("p (j k) -> p k j", k=KT)[:, n, :]), f"taps{p}")
                            act_v.wait(dve, f"sig{p}", i)
                            dve_v.mark(dve.tensor_tensor(padded[:, p, PAD:], pair(0), sig[:, :], ALU.mult), f"cu{p}")
                            dve_v.wait(dve, f"cu{p}", i)
                            dve_v.mark(dve.tensor_scalar(acc[:, p, :], padded[:, p, 0:S], taps[:, p, 0:1], vec("conv_b2", n), ALU.mult, ALU.add), f"t0_{p}")
                            for j in range(1, TAPS31):
                                dve_v.wait(dve, f"t{j - 1}_{p}", i)
                                dst = acc[:, p, :] if j < TAPS31 - 1 else yT[:, n, :]
                                dve_v.mark(dve.scalar_tensor_tensor(out=dst, in0=padded[:, p, j:j + S], scalar=taps[:, p, j:j + 1],
                                                                    in1=acc[:, p, :], op0=ALU.mult, op1=ALU.add), f"t{j}_{p}")

        with ExitStack() as scope:
            sq = sb("ln_sq", [P, 2, S], scope)
            mean = sb("ln_mean", [P, TT], scope)
            inv_std = sb("ln_inv_std", [P, TT], scope)
            eps = sb("ln_eps", [P, 1], scope)
            pe_n = Steps(sem("ln_pe"), ["sums", "mean"] + [f"sq{k}" for k in range(KT)] + ["inv"])
            act_n = Steps(sem("ln_act"), ["mean"] + [f"sq{k}" for k in range(KT)] + ["std"] + [f"silu{k}" for k in range(KT)])
            dve_n = Steps(sem("ln_dve"), [f"centred{k}" for k in range(KT)] + ["var", "inv"] + [f"scaled{k}" for k in range(KT)])
            pool_n = Steps(sem("ln_pool"), ["eps"])
            with nc.Block() as block:
                @block.gpsimd
                def _(g):
                    pool_n.ready(g)
                    pool_n.mark(g.memset(eps[:, :], LN_EPS), "eps")

                @block.tensor
                def _(pe):
                    pe_n.ready(pe)
                    for t in range(TT):
                        for k in range(KT):
                            last = nc.tensor.matmul(bank[:, 0, t:t + 1], yT[:, k, t * P:(t + 1) * P], ones[:, 0:1], start=(k == 0), stop=(k == KT - 1))
                    pe_n.mark(last, "sums")
                    act_n.wait(pe, "mean")
                    for t in range(TT):
                        last = nc.tensor.matmul(bank[:, 2 + t // 4, (t % 4) * P:(t % 4 + 1) * P], mean[:, t:t + 1].broadcast_to([P, P]), ident[:, :],
                                                start=True, stop=True)
                    pe_n.mark(last, "mean")
                    for k in range(KT):
                        act_n.wait(pe, f"sq{k}")
                        for t in range(TT):
                            last = nc.tensor.matmul(bank[:, 1, k * TT + t:k * TT + t + 1], sq[:, k % 2, t * P:(t + 1) * P], ones[:, 0:1], start=True, stop=True)
                        pe_n.mark(last, f"sq{k}")
                    dve_n.wait(pe, "inv")
                    for t in range(TT):
                        last = nc.tensor.matmul(bank[:, 4 + t // 4, (t % 4) * P:(t % 4 + 1) * P], inv_std[:, t:t + 1].broadcast_to([P, P]), ident[:, :],
                                                start=True, stop=True)
                    pe_n.mark(last, "inv")

                @block.scalar
                def _(act):
                    act_n.ready(act)
                    pe_n.wait(act, "sums")
                    act_n.mark(act.activation(mean[:, :], bank[:, 0, 0:TT], ACT.Copy, scale=1.0 / D), "mean")
                    for k in range(KT):
                        dve_n.wait(act, f"centred{k}")
                        if k >= 2:
                            pe_n.wait(act, f"sq{k - 2}")
                        act_n.mark(act.activation(sq[:, k % 2, :], yT[:, k, :], ACT.Square), f"sq{k}")
                    pool_n.wait(act, "eps")
                    dve_n.wait(act, "var")
                    act_n.mark(act.activation(inv_std[:, :], inv_std[:, :], ACT.Sqrt, bias=eps[:, 0:1], scale=1.0 / D), "std")
                    for k in range(KT):
                        dve_n.wait(act, f"scaled{k}")
                        act_n.mark(act.activation(yT[:, k, :], yT[:, k, :], ACT.Silu, scale=vec("ln_g", k), bias=vec("ln_b", k)), f"silu{k}")

                @block.vector
                def _(dve):
                    dve_n.ready(dve)
                    pe_n.wait(dve, "mean")
                    for k in range(KT):
                        dve_n.mark(dve.tensor_tensor(yT[:, k, :], yT[:, k, :], pair(1), ALU.subtract), f"centred{k}")
                    pe_n.wait(dve, f"sq{KT - 1}")
                    dve_n.mark(dve.tensor_reduce(out=inv_std[:, :], in_=bank[:, 1, 0:KT * TT].rearrange("p (k t) -> p t k", t=TT), op=ALU.add, axis=AX.X), "var")
                    act_n.wait(dve, "std")
                    dve_n.mark(dve.reciprocal(inv_std[:, :], inv_std[:, :]), "inv")
                    pe_n.wait(dve, "inv")
                    for k in range(KT):
                        act_n.wait(dve, f"sq{k}")
                        dve_n.wait(dve, f"centred{k}")
                        dve_n.mark(dve.tensor_tensor(yT[:, k, :], yT[:, k, :], pair(2), ALU.mult), f"scaled{k}")

        with ExitStack() as scope:
            silu_z = sb("zc_silu", [P, 2, S], scope)
            pe_z = Steps(sem("zc_pe"), [f"tile{b}" for b in range(4)])
            act_z = Steps(sem("zc_act"), [f"silu{b}" for b in range(4)])
            dve_z = Steps(sem("zc_dve"), [f"gated{b}" for b in range(4)])
            q0 = quads[0]
            quads[0] += KT // 4
            with nc.Block() as block:
                @block.sync
                def _(sp):
                    with sp.Fori(0, KT // 4) as i:
                        load_quad(sp, pe_z, i, [(ring[:, b, :, :], columns(w_in, i * 4 + (ZC + b))) for b in range(4)])

                @block.tensor
                def _(pe):
                    pe_z.ready(pe)
                    with pe.Fori(0, KT // 4) as i:
                        for b in range(4):
                            pe.wait_ge(w_loaded[b], (i + (q0 + 1)) * 16)
                            act_z.wait(pe, f"silu{(b + 2) % 4}", i, back=int(b < 2))
                            pe_z.mark(project(b, hT), f"tile{b}")

                @block.scalar
                def _(act):
                    act_z.ready(act)
                    with act.Fori(0, KT // 4) as i:
                        for b in range(4):
                            pe_z.wait(act, f"tile{b}", i)
                            dve_z.wait(act, f"gated{(b + 2) % 4}", i, back=int(b < 2))
                            act_z.mark(act.activation(silu_z[:, b % 2, :], pair(b % 2), ACT.Silu), f"silu{b}")

                @block.vector
                def _(dve):
                    dve_z.ready(dve)
                    with dve.Fori(0, KT // 4) as i:
                        for b in range(4):
                            act_z.wait(dve, f"silu{b}", i)
                            y_n = yT[:, i * 4 + b, :]
                            dve_z.mark(dve.tensor_tensor(y_n, y_n, silu_z[:, b % 2, :], ALU.mult), f"gated{b}")

        merged = sb("merged", [P, KT, S])
        with ExitStack() as scope:
            sig = sb("merge_sig", [P, 2, S], scope)
            branch = sb("merge_branch", [P, 2, S], scope)
            pe_m = Steps(sem("merge_pe"), [f"tile{b}" for b in range(4)])
            act_m = Steps(sem("merge_act"), ["sig0", "sig1"])
            dve_m = Steps(sem("merge_dve"), ["conv", "ssm", "merged"])
            q0 = quads[0]
            quads[0] += KT
            with nc.Block() as block:
                @block.sync
                def _(sp):
                    with sp.Fori(0, KT) as n:
                        load_quad(sp, pe_m, n, [(ring[:, 0, :, :], columns(w_in, n + GC)), (ring[:, 1, :, :], columns(a["w_conv_out_2"][0], n)),
                                                (ring[:, 2, :, :], columns(w_in, n + GS)), (ring[:, 3, 0:ST, :], columns(a["w_ssm_out_2"][0], n))])

                @block.tensor
                def _(pe):
                    pe_m.ready(pe)
                    with pe.Fori(0, KT) as n:
                        for b, (src, kt) in enumerate(((hT, KT), (yT, KT), (hT, KT), (ssm_y, ST))):
                            pe.wait_ge(w_loaded[b], (n + (q0 + 1)) * 16)
                            if b % 2 == 0:
                                act_m.wait(pe, f"sig{1 - b // 2}", n, back=int(b == 0))
                            else:
                                dve_m.wait(pe, ("ssm", "conv")[b // 2], n, back=int(b == 1))
                            pe_m.mark(project(b, src, kt), f"tile{b}")

                @block.scalar
                def _(act):
                    act_m.ready(act)
                    with act.Fori(0, KT) as n:
                        for p in range(2):
                            pe_m.wait(act, f"tile{2 * p}", n)
                            dve_m.wait(act, ("conv", "ssm")[p], n, back=1)
                            act_m.mark(act.activation(sig[:, p, :], pair(0), ACT.Sigmoid), f"sig{p}")

                @block.vector
                def _(dve):
                    dve_m.ready(dve)
                    with dve.Fori(0, KT) as n:
                        for p, name in enumerate(("conv", "ssm")):
                            pe_m.wait(dve, f"tile{2 * p + 1}", n)
                            act_m.wait(dve, f"sig{p}", n)
                            if p == 0:
                                dve_m.wait(dve, "merged", n, back=1)
                            dve_m.mark(dve.tensor_tensor(branch[:, p, :], pair(1), sig[:, p, :], ALU.mult), name)
                        dve_m.wait(dve, "ssm", n)
                        dve_m.mark(dve.tensor_tensor(merged[:, n, :], branch[:, 0, :], branch[:, 1, :], ALU.add), "merged")

        with ExitStack() as scope:
            w_out = yT[:, :, :].rearrange("p k (c n) -> p k c n", c=2)
            gain = sb("post_gain", [P, D], scope)
            junk = sb("post_junk", [P, D], scope)
            stat = sb("post_stat", [P, 2, TT], scope)
            eps = sb("post_eps", [P, 1], scope)
            w_ready, gain_loaded, out_stored = sem("post_w_loaded"), sem("post_gain_loaded"), sem("out_stored")
            pe_p = Steps(sem("post_pe"), [f"tok{t}" for t in range(TT)])
            act_p = Steps(sem("post_act"), [f"{s}{t}" for t in range(TT) for s in ("sq", "rms")])
            dve_p = Steps(sem("post_dve"), [f"{s}{t}" for t in range(TT) for s in ("inv", "scaled", "out")])
            pool_p = Steps(sem("post_pool"), ["eps"])
            with nc.Block() as block:
                @block.sync
                def _(sp):
                    sp.dma_start(w_out, a["w_out_2"][0].rearrange("(k p) (c n) -> p k c n", p=P, c=2)).then_inc(w_ready, 16)
                    sp.dma_start(gain[:, :], a["post_norm_gain_2"][0].partition_broadcast(P)).then_inc(gain_loaded, 16)
                    for t in range(TT):
                        dve_p.wait(sp, f"out{t}")
                        sp.dma_start(out[0, t * P:(t + 1) * P, :], hT[:, t, :]).then_inc(out_stored, 16)
                    sp.wait_ge(out_stored, 16 * TT)

                @block.gpsimd
                def _(g):
                    pool_p.ready(g)
                    pool_p.mark(g.memset(eps[:, :], EPS), "eps")

                @block.tensor
                def _(pe):
                    pe_p.ready(pe)
                    pe.wait_ge(w_ready, 16)
                    for t in range(TT):
                        if t >= 4:
                            dve_p.wait(pe, f"scaled{t - 4}")
                        for c in range(2):
                            for k in range(KT):
                                last = nc.tensor.matmul(bank[:, 2 * (t % 4) + c, :], merged[:, k, t * P:(t + 1) * P], w_out[:, k, c, :],
                                                        start=(k == 0), stop=(k == KT - 1))
                        pe_p.mark(last, f"tok{t}")

                @block.scalar
                def _(act):
                    act_p.ready(act)
                    pool_p.wait(act, "eps")
                    for t in range(TT):
                        pe_p.wait(act, f"tok{t}")
                        act_p.mark(act.activation(junk[:, :], pair(t % 4), ACT.Square, accum_out=stat[:, 0, t:t + 1]), f"sq{t}")
                        act_p.wait(act, f"sq{t}")
                        act_p.mark(act.activation(stat[:, 1, t:t + 1], stat[:, 0, t:t + 1], ACT.Sqrt, bias=eps[:, 0:1], scale=1.0 / D), f"rms{t}")

                @block.vector
                def _(dve):
                    dve_p.ready(dve)
                    dve.wait_ge(gain_loaded, 16)
                    for t in range(TT):
                        act_p.wait(dve, f"rms{t}")
                        dve_p.mark(dve.reciprocal(stat[:, 1, t:t + 1], stat[:, 1, t:t + 1]), f"inv{t}")
                        dve_p.wait(dve, f"inv{t}")
                        dve_p.mark(dve.scalar_tensor_tensor(out=hT[:, t, :], in0=pair(t % 4), scalar=stat[:, 1, t:t + 1], in1=gain[:, :],
                                                            op0=ALU.mult, op1=ALU.mult), f"scaled{t}")
                        dve_p.wait(dve, f"scaled{t}")
                        dve_p.mark(dve.tensor_tensor(hT[:, t, :], hT[:, t, :], resid[:, t, :], ALU.add), f"out{t}")


_OUT_SHAPE = (1, S, D)


def kernel(**inputs):
    import concourse.bacc as bacc
    from concourse.bass_utils import run_bass_kernel_spmd

    nc = bacc.Bacc("TRN2", target_bir_lowering=False, num_devices=1)
    arrays, patterns = {}, {}
    for name, value in inputs.items():
        arrays[f"in_{name}"] = np.ascontiguousarray(value)
        patterns[name] = nc.dram_tensor(f"in_{name}", arrays[f"in_{name}"].shape, F32, kind="ExternalInput").ap()
    out = nc.dram_tensor("out", _OUT_SHAPE, F32, kind="ExternalOutput").ap()
    block_program(nc, patterns, out)
    return run_bass_kernel_spmd(nc, [arrays], core_ids=[0]).results[0]["out"]
```

```python
import math
from contextlib import ExitStack

import concourse.bass as bass
import numpy as np
from concourse import mybir
from concourse.alu_op_type import AluOpType as ALU

ACT = mybir.ActivationFunctionType
AX = mybir.AxisListType
F32 = mybir.dt.float32

P = 128
D = 1024
S = 1024
KT = D // P
TT = S // P
HALF = 512
HEADS = 8
CH = P
NCH = S // CH
TAPS4 = 4
TAPS31 = 31
EPS = 1e-6
LN_EPS = 1e-5
RG_C = 8.0
GDN_Z = 4 * D
GROUPS = 32
PAIRS = GROUPS // 2
NS = 64
GH = 16
BLK = P // GH
NBLK = S // BLK
MASKED = -1.0e30


class Steps:

    def __init__(self, sem, names):
        self.sem, self.names = sem, names
        self.at = {n: k + 1 for k, n in enumerate(names)}
        assert len(self.at) == len(names)
        self.next = 0

    def ready(self, eng):
        eng.sem_inc(self.sem, len(self.names))

    def mark(self, ins, name):
        assert self.names[self.next] == name, (name, self.names[self.next])
        self.next = (self.next + 1) % len(self.names)
        ins.then_inc(self.sem, 1)

    def wait(self, eng, name, body=0, back=0):
        eng.wait_ge(self.sem, (body + 1 - back) * len(self.names) + self.at[name])


def block_program(nc, a, out):
    ctx = ExitStack()

    with ctx:
        def sem(name):
            return ctx.enter_context(nc.semaphore(name))

        def sb(name, shape, scope=ctx):
            return scope.enter_context(nc.sbuf_tensor(name, shape, F32))

        bank = ctx.enter_context(nc.psum_tensor("bank", [P, 8, HALF], F32))
        ident = sb("ident", [P, P])
        ones = sb("ones", [P, P])
        resid = sb("resid", [P, TT, D])
        hT = sb("hT", [P, KT, S])
        yT = sb("yT", [P, KT, S])
        ring = sb("ring", [P, 4, KT, P])
        vecs = sb("vecs", [P, 5, P])
        cond = sb("cond", [P, 2, 2 * KT])
        inv_rms = sb("inv_rms", [P, TT])
        norm_eps = sb("norm_eps", [P, 1])
        layers = ctx.enter_context(ExitStack())
        gate_b = sb("gate_b", [P, 2, D], layers)
        w_loaded = [sem(f"w_loaded{b}") for b in range(4)]
        quads = [0]

        def pair(n):
            return bank[:, 2 * n:2 * n + 2, :].rearrange("p a c -> p (a c)")

        VEC = {}

        def vec(name, k, n=1):
            tile, at = VEC[name]
            return vecs[:, tile, bass.ds(at + k, n)]

        def load_quad(sp, pe, body, tiles, names=("tile0", "tile1", "tile2", "tile3")):
            for b, (dst, src) in enumerate(tiles):
                pe.wait(sp, names[b], body, back=1)
                sp.dma_start(dst, src).then_inc(w_loaded[b], 16)

        def columns(w, n, kt=KT):
            return w.rearrange("(k p) c -> p k c", p=P)[:, :, bass.ts(n, P)]

        def project(b, src, kt=KT, w=None):
            to, w = (b % 2, ring[:, b]) if w is None else (b, w)
            for h in range(2):
                for k in range(kt):
                    last = nc.tensor.matmul(bank[:, 2 * to + h, :], w[:, k, :],
                                            src[:, k, h * HALF:(h + 1) * HALF],
                                            start=(k == 0), stop=(k == kt - 1))
            return last

        def log1p_steps(dve, link, p, e, z, z2):
            link(dve.tensor_scalar(z, e, 2.0, None, ALU.add))
            link(dve.reciprocal(z, z))
            link(dve.tensor_tensor(z, z, e, ALU.mult))
            link(dve.tensor_tensor(z2, z, z, ALU.mult))
            link(dve.tensor_scalar(p, z2, 1.0 / 19.0, None, ALU.mult))
            for n in range(17, 1, -2):
                link(dve.scalar_tensor_tensor(out=p, in0=p, scalar=1.0 / n, in1=z2, op0=ALU.add, op1=ALU.mult))
            link(dve.scalar_tensor_tensor(out=p, in0=p, scalar=1.0, in1=z, op0=ALU.add, op1=ALU.mult))
            link(dve.tensor_scalar(p, p, 2.0, None, ALU.mult))

        SQUARES = [f"sq{t}" for t in range(TT)] + ["rms"]

        def token_rms(act, steps, junk, rms, ready=None):
            for t in range(TT):
                if ready:
                    ready(t)
                if t >= 2:
                    steps.wait(act, f"sq{t - 2}")
                steps.mark(act.activation(junk[:, t % 2, :], resid[:, t, :], ACT.Square, accum_out=rms[:, t:t + 1]), f"sq{t}")
            steps.wait(act, f"sq{TT - 1}")
            steps.mark(act.activation(rms[:, :], rms[:, :], ACT.Sqrt, bias=norm_eps[:, 0:1], scale=1.0 / D), "rms")

        def linker(eng, s):
            count = [0]

            def link(ins):
                count[0] += 1
                ins.then_inc(s, 1)
                eng.wait_ge(s, count[0])
            return link

        def flat(v):
            return v.rearrange("(k p) -> k p", p=P) if len(v.shape) == 1 else v.rearrange("n (k p) -> (n k) p", p=P)

        rows = [
            [(["norm_g0", "norm_g1"], a["norm_g"]), (["conv_b"], a["lru_conv_b"][0]), (["gate_b0", "gate_b1"], a["lru_gate_b"][0]),
             (["lam"], a["lru_lambda"][0]), (["ada_b0"], a["ada_b"][0, 0:2 * D]), (["ada_b1"], a["ada_b"][1, 0:2 * D])],
            [(["c"], a["c"][0]), (["conv_b2"], a["conv_b_2"][0]), (["ln_g"], a["conv_ln_gain_2"][0]), (["ln_b"], a["conv_ln_bias_2"][0]),
             (["glu_b"], a["b_ssm_glu_2"][0]), (["pre_g"], a["pre_norm_gain_2"][0]), (["onorm"], a["gdn_onorm_g"][0]),
             ([f"lru_conv{j}" for j in range(TAPS4)], a["lru_conv_w"][0])],
            [([f"gdn_conv{j}" for j in range(TAPS4)], a["gdn_conv_w"][0])],
            [([f"conv31_{j}" for j in range(16)], a["conv_w_2"][0, 0:16])],
            [([f"conv31_{j}" for j in range(16, TAPS31)], a["conv_w_2"][0, 16:TAPS31])],
        ]
        with ExitStack() as scope:
            row_tiles = sb("row_tiles", [P, 5, P], scope)
            c_act = sb("c_act", [P, KT], scope)
            c_wide = sb("c_wide", [P, KT, P], scope)
            junk = sb("setup_junk", [P, 2, D], scope)
            diagonal = sb("cond_diagonal", [P, 2, 4, P], scope)
            ada = sb("ada", [P, 2, KT, HALF], scope)
            gate_bias = sb("gate_bias", [P, 2, D], scope)
            rows_loaded, biases_loaded = sem("rows_loaded"), sem("biases_loaded")
            ada_loaded = [sem("ada_loaded0"), sem("ada_loaded1")]
            x_loaded = sem("x_loaded")
            pool = Steps(sem("setup_pool"), ["ident0", "ident", "ones", "eps", "row0"])
            pe_s = Steps(sem("setup_pe"), ["rows_flipped"])
            act_s = Steps(sem("setup_act"), ["vecs", "c_act"] + SQUARES)
            dve_s = Steps(sem("setup_dve"), ["c_wide", "cond0"])
            pe_c = Steps(sem("cond_pe"), [f"chunk{q}" for q in range(6)])
            dve_c = Steps(sem("cond_dve"), [f"{n}{q}" for q in range(4) for n in ("diagonal", "cond")] + ["gate4", "gate5"])

            loads = []
            for tile, vectors in enumerate(rows):
                at = 0
                for names, v in vectors:
                    v = flat(v)
                    for n, name in enumerate(names):
                        VEC[name] = (tile, at + n * (v.shape[0] // len(names)))
                    loads.append((at, tile, v))
                    at += v.shape[0]
                assert at <= P
            n_rows = len(loads)

            with nc.Block() as block:
                @block.sync
                def _(sp):
                    def chunk(layer, q):
                        pe_c.wait(sp, f"chunk{q - 2}" if q >= 2 else f"chunk{q + 4}", layer, back=int(q < 2))
                        src = a["ada_w"][layer].rearrange("(k p) c -> p k c", p=P)
                        sp.dma_start(ada[:, q % 2, :, :], src[:, :, q * HALF:(q + 1) * HALF]).then_inc(ada_loaded[q % 2], 16)

                    chunk(0, 0)
                    sp.wait_ge(rows_loaded, 16 * n_rows)
                    for q in range(1, 6):
                        chunk(0, q)
                        if q == 1:
                            sp.dma_start(resid[:, :, :], a["x"][0].rearrange("(t p) c -> p t c", p=P)).then_inc(x_loaded, 16)
                    for q in range(6):
                        chunk(1, q)

                @block.gpsimd
                def _(g):
                    pool.ready(g)
                    pool.mark(g.memset(ident[:, :], 0.0), "ident0")
                    pool.wait(g, "ident0")
                    pool.mark(g.affine_select(out=ident[:, :], in_=ident[:, :], compare_op=ALU.not_equal, fill=1.0,
                                              base=0, pattern=[[-1, P]], channel_multiplier=1), "ident")
                    pool.mark(g.memset(ones[:, :], 1.0), "ones")
                    pool.mark(g.memset(norm_eps[:, :], EPS), "eps")
                    pool.mark(g.memset(row_tiles[:, :, :], 0.0), "row0")

                @block.scalar
                def _(act):
                    act_s.ready(act)
                    pool.wait(act, "row0")
                    for at, tile, v in loads:
                        act.dma_start(row_tiles[at:at + v.shape[0], tile, :], v).then_inc(rows_loaded, 16)
                    for layer in range(2):
                        act.dma_start(gate_bias[:, layer, :],
                                      a["ada_b"][layer, 2 * D:3 * D].partition_broadcast(P)).then_inc(biases_loaded, 16)
                    pe_s.wait(act, "rows_flipped")
                    act.activation(vecs[:, 4, :], bank[:, 1, 0:P], ACT.Copy)
                    act_s.mark(act.activation(vecs[:, 0:4, :].rearrange("p t c -> p (t c)"), bank[:, 0, :], ACT.Copy),
                               "vecs")
                    act_s.wait(act, "vecs")
                    act_s.mark(act.activation(c_act[:, :], vec("c", 0, KT), ACT.Silu), "c_act")
                    act.wait_ge(x_loaded, 16)
                    token_rms(act, act_s, junk, inv_rms)

                @block.tensor
                def _(pe):
                    pe_s.ready(pe)
                    pe_c.ready(pe)
                    pool.wait(pe, "row0")
                    pe.wait_ge(rows_loaded, 16 * n_rows)
                    for tile in range(5):
                        last = nc.tensor.transpose(bank[:, tile // 4, (tile % 4) * P:(tile % 4 + 1) * P],
                                                   row_tiles[:, tile, :], ident[:, :])
                    pe_s.mark(last, "rows_flipped")
                    dve_s.wait(pe, "c_wide")
                    with pe.Fori(0, 2) as layer:
                        for q in range(6):
                            pe.wait_ge(ada_loaded[q % 2], (layer * 3 + q // 2 + 1) * 16)
                            dve_c.wait(pe, f"cond{q}" if q < 4 else f"gate{q}", layer, back=1)
                            for k in range(KT):
                                last = nc.tensor.matmul(bank[:, 2 + q, :], c_wide[:, k, :], ada[:, q % 2, k, :],
                                                        start=(k == 0), stop=(k == KT - 1))
                            pe_c.mark(last, f"chunk{q}")

                @block.vector
                def _(dve):
                    dve_s.ready(dve)
                    dve_c.ready(dve)
                    act_s.wait(dve, "c_act")
                    dve_s.mark(dve.tensor_copy(c_wide[:, :, :], c_act[:, :].unsqueeze(2).broadcast_to([P, KT, P])), "c_wide")
                    dve.wait_ge(biases_loaded, 32)
                    for layer in range(2):
                        for q in range(4):
                            pe_c.wait(dve, f"chunk{q}", layer)
                            dve_c.mark(dve.tensor_tensor(diagonal[:, q % 2, :, :], bank[:, 2 + q, :].rearrange("p (m c) -> p m c", c=P),
                                                         ident[:, :].unsqueeze(1).broadcast_to([P, 4, P]), ALU.mult), f"diagonal{q}")
                            dve_c.wait(dve, f"diagonal{q}", layer)
                            dve_c.mark(dve.tensor_reduce(out=cond[:, layer, 4 * q:4 * q + 4], in_=diagonal[:, q % 2, :, :], op=ALU.add, axis=AX.X),
                                       f"cond{q}")
                        for q in range(2):
                            pe_c.wait(dve, f"chunk{4 + q}", layer)
                            dve_c.mark(dve.tensor_tensor(gate_b[:, layer, q * HALF:(q + 1) * HALF], bank[:, 6 + q, :],
                                                         gate_bias[:, layer, q * HALF:(q + 1) * HALF], ALU.add), f"gate{4 + q}")
                    act_s.wait(dve, "rms")
                    dve.reciprocal(inv_rms[:, :], inv_rms[:, :])
                    dve_c.wait(dve, "cond3", 1)
                    for layer in range(2):
                        ins = dve.tensor_tensor(cond[:, layer, :], cond[:, layer, :], vec(f"ada_b{layer}", 0, 2 * KT), ALU.add)
                    dve_s.mark(ins, "cond0")
                    dve_s.wait(dve, "cond0")
                    for layer in range(2):
                        dve.scalar_tensor_tensor(out=cond[:, layer, KT:2 * KT], in0=cond[:, layer, KT:2 * KT], scalar=1.0,
                                                 in1=vec(f"norm_g{layer}", 0, KT), op0=ALU.add, op1=ALU.mult)

        def norm_transpose(name, scale, shift):
            with ExitStack() as scope:
                normed = sb(f"{name}_normed", [P, 4, D], scope)
                act_n = Steps(sem(f"{name}_act"), [f"low{p}" for p in range(4)])
                dve_n = Steps(sem(f"{name}_dve"), ["normed0"] + [n for p in range(4) for n in ([f"normed{p + 1}"] if p < 3 else []) + [f"high{p}"]])
                pe_n = Steps(sem(f"{name}_pe"), [f"flip{p}" for p in range(4)])
                with nc.Block() as block:
                    @block.scalar
                    def _(act):
                        act_n.ready(act)
                        for i in range(TT // 4):
                            for p in range(4):
                                pe_n.wait(act, f"flip{p}", i)
                                for k in range(KT // 2):
                                    ins = act.activation(hT[:, k, bass.ts(i * 4 + p, P)], bank[:, 2 * p, k * P:(k + 1) * P],
                                                         ACT.Identity, scale=scale(k), bias=shift(k))
                                act_n.mark(ins, f"low{p}")

                    @block.vector
                    def _(dve):
                        dve_n.ready(dve)

                        def normalise(i, p):
                            t = i * 4 + p
                            pe_n.wait(dve, f"flip{p}", i, back=1)
                            dve_n.mark(dve.tensor_scalar(normed[:, p, :], resid[:, t, :], inv_rms[:, t:t + 1], None, ALU.mult), f"normed{p}")

                        for i in range(TT // 4):
                            normalise(i, 0)
                            for p in range(4):
                                if p < 3:
                                    normalise(i, p + 1)
                                pe_n.wait(dve, f"flip{p}", i)
                                for k in range(KT // 2):
                                    ins = dve.tensor_scalar(hT[:, KT // 2 + k, bass.ts(i * 4 + p, P)],
                                                            bank[:, 2 * p + 1, k * P:(k + 1) * P],
                                                            scale(KT // 2 + k), shift(KT // 2 + k), ALU.mult, ALU.add)
                                dve_n.mark(ins, f"high{p}")

                    @block.tensor
                    def _(pe):
                        pe_n.ready(pe)
                        for i in range(TT // 4):
                            for p in range(4):
                                dve_n.wait(pe, f"normed{p}", i)
                                act_n.wait(pe, f"low{p}", i, back=1)
                                dve_n.wait(pe, f"high{p}", i, back=1)
                                for k in range(KT):
                                    last = nc.tensor.transpose(bank[:, 2 * p + k // 4, (k % 4) * P:(k % 4 + 1) * P],
                                                               normed[:, p, k * P:(k + 1) * P], ident[:, :])
                                pe_n.mark(last, f"flip{p}")

        ring_half = ring[:, :, :, :].rearrange("p b k c -> p (b k c)").rearrange("p (k c) -> p k c", k=KT)
        half_loaded = [sem("out0_half_loaded"), sem("out1_half_loaded")]

        def out_half(w, c):
            return w.rearrange("(k p) c -> p k c", p=P)[:, :, c * HALF:(c + 1) * HALF]

        def load_first_half(sp, w, layer):
            sp.dma_start(ring_half, out_half(w, 0)).then_inc(half_loaded[layer], 16)

        def project_out(name, w, layer):
            with ExitStack() as scope:
                second_half = sb(f"{name}_w", [P, KT, HALF], scope)
                gated = sb(f"{name}_gated", [P, 2, HALF], scope)
                junk = sb(f"{name}_junk", [P, 2, D], scope)
                loaded = [half_loaded[layer], sem(f"{name}_second_loaded")]
                pe_o = Steps(sem(f"{name}_pe"), [f"tok{t}" for t in range(TT)])
                dve_o = Steps(sem(f"{name}_dve"), [f"{s}{t}" for t in range(TT) for s in ("gated", "added")])
                act_o = Steps(sem(f"{name}_act"), SQUARES)
                with nc.Block() as block:
                    @block.sync
                    def _(sp):
                        sp.dma_start(second_half[:, :, :], out_half(w, 1)).then_inc(loaded[1], 16)

                    @block.tensor
                    def _(pe):
                        pe_o.ready(pe)
                        for c in range(2):
                            pe.wait_ge(loaded[c], 16)
                            for t in range(TT):
                                dve_o.wait(pe, f"gated{t}", c, back=1)
                                for k in range(KT):
                                    last = nc.tensor.matmul(bank[:, t, :], yT[:, k, t * P:(t + 1) * P], (ring_half, second_half)[c][:, k, :],
                                                            start=(k == 0), stop=(k == KT - 1))
                                pe_o.mark(last, f"tok{t}")

                    @block.scalar
                    def _(act):
                        act_o.ready(act)
                        token_rms(act, act_o, junk, inv_rms, lambda t: dve_o.wait(act, f"added{t}", 1))

                    @block.vector
                    def _(dve):
                        dve_o.ready(dve)
                        for c in range(2):
                            half = slice(c * HALF, (c + 1) * HALF)
                            for t in range(TT):
                                pe_o.wait(dve, f"tok{t}", c)
                                x_t = resid[:, t, half]
                                dve_o.mark(dve.tensor_tensor(gated[:, t % 2, :], bank[:, t, :], gate_b[:, layer, half], ALU.mult), f"gated{t}")
                                dve_o.wait(dve, f"gated{t}", c)
                                dve_o.mark(dve.tensor_tensor(x_t, x_t, gated[:, t % 2, :], ALU.add), f"added{t}")
                        act_o.wait(dve, "rms")
                        dve.reciprocal(inv_rms[:, :], inv_rms[:, :])

        norm_transpose("norm0", lambda k: cond[:, 0, KT + k:KT + k + 1], lambda k: cond[:, 0, k:k + 1])

        with ExitStack() as scope:
            PAD = TAPS4 - 1
            rate = sb("rate", [P, KT], scope)
            nrate = sb("nrate", [P, KT], scope)
            small = sb("lru_small", [P, 5, KT], scope)
            padded = sb("padded", [P, 2, PAD + S], scope)
            conv = sb("conv", [P, 2, S], scope)
            gw = sb("gw", [P, 2, 2, P], scope)
            gate_r = sb("gate_r", [P, S], scope)
            gate_i = sb("gate_i", [P, S], scope)
            sig_z = sb("sig_z", [P, 2, S], scope)
            tau = sb("tau", [P, S], scope)
            decay = sb("decay", [P, S], scope)
            mult = sb("mult", [P, S], scope)
            inp = sb("inp", [P, S], scope)
            state = sb("state", [P, S], scope)
            gw_loaded = [sem("gw_loaded0"), sem("gw_loaded1")]
            pe_l = Steps(sem("lru_pe"), ["tile0", "tile1", "gates0", "tile2", "tile3", "gates1"])
            act_names = ["x_in", "sig_z", "gate_r", "gate_i", "tau", "decay", "decay2", "mult"]
            act_l = Steps(sem("lru_act"), [s + str(p) for p in range(2) for s in act_names])
            dve_names = ["c0_", "c1_", "c2_", "conv", "sz", "ix", "m2", "b", "scan", "y"]
            dve_l = Steps(sem("lru_dve"), [s + str(p) for p in range(2) for s in dve_names])
            chain, e_ready = sem("lru_chain"), sem("lru_e_ready")
            pad_zero = sem("lru_pad_zero")
            q0 = quads[0]
            quads[0] += KT // 2

            with nc.Block() as block:
                @block.sync
                def _(sp):
                    w = a["lru_in_w"][0]
                    with sp.Fori(0, KT // 2) as i:
                        load_quad(sp, pe_l, i, [(ring[:, 2 * p + z, :, :], columns(w, i * 2 + (z * KT + p)))
                                                for p in range(2) for z in range(2)])
                    pe_l.wait(sp, "tile3", KT // 2 - 1)
                    load_first_half(sp, a["lru_out_w"][0], 0)

                @block.gpsimd
                def _(g):
                    g.memset(padded[:, :, 0:PAD], 0.0).then_inc(pad_zero, 1)
                    with g.Fori(0, KT // 2) as i:
                        for p in range(2):
                            pe_l.wait(g, f"gates{p}", i, back=1)
                            g.dma_start(gw[:, p, :, :], a["lru_gate_w"][0].rearrange("g n i j -> n i g j")[i * 2 + p]) \
                                .then_inc(gw_loaded[p], 16)

                @block.tensor
                def _(pe):
                    pe_l.ready(pe)

                    def gates(i, p):
                        pe.wait_ge(gw_loaded[p], (i + 1) * 16)
                        dve_l.wait(pe, f"conv{p}", i)
                        act_l.wait(pe, f"gate_i{1 - p}", i, back=int(p == 0))
                        for g in range(2):
                            for h in range(2):
                                last = nc.tensor.matmul(bank[:, 4 + 2 * g + h, :], gw[:, p, g, :],
                                                        conv[:, p, h * HALF:(h + 1) * HALF], start=True, stop=True)
                        pe_l.mark(last, f"gates{p}")

                    with pe.Fori(0, KT // 2) as i:
                        for b in range(4):
                            pe.wait_ge(w_loaded[b], (i + (q0 + 1)) * 16)
                            if b % 2 == 0:
                                act_l.wait(pe, f"x_in{1 - b // 2}", i, back=int(b == 0))
                            else:
                                dve_l.wait(pe, f"sz{1 - b // 2}", i, back=int(b == 1))
                            pe_l.mark(project(b, hT), f"tile{b}")
                            if b % 2 == 1:
                                gates(i, b // 2)

                @block.scalar
                def _(act):
                    act_l.ready(act)
                    act.activation(small[:, 0, :], vec("lam", 0, KT), ACT.Abs).then_inc(e_ready, 1)
                    act.wait_ge(e_ready, 1)
                    act.activation(small[:, 1, :], small[:, 0, :], ACT.Exp, scale=-1.0).then_inc(e_ready, 1)
                    act.wait_ge(pad_zero, 1)
                    act.wait_ge(chain, 17)
                    with act.Fori(0, KT // 2) as i:
                        for p in range(2):
                            n = i * 2 + p
                            pe_l.wait(act, f"tile{2 * p}", i)
                            dve_l.wait(act, f"conv{p}", i, back=1)
                            act_l.mark(act.activation(padded[:, p, PAD:], pair(0), ACT.Copy), f"x_in{p}")
                            pe_l.wait(act, f"tile{2 * p + 1}", i)
                            act_l.mark(act.activation(sig_z[:, p, :], pair(1), ACT.Sigmoid), f"sig_z{p}")
                            pe_l.wait(act, f"gates{p}", i)
                            act_l.mark(act.activation(gate_r[:, :], pair(2), ACT.Sigmoid, bias=vec("gate_b0", n)), f"gate_r{p}")
                            dve_l.wait(act, f"ix{1 - p}", i, back=int(p == 0))
                            act_l.mark(act.activation(gate_i[:, :], pair(3), ACT.Sigmoid, bias=vec("gate_b1", n)), f"gate_i{p}")
                            act_l.wait(act, f"gate_r{p}", i)
                            dve_l.wait(act, f"m2{1 - p}", i, back=int(p == 0))
                            act_l.mark(act.activation(tau[:, :], gate_r[:, :], ACT.Tanh, scale=nrate[:, bass.ds(n, 1)]), f"tau{p}")
                            dve_l.wait(act, f"scan{1 - p}", i, back=int(p == 0))
                            act_l.mark(act.activation(decay[:, :], gate_r[:, :], ACT.Exp, scale=rate[:, bass.ds(n, 1)]), f"decay{p}")
                            act_l.wait(act, f"decay{p}", i)
                            act_l.mark(act.activation(mult[:, :], decay[:, :], ACT.Square), f"decay2{p}")
                            dve_l.wait(act, f"m2{p}", i)
                            act_l.mark(act.activation(mult[:, :], mult[:, :], ACT.Sqrt), f"mult{p}")

                @block.vector
                def _(dve):
                    dve_l.ready(dve)
                    link = linker(dve, chain)
                    dve.wait_ge(e_ready, 2)
                    log1p_steps(dve, link, small[:, 2, :], small[:, 1, :], small[:, 3, :], small[:, 4, :])
                    link(dve.tensor_scalar(small[:, 0, :], vec("lam", 0, KT), -1.0, 0.0, ALU.mult, ALU.max))
                    link(dve.tensor_tensor(small[:, 2, :], small[:, 2, :], small[:, 0, :], ALU.add))
                    dve.tensor_scalar(rate[:, :], small[:, 2, :], -RG_C, None, ALU.mult)
                    link(dve.tensor_scalar(nrate[:, :], small[:, 2, :], RG_C, None, ALU.mult))
                    with dve.Fori(0, KT // 2) as i:
                        for p in range(2):
                            n = i * 2 + p
                            acc = conv[:, p, :]
                            act_l.wait(dve, f"x_in{p}", i)
                            pe_l.wait(dve, f"gates{p}", i, back=1)
                            dve_l.mark(dve.tensor_scalar(acc, padded[:, p, 0:S], vec("lru_conv0", n), vec("conv_b", n),
                                                         ALU.mult, ALU.add), f"c0_{p}")
                            for j in range(1, TAPS4):
                                dve_l.wait(dve, f"c{j - 1}_{p}", i)
                                dve_l.mark(dve.scalar_tensor_tensor(out=acc, in0=padded[:, p, j:j + S], scalar=vec(f"lru_conv{j}", n),
                                                                    in1=acc, op0=ALU.mult, op1=ALU.add),
                                           f"c{j}_{p}" if j < TAPS4 - 1 else f"conv{p}")
                            act_l.wait(dve, f"sig_z{p}", i)
                            dve_l.mark(dve.tensor_tensor(sig_z[:, p, :], pair(1), sig_z[:, p, :], ALU.mult), f"sz{p}")
                            act_l.wait(dve, f"gate_i{p}", i)
                            dve_l.mark(dve.tensor_tensor(inp[:, :], gate_i[:, :], acc, ALU.mult), f"ix{p}")
                            act_l.wait(dve, f"decay2{p}", i)
                            dve_l.mark(dve.scalar_tensor_tensor(out=mult[:, :], in0=mult[:, :], scalar=1.0, in1=tau[:, :],
                                                                op0=ALU.add, op1=ALU.mult), f"m2{p}")
                            act_l.wait(dve, f"mult{p}", i)
                            dve_l.mark(dve.tensor_tensor(inp[:, :], inp[:, :], mult[:, :], ALU.mult), f"b{p}")
                            dve_l.wait(dve, f"b{p}", i)
                            dve_l.mark(dve.tensor_tensor_scan(state[:, :], decay[:, :], inp[:, :], 0.0, ALU.mult, ALU.add), f"scan{p}")
                            dve_l.wait(dve, f"scan{p}", i)
                            dve_l.mark(dve.tensor_tensor(yT[:, n, :], state[:, :], sig_z[:, p, :], ALU.mult), f"y{p}")
        project_out("out0", a["lru_out_w"][0], 0)
        norm_transpose("norm1", lambda k: cond[:, 1, KT + k:KT + k + 1], lambda k: cond[:, 1, k:k + 1])

        with ExitStack() as scope:
            levels = [1 << s for s in range(7)]
            cols = {n: sb(f"col_{n}", [P, HEADS, NCH], scope)
                    for n in ("g", "beta", "exp_g", "exp_rest", "exp_last", "neg_beta_exp_g")}
            level_mask = sb("level_mask", [P, len(levels), P], scope)
            causal = sb("causal", [P, P], scope)

            with ExitStack() as inner:
                w_ab = sb("w_ab", [P, KT, 2 * HEADS], inner)
                tri = sb("tri", [P, P], inner)
                last_row = sb("last_row", [P, P], inner)
                dt_bias = sb("dt_bias", [P, HEADS], inner)
                neg_a = sb("neg_a", [P, HEADS], inner)
                a_in = sb("a_in", [P, HEADS, NCH], inner)
                step = sb("step", [P, HEADS, NCH], inner)
                tmp = [sb(f"ab_tmp{n}", [P, HEADS, NCH], inner) for n in range(5)]
                ab_loaded, row_loaded = sem("ab_loaded"), sem("ab_row_loaded")
                pe_a = Steps(sem("ab_pe"), ["ab", "cum", "last"])
                act_a = Steps(sem("ab_act"), ["neg_a", "beta", "abs", "exp", "exp_g", "exp_last", "exp_rest"])
                dve_a = Steps(sem("ab_dve"), ["a_in", "g_step", "g", "rest", "neg"])
                pool_a = Steps(sem("ab_pool"), ["fill", "masks"])
                chain = sem("ab_chain")
                pool_chain = sem("ab_pool_chain")
                with nc.Block() as block:
                    @block.sync
                    def _(sp):
                        sp.dma_start(w_ab[:, :, :], a["gdn_in_w"][0].rearrange("(k p) c -> p k c", p=P)[:, :, GDN_Z:]) \
                            .then_inc(ab_loaded, 16)
                        sp.dma_start(dt_bias[:, :], a["gdn_dt_bias"][0].partition_broadcast(P)).then_inc(row_loaded, 16)
                        sp.dma_start(neg_a[:, :], a["gdn_a_log"][0].partition_broadcast(P)).then_inc(row_loaded, 16)

                    @block.gpsimd
                    def _(g):
                        pool_a.ready(g)
                        link = linker(g, pool_chain)

                        def select(m, pattern, base, mult, fill, op=ALU.is_ge):
                            link(g.affine_select(out=m, in_=m, compare_op=op, fill=fill, base=base, pattern=pattern,
                                                 channel_multiplier=mult))

                        g.memset(tri[:, :], 1.0)
                        g.memset(causal[:, :], 0.0)
                        g.memset(last_row[:, :], 1.0)
                        pool_a.mark(g.memset(level_mask[:, :, :], 1.0), "fill")
                        pool_a.wait(g, "fill")
                        select(tri[:, :], [[1, P]], 0, -1, 0.0)
                        select(causal[:, :], [[1, P]], 0, -1, MASKED)
                        select(last_row[:, :], [[0, P]], -(P - 1), 1, 0.0)
                        for n, s in enumerate(levels):
                            nb = P // (2 * s)
                            m = level_mask[:, n, :].rearrange("p (b r e) -> p b r e", r=2, e=s)
                            select(m, [[0, nb], [1, 2], [0, s]], -1, 0, 0.0)
                            select(m, [[-2 * s, nb], [0, 2], [0, s]], 0, 1, 0.0)
                            select(m, [[2 * s, nb], [0, 2], [0, s]], s - 1, -1, 0.0)
                        pool_a.mark(g.memset(a_in[:, :, :], 0.0), "masks")

                    @block.tensor
                    def _(pe):
                        pe_a.ready(pe)
                        pe.wait_ge(ab_loaded, 16)
                        for t in range(TT):
                            for k in range(KT):
                                last = nc.tensor.matmul(bank[:, 4, t * 16:t * 16 + 16], hT[:, k, t * P:(t + 1) * P], w_ab[:, k, :],
                                                        start=(k == 0), stop=(k == KT - 1))
                        pe_a.mark(last, "ab")
                        pool_a.wait(pe, "masks")
                        dve_a.wait(pe, "g_step")
                        pe_a.mark(nc.tensor.matmul(bank[:, 5, 0:HEADS * NCH], tri[:, :], step[:, :, :].rearrange("p h c -> p (h c)"),
                                                   start=True, stop=True), "cum")
                        dve_a.wait(pe, "g")
                        pe_a.mark(nc.tensor.matmul(bank[:, 6, 0:HEADS * NCH], last_row[:, :],
                                                   cols["g"][:, :, :].rearrange("p h c -> p (h c)"), start=True, stop=True), "last")

                    @block.scalar
                    def _(act):
                        act_a.ready(act)
                        ab = bank[:, 4, 0:P].rearrange("p (t x h) -> p x h t", x=2, h=HEADS)
                        act.wait_ge(row_loaded, 32)
                        act_a.mark(act.activation(neg_a[:, :], neg_a[:, :], ACT.Exp), "neg_a")
                        pe_a.wait(act, "ab")
                        act_a.mark(act.activation(cols["beta"][:, :, :], ab[:, 1], ACT.Sigmoid), "beta")
                        dve_a.wait(act, "a_in")
                        act_a.mark(act.activation(tmp[0][:, :, :], a_in[:, :, :], ACT.Abs), "abs")
                        act_a.wait(act, "abs")
                        act_a.mark(act.activation(tmp[1][:, :, :], tmp[0][:, :, :], ACT.Exp, scale=-1.0), "exp")
                        dve_a.wait(act, "g")
                        act_a.mark(act.activation(cols["exp_g"][:, :, :], cols["g"][:, :, :], ACT.Exp), "exp_g")
                        pe_a.wait(act, "last")
                        act_a.mark(act.activation(cols["exp_last"][:, :, :],
                                                  bank[:, 6, 0:HEADS * NCH].rearrange("p (h c) -> p h c", h=HEADS), ACT.Exp), "exp_last")
                        dve_a.wait(act, "rest")
                        act_a.mark(act.activation(cols["exp_rest"][:, :, :], tmp[2][:, :, :], ACT.Exp), "exp_rest")

                    @block.vector
                    def _(dve):
                        dve_a.ready(dve)
                        link = linker(dve, chain)
                        ab = bank[:, 4, 0:P].rearrange("p (t x h) -> p x h t", x=2, h=HEADS)
                        dve.wait_ge(row_loaded, 32)
                        pool_a.wait(dve, "masks")
                        pe_a.wait(dve, "ab")
                        act_a.wait(dve, "beta")
                        dve_a.mark(dve.tensor_tensor(a_in[:, :, :], ab[:, 0], dt_bias[:, :].unsqueeze(2).broadcast_to([P, HEADS, NCH]),
                                                     ALU.add), "a_in")
                        act_a.wait(dve, "exp")
                        log1p_steps(dve, link, tmp[2][:, :, :], tmp[1][:, :, :], tmp[3][:, :, :], tmp[4][:, :, :])
                        link(dve.scalar_tensor_tensor(out=tmp[2][:, :, :], in0=a_in[:, :, :], scalar=0.0, in1=tmp[2][:, :, :],
                                                      op0=ALU.max, op1=ALU.add))
                        act_a.wait(dve, "neg_a")
                        dve_a.mark(dve.scalar_tensor_tensor(out=step[:, :, :], in0=tmp[2][:, :, :], scalar=-1.0,
                                                            in1=neg_a[:, :].unsqueeze(2).broadcast_to([P, HEADS, NCH]),
                                                            op0=ALU.mult, op1=ALU.mult), "g_step")
                        pe_a.wait(dve, "cum")
                        dve_a.mark(dve.tensor_copy(cols["g"][:, :, :], bank[:, 5, 0:HEADS * NCH].rearrange("p (h c) -> p h c", h=HEADS)), "g")
                        pe_a.wait(dve, "last")
                        act_a.wait(dve, "exp_last")
                        dve_a.wait(dve, "g")
                        dve_a.mark(dve.tensor_tensor(tmp[2][:, :, :], bank[:, 6, 0:HEADS * NCH].rearrange("p (h c) -> p h c", h=HEADS),
                                                     cols["g"][:, :, :], ALU.subtract), "rest")
                        act_a.wait(dve, "exp_g")
                        dve_a.mark(dve.scalar_tensor_tensor(out=cols["neg_beta_exp_g"][:, :, :], in0=cols["beta"][:, :, :], scalar=-1.0,
                                                            in1=cols["exp_g"][:, :, :], op0=ALU.mult, op1=ALU.mult), "neg")

            PAD = TAPS4 - 1
            padded = sb("qkv_padded", [P, 3, PAD + S], scope)
            tok_shape = [P, NCH, P]
            cq, ck, cv = (sb(n, [P, S], scope) for n in ("cq", "ck", "cv"))
            silu_z = sb("silu_z", [P, S], scope)
            k_tok, k_rest, v_tok, buf_a, buf_b, buf_c = (sb(n, tok_shape, scope) for n in ("k_tok", "k_rest", "v_tok", "buf_a", "buf_b", "buf_c"))
            kT, kbT, part0 = (sb(n, tok_shape, scope) for n in ("kT", "kbT", "part0"))
            decayT, attnT = (sb(n, tok_shape, scope) for n in ("decayT", "attnT"))
            kb_tok = ck[:, :].rearrange("p (c d) -> p c d", c=NCH)
            qT = cq[:, :].rearrange("p (c d) -> p c d", c=NCH)
            AT, inv, invT = buf_a, buf_b, buf_c
            part = [part0, k_tok]
            prod = kbT
            o_tok, o_normed = kb_tok, AT
            memory = sb("memory", [P, P], scope)
            delta = sb("delta", [P, 2, P], scope)
            g_col = sb("g_col", [P, NCH], scope)
            stat = sb("gdn_stat", [P, 4, NCH], scope)
            eps2 = sb("gdn_eps", [P, 2], scope)
            pj_pe = Steps(sem("gdn_proj_pe"), ["q", "k", "v", "z"])
            pj_act = Steps(sem("gdn_proj_act"), ["q_in", "k_in", "v_in", "z"])
            hd_pe = Steps(sem("gdn_pe"), ["g_row", "k_flip", "q_ss", "kT", "kbT", "qk", "kk", "Y1"]
                          + [n for s in levels[1:] for n in ((f"Y{s}", f"TY{s}", f"YT{s}") if s < 64 else ("v_flip", f"Y{s}", f"YT{s}"))]
                          + [f"{n}{c}" for c in range(NCH) for n in ("read", "new", "mem", "o")] + ["o_flip"])
            hd_act = Steps(sem("gdn_act"), ["decay", "k_silu", "k_sq", "k_rms", "q_silu", "q_sq", "q_rms", "kT", "kbT"]
                           + [n for s in levels[1:] for n in ((f"prod{s}",) if s != 32 else (f"prod{s}", "v_silu"))]
                           + [f"{n}{c}" for c in range(NCH) for n in ("new", "o")] + ["o_sq", "o_rms"])
            hd_dve = Steps(sem("gdn_dve"), ["rel"] + [f"{n}{j}" for n in ("kc", "qc") for j in range(TAPS4)]
                           + ["k_ss", "k_inv", "k_tok", "q_inv", "q_dec", "attn", "AT", "inv1", "invT1", "vc0"]
                           + [n for k, s in enumerate(levels[1:]) for n in ((f"inv{s}", f"invT{s}") if s < 64 else ("v_tok", f"invT{s}"))
                              + ((f"vc{k + 1}",) if k + 1 < TAPS4 else ())]
                           + ["mem_zero"] + [f"{n}{c}" for c in range(NCH) for n in ("delta", "mem", "o")]
                           + ["g_col", "o_ss", "o_inv", "o_tok", "y"])
            hd_pool = Steps(sem("gdn_pool"), ["rel", "kb_tok", "k_rest"] + [f"part{s}" for s in levels])
            gdn_zero, g_first = sem("gdn_zero"), sem("gdn_g_first")
            q0 = quads[0]
            quads[0] += HEADS
            R4, R5 = pair(2).rearrange("p (c d) -> p c d", c=NCH), pair(3).rearrange("p (c d) -> p c d", c=NCH)

            def per_tok(name, h):
                return cols[name][:, h, :].unsqueeze(2).broadcast_to(tok_shape)

            def along(m):
                return m.unsqueeze(1).broadcast_to(tok_shape)

            def for_heads(eng, body):
                with eng.Fori(0, HEADS - 1) as h:
                    body(h, h + 1)
                body(HEADS - 1, None)

            with nc.Block() as block:
                @block.sync
                def _(sp):
                    w = a["gdn_in_w"][0].rearrange("(k p) c -> p k c", p=P)
                    with sp.Fori(0, HEADS) as h:
                        for b, name in enumerate(("q", "k", "v", "z")):
                            pj_pe.wait(sp, name, h, back=1)
                            sp.dma_start(ring[:, b, :, :], w[:, :, bass.ts(h + b * HEADS, P)]).then_inc(w_loaded[b], 16)
                    pj_pe.wait(sp, "z", HEADS - 1)
                    load_first_half(sp, a["gdn_out_w"][0], 1)

                @block.gpsimd
                def _(g):
                    hd_pool.ready(g)
                    g.memset(padded[:, :, 0:PAD], 0.0).then_inc(gdn_zero, 1)
                    g.memset(eps2[:, 0:1], EPS).then_inc(gdn_zero, 1)
                    g.memset(eps2[:, 1:2], EPS * P).then_inc(gdn_zero, 1)

                    def body(h, _):
                        hd_dve.wait(g, "rel", h)
                        hd_pool.mark(g.tensor_tensor(decayT[:, :, :], decayT[:, :, :], along(causal[:, :]), ALU.add), "rel")
                        hd_dve.wait(g, "k_tok", h)
                        hd_pe.wait(g, "k_flip", h)
                        hd_pool.mark(g.tensor_tensor(kb_tok, k_tok[:, :, :], per_tok("beta", h), ALU.mult), "kb_tok")
                        hd_pool.mark(g.tensor_tensor(k_rest[:, :, :], k_tok[:, :, :], per_tok("exp_rest", h), ALU.mult), "k_rest")
                        hd_dve.wait(g, "AT", h)
                        hd_pe.wait(g, "kT", h)
                        hd_pool.wait(g, "k_rest", h)
                        for n, s in enumerate(levels):
                            if n >= 2:
                                hd_pe.wait(g, f"Y{levels[n - 2]}", h)
                            if n == 2:
                                hd_dve.wait(g, "invT1", h)
                            hd_pool.mark(g.tensor_tensor(part[n % 2][:, :, :], AT[:, :, :], along(level_mask[:, n, :]), ALU.mult), f"part{s}")
                    for_heads(g, body)

                @block.tensor
                def _(pe):
                    hd_pe.ready(pe)
                    pj_pe.ready(pe)

                    def project_head(head):
                        for b, name in enumerate(("q", "k", "v", "z")):
                            pe.wait_ge(w_loaded[b], (head + (q0 + 1)) * 16)
                            if b < 2:
                                pj_act.wait(pe, ("v_in", "z")[b], head, back=1)
                            else:
                                pj_act.wait(pe, ("q_in", "k_in")[b - 2], head)
                            for n in range(2):
                                for k in range(KT):
                                    last = nc.tensor.matmul(bank[:, 2 * (b % 2) + n, :], ring[:, b, k, :], hT[:, k, n * HALF:(n + 1) * HALF],
                                                            start=(k == 0), stop=(k == KT - 1))
                                    if (n, k) == (1, KT - 1):
                                        pj_pe.mark(last, name)
                                    yield

                    def each(dst, lhs, rhs, name):
                        for c in range(NCH):
                            last = nc.tensor.matmul(dst[:, c, :], lhs(c), rhs(c), start=True, stop=True)
                        hd_pe.mark(last, name)

                    def flip(dst, src, name):
                        for c in range(NCH):
                            last = nc.tensor.transpose(dst[:, c, :], src(c), ident[:, :])
                        hd_pe.mark(last, name)

                    def body(h, after):
                        coming = project_head(after) if after is not None else iter(())

                        def fill(n):
                            for _ in range(n):
                                next(coming, None)

                        hd_dve.wait(pe, "g_col", h, back=1)
                        hd_dve.wait(pe, f"o{NCH - 1}", h, back=1)
                        for c in range(NCH):
                            last = nc.tensor.matmul(R5[:, c, :], g_col[:, c:c + 1].broadcast_to([P, P]), ident[:, :], start=True, stop=True)
                        hd_pe.mark(last, "g_row")
                        fill(6)
                        hd_act.wait(pe, "k_silu", h)
                        hd_dve.wait(pe, "y", h, back=1)
                        flip(R4, lambda c: ck[:, c * P:(c + 1) * P], "k_flip")
                        fill(5)
                        hd_act.wait(pe, "q_sq", h)
                        hd_dve.wait(pe, "rel", h)
                        for c in range(NCH):
                            last = nc.tensor.matmul(R5[:, 0, c:c + 1], prod[:, c, :], ones[:, 0:1], start=True, stop=True)
                        hd_pe.mark(last, "q_ss")
                        hd_dve.wait(pe, "k_tok", h)
                        hd_act.wait(pe, "q_rms", h)
                        flip(R5, lambda c: k_tok[:, c, :], "kT")
                        fill(3)
                        hd_pool.wait(pe, "kb_tok", h)
                        hd_act.wait(pe, "k_sq", h)
                        flip(R4, lambda c: kb_tok[:, c, :], "kbT")
                        fill(1)
                        hd_act.wait(pe, "kT", h)
                        each(R5, lambda c: kT[:, c, :], lambda c: qT[:, c, :], "qk")
                        hd_act.wait(pe, "kbT", h)
                        each(R4, lambda c: kT[:, c, :], lambda c: kbT[:, c, :], "kk")
                        fill(4)
                        hd_dve.wait(pe, "AT", h)
                        hd_pool.wait(pe, "part1", h)
                        each(R4, lambda c: part[0][:, c, :], lambda c: ident[:, :], "Y1")
                        for n, s in enumerate(levels):
                            if n == 0:
                                continue
                            fill(1)
                            hd_dve.wait(pe, f"inv{levels[n - 1]}", h)
                            if s == 64:
                                hd_act.wait(pe, "v_silu", h)
                                flip(R5, lambda c: cv[:, c * P:(c + 1) * P], "v_flip")
                            hd_pool.wait(pe, f"part{s}", h)
                            hd_dve.wait(pe, f"invT{levels[n - 1]}", h)
                            each(R4, lambda c: part[n % 2][:, c, :], lambda c: inv[:, c, :], f"Y{s}")
                            fill(2)
                            hd_act.wait(pe, f"prod{s}", h)
                            if s < 64:
                                if n == 1:
                                    hd_dve.wait(pe, "attn", h)
                                each(R5, lambda c: invT[:, c, :], lambda c: prod[:, c, :], f"TY{s}")
                            each(R4, lambda c: prod[:, c, :], lambda c: invT[:, c, :], f"YT{s}")
                        for c in range(NCH):
                            fill(2)
                            if c == 0:
                                hd_dve.wait(pe, "invT64", h)
                                hd_dve.wait(pe, "mem_zero", h)
                                hd_dve.wait(pe, "v_tok", h)
                            else:
                                hd_dve.wait(pe, f"mem{c - 1}", h)
                            hd_pe.mark(nc.tensor.matmul(R4[:, 0, :], kT[:, c, :], memory[:, :], start=True, stop=True), f"read{c}")
                            if c:
                                hd_dve.wait(pe, f"o{c - 1}", h)
                                hd_act.wait(pe, f"o{c - 1}", h)
                            nc.tensor.matmul(R5[:, 4, :], qT[:, c, :], memory[:, :], start=True, stop=True)
                            hd_dve.wait(pe, f"delta{c}", h)
                            hd_pe.mark(nc.tensor.matmul(R4[:, 4, :], invT[:, c, :], delta[:, 0, :], start=True, stop=True), f"new{c}")
                            hd_act.wait(pe, f"new{c}", h)
                            hd_pool.wait(pe, "k_rest", h)
                            hd_pe.mark(nc.tensor.matmul(R5[:, 0, :], k_rest[:, c, :], delta[:, 1, :], start=True, stop=True), f"mem{c}")
                            hd_pe.mark(nc.tensor.matmul(R4[:, 4, :], attnT[:, c, :], delta[:, 1, :], start=True, stop=True), f"o{c}")
                        fill(64)
                        hd_dve.wait(pe, "o_tok", h)
                        flip(R4, lambda c: o_normed[:, c, :], "o_flip")

                    for _ in project_head(0):
                        pass
                    pe.wait_ge(g_first, 1)
                    for_heads(pe, body)

                @block.scalar
                def _(act):
                    hd_act.ready(act)
                    pj_act.ready(act)
                    act.wait_ge(gdn_zero, 3)

                    def take(head, n, name):
                        pj_pe.wait(act, name, head)
                        hd_dve.wait(act, f"{name}c{TAPS4 - 1}", head, back=1)
                        pj_act.mark(act.activation(padded[:, n, PAD:], pair(n % 2), ACT.Copy), f"{name}_in")

                    def take_z(head):
                        pj_pe.wait(act, "z", head)
                        hd_dve.wait(act, "y", head, back=1)
                        pj_act.mark(act.activation(silu_z[:, :], pair(1), ACT.Silu), "z")

                    def body(h, after):
                        hd_pool.wait(act, "rel", h)
                        hd_act.mark(act.activation(decayT[:, :, :], decayT[:, :, :], ACT.Exp), "decay")
                        hd_dve.wait(act, f"kc{TAPS4 - 1}", h)
                        hd_act.mark(act.activation(ck[:, :], ck[:, :], ACT.Silu), "k_silu")
                        hd_pe.wait(act, "k_flip", h)
                        hd_act.mark(act.activation(inv[:, :, :], R4, ACT.Square), "k_sq")
                        hd_dve.wait(act, f"qc{TAPS4 - 1}", h)
                        hd_dve.wait(act, "k_ss", h)
                        hd_act.mark(act.activation(stat[:, 0, :], stat[:, 0, :], ACT.Sqrt, bias=eps2[:, 0:1]), "k_rms")
                        hd_act.mark(act.activation(cq[:, :], cq[:, :], ACT.Silu), "q_silu")
                        hd_act.wait(act, "q_silu", h)
                        hd_act.mark(act.activation(prod[:, :, :], qT, ACT.Square), "q_sq")
                        hd_pe.wait(act, "q_ss", h)
                        hd_act.mark(act.activation(stat[:, 1, :], R5[:, 0, 0:NCH], ACT.Sqrt, bias=eps2[:, 1:2], scale=float(P)), "q_rms")
                        for name, r, dst in (("kT", R5, kT), ("kbT", R4, kbT)):
                            hd_pe.wait(act, name, h)
                            hd_act.mark(act.activation(dst[:, :, :], r, ACT.Copy), name)
                        for s in levels[1:]:
                            hd_pe.wait(act, f"Y{s}", h)
                            hd_act.mark(act.activation(prod[:, :, :], R4, ACT.Copy), f"prod{s}")
                            if s == 4 and after is not None:
                                take(after, 0, "q")
                            if s == 32:
                                hd_dve.wait(act, f"vc{TAPS4 - 1}", h)
                                hd_act.mark(act.activation(cv[:, :], cv[:, :], ACT.Silu), "v_silu")
                        if after is not None:
                            take(after, 1, "k")
                        for c in range(NCH):
                            hd_pe.wait(act, f"new{c}", h)
                            hd_act.mark(act.activation(delta[:, 1, :], R4[:, 4, :], ACT.Copy), f"new{c}")
                            hd_dve.wait(act, "q_inv", h)
                            hd_pe.wait(act, f"o{c}", h)
                            hd_act.mark(act.activation(o_tok[:, c, :], R4[:, 4, :], ACT.Copy, scale=stat[:, 1, c:c + 1]), f"o{c}")
                            if c == 6 and after is not None:
                                take(after, 2, "v")
                        hd_dve.wait(act, f"o{NCH - 1}", h)
                        hd_act.mark(act.activation(inv[:, :, :], o_tok, ACT.Square), "o_sq")
                        hd_dve.wait(act, "o_ss", h)
                        hd_act.mark(act.activation(stat[:, 2, :], stat[:, 2, :], ACT.Sqrt, bias=eps2[:, 0:1], scale=1.0 / P), "o_rms")
                        if after is not None:
                            take_z(after)

                    for n, name in enumerate(("q", "k", "v")):
                        take(0, n, name)
                    take_z(0)
                    for_heads(act, body)

                @block.vector
                def _(dve):
                    hd_dve.ready(dve)
                    dve.wait_ge(gdn_zero, 3)

                    def tap(h, n, j, name, dst):
                        w = vec(f"gdn_conv{j}", h + n * HEADS)
                        if j == 0:
                            pj_act.wait(dve, f"{name}_in", h)
                            hd_dve.mark(dve.tensor_scalar(dst[:, :], padded[:, n, 0:S], w, None, ALU.mult), f"{name}c0")
                        else:
                            hd_dve.wait(dve, f"{name}c{j - 1}", h)
                            hd_dve.mark(dve.scalar_tensor_tensor(out=dst[:, :], in0=padded[:, n, j:j + S], scalar=w, in1=dst[:, :],
                                                                 op0=ALU.mult, op1=ALU.add), f"{name}c{j}")

                    def inverse_root(h, n, name, source):
                        hd_act.wait(dve, f"{name}_sq", h)
                        hd_dve.mark(dve.tensor_reduce(out=stat[:, n, :], in_=source, op=ALU.add, axis=AX.X), f"{name}_ss")
                        hd_act.wait(dve, f"{name}_rms", h)
                        hd_dve.mark(dve.reciprocal(stat[:, n, :], stat[:, n, :]), f"{name}_inv")
                        hd_dve.wait(dve, f"{name}_inv", h)
                        return stat[:, n, :].unsqueeze(2).broadcast_to(tok_shape)

                    dve.tensor_copy(g_col[:, :], cols["g"][:, 0, :]).then_inc(g_first, 1)

                    def body(h, after):
                        hd_pe.wait(dve, "g_row", h)
                        hd_dve.mark(dve.tensor_tensor(decayT[:, :, :], R5, per_tok("g", h), ALU.subtract), "rel")
                        for j in range(TAPS4):
                            tap(h, 1, j, "k", ck)
                        for j in range(TAPS4):
                            tap(h, 0, j, "q", cq)
                        by = inverse_root(h, 0, "k", inv[:, :, :])
                        hd_dve.mark(dve.tensor_tensor(k_tok[:, :, :], R4, by, ALU.mult), "k_tok")
                        hd_act.wait(dve, "q_rms", h)
                        hd_dve.mark(dve.reciprocal(stat[:, 1, :], stat[:, 1, :]), "q_inv")
                        hd_dve.wait(dve, "q_inv", h)
                        hd_dve.mark(dve.tensor_tensor(stat[:, 3, :], stat[:, 1, :], cols["exp_g"][:, h, :], ALU.mult), "q_dec")
                        hd_act.wait(dve, "decay", h)
                        hd_pe.wait(dve, "qk", h)
                        hd_dve.mark(dve.tensor_tensor(attnT[:, :, :], R5, decayT[:, :, :], ALU.mult), "attn")
                        hd_pe.wait(dve, "kk", h)
                        hd_dve.mark(dve.tensor_tensor(AT[:, :, :], R4, decayT[:, :, :], ALU.mult), "AT")
                        hd_pe.wait(dve, "Y1", h)
                        hd_dve.mark(dve.scalar_tensor_tensor(out=inv[:, :, :], in0=R4, scalar=-1.0, in1=along(ident[:, :]),
                                                             op0=ALU.mult, op1=ALU.add), "inv1")
                        hd_dve.mark(dve.scalar_tensor_tensor(out=invT[:, :, :], in0=part[0][:, :, :], scalar=-1.0, in1=along(ident[:, :]),
                                                             op0=ALU.mult, op1=ALU.add), "invT1")
                        tap(h, 2, 0, "v", cv)
                        for n, s in enumerate(levels):
                            if n == 0:
                                continue
                            if s < 64:
                                hd_dve.wait(dve, f"inv{levels[n - 1]}", h)
                                hd_pe.wait(dve, f"TY{s}", h)
                                hd_dve.mark(dve.tensor_tensor(inv[:, :, :], inv[:, :, :], R5, ALU.subtract), f"inv{s}")
                            else:
                                hd_pe.wait(dve, "v_flip", h)
                                hd_dve.mark(dve.tensor_tensor(v_tok[:, :, :], R5, per_tok("beta", h), ALU.mult), "v_tok")
                            hd_pe.wait(dve, f"YT{s}", h)
                            hd_dve.wait(dve, f"invT{levels[n - 1]}", h)
                            hd_dve.mark(dve.tensor_tensor(invT[:, :, :], invT[:, :, :], R4, ALU.subtract), f"invT{s}")
                            if n < TAPS4:
                                tap(h, 2, n, "v", cv)
                        hd_pe.wait(dve, f"o{NCH - 1}", h, back=1)
                        hd_dve.mark(dve.memset(memory[:, :], 0.0), "mem_zero")
                        for c in range(NCH):
                            hd_pe.wait(dve, f"read{c}", h)
                            hd_dve.mark(dve.scalar_tensor_tensor(out=delta[:, 0, :], in0=R4[:, 0, :],
                                                                 scalar=cols["neg_beta_exp_g"][:, h, c:c + 1],
                                                                 in1=v_tok[:, c, :], op0=ALU.mult, op1=ALU.add), f"delta{c}")
                            hd_pe.wait(dve, f"mem{c}", h)
                            hd_dve.mark(dve.scalar_tensor_tensor(out=memory[:, :], in0=memory[:, :], scalar=cols["exp_last"][:, h, c:c + 1],
                                                                 in1=R5[:, 0, :], op0=ALU.mult, op1=ALU.add), f"mem{c}")
                            hd_act.wait(dve, f"o{c}", h)
                            hd_dve.mark(dve.scalar_tensor_tensor(out=o_tok[:, c, :], in0=R5[:, 4, :], scalar=stat[:, 3, c:c + 1],
                                                                 in1=o_tok[:, c, :], op0=ALU.mult, op1=ALU.add), f"o{c}")
                        hd_dve.mark(dve.tensor_copy(g_col[:, :], cols["g"][:, h if after is None else after, :]), "g_col")
                        by = inverse_root(h, 2, "o", inv[:, :, :])
                        hd_dve.mark(dve.tensor_tensor(o_normed[:, :, :], o_tok, by, ALU.mult), "o_tok")
                        hd_pe.wait(dve, "o_flip", h)
                        hd_dve.mark(dve.scalar_tensor_tensor(out=yT[:, h, :], in0=pair(2), scalar=vec("onorm", 0), in1=silu_z[:, :],
                                                             op0=ALU.mult, op1=ALU.mult), "y")
                    for_heads(dve, body)
        project_out("out1", a["gdn_out_w"][0], 1)

        layers.close()
        with ExitStack() as scope:
            gain = sb("final_gain", [P, D], scope)
            junk = sb("final_junk", [P, 2, D], scope)
            sums = sb("final_sums", [P, TT], scope)
            gain_loaded = sem("final_gain_loaded")
            act_f = Steps(sem("final_act"), SQUARES)
            dve_f = Steps(sem("final_dve"), [f"tok{t}" for t in range(TT)])
            with nc.Block() as block:
                @block.sync
                def _(sp):
                    sp.dma_start(gain[:, :], a["final_g"].partition_broadcast(P)).then_inc(gain_loaded, 16)

                @block.vector
                def _(dve):
                    dve_f.ready(dve)
                    dve.wait_ge(gain_loaded, 16)
                    for t in range(TT):
                        dve_f.mark(dve.scalar_tensor_tensor(out=resid[:, t, :], in0=resid[:, t, :], scalar=inv_rms[:, t:t + 1], in1=gain[:, :],
                                                            op0=ALU.mult, op1=ALU.mult), f"tok{t}")
                    act_f.wait(dve, "rms")
                    dve_f.wait(dve, f"tok{TT - 1}")
                    dve.reciprocal(inv_rms[:, :], sums[:, :])

                @block.scalar
                def _(act):
                    act_f.ready(act)
                    token_rms(act, act_f, junk, sums, lambda t: dve_f.wait(act, f"tok{t}"))
        norm_transpose("norm2", lambda k: vec("pre_g", k), lambda k: 0.0)
        w_in = a["w_in_2"][0]
        CA, CB, ZC, US, ZS, GC, GS = (c // P for c in (0, D, 2 * D, 3 * D, 3 * D + 512, 4 * D, 5 * D))
        ST = GROUPS * GH // P
        u_dram = nc.dram_tensor("u_scratch", (ST * P, BLK, NBLK), F32, kind="Internal").ap()
        y_dram = nc.dram_tensor("y_scratch", (ST * P, BLK, NBLK), F32, kind="Internal").ap()
        ssm_y = sb("ssm_y", [P, ST, S])

        with ExitStack() as scope:
            u_perm = sb("u_perm", [P, 2, BLK, NBLK], scope)
            pe_u = Steps(sem("u_pe"), [f"tile{b}" for b in range(4)])
            act_u = Steps(sem("u_act"), [f"u{b}" for b in range(4)])
            u_stored = [sem("u_stored0"), sem("u_stored1")]
            q0 = quads[0]
            quads[0] += 1
            with nc.Block() as block:
                @block.sync
                def _(sp):
                    load_quad(sp, pe_u, 0, [(ring[:, b, :, :], columns(w_in, US + b)) for b in range(4)])
                    for b in range(4):
                        act_u.wait(sp, f"u{b}")
                        sp.dma_start(u_dram[b * P:(b + 1) * P], u_perm[:, b % 2, :, :]).then_inc(u_stored[b % 2], 16)
                    for p in range(2):
                        sp.wait_ge(u_stored[p], 32)

                @block.tensor
                def _(pe):
                    pe_u.ready(pe)
                    for b in range(4):
                        pe.wait_ge(w_loaded[b], (q0 + 1) * 16)
                        if b >= 2:
                            act_u.wait(pe, f"u{b - 2}")
                        pe_u.mark(project(b, hT), f"tile{b}")

                @block.scalar
                def _(act):
                    act_u.ready(act)
                    for b in range(4):
                        pe_u.wait(act, f"tile{b}")
                        if b >= 2:
                            act.wait_ge(u_stored[b % 2], 16)
                        act_u.mark(act.activation(u_perm[:, b % 2, :, :], pair(b % 2).rearrange("p (k t) -> p t k", t=BLK), ACT.Copy), f"u{b}")

        with ExitStack() as scope:
            flat = yT[:, :, :].rearrange("p k s -> p (k s)")
            lift = flat[:, 0:4096].rearrange("p (x j t h) -> p x j t h", x=2, j=PAIRS, t=BLK)
            kernel16 = flat[0:GH, 4096:8192].rearrange("p (g c) -> p g c", g=GROUPS)
            u_blk = flat[:, 0:4096].rearrange("p (g k) -> p g k", g=GROUPS)
            HP = PAIRS // 2
            w1, w2, w3, z_re = (flat[:, 4096 + n * 1024:5120 + n * 1024].rearrange("p (j k) -> p j k", j=HP) for n in range(4))
            turn = ring[:, :, :, :].rearrange("p b k c -> p (b k c)").rearrange("p (x j k) -> p x j k", x=2, j=PAIRS)
            turn_re, turn_im = turn[:, 0], turn[:, 1]
            B_lift = sb("B_lift", [P, 2, PAIRS, P], scope)
            C_pow = sb("C_pow", [P, 2, PAIRS, BLK + 1, GH], scope)
            K_lift = sb("K_lift", [P, GROUPS, P], scope)
            shrink = sb("shrink", [P, PAIRS, NBLK], scope)
            z_im = ssm_y[:, 2, :].rearrange("p (j k) -> p j k", j=HP)
            y_blk = ssm_y[:, 0:2, :].rearrange("p c (g k) -> p (c g) k", k=NBLK)
            st_re, st_im = (sb(n, [P, HP, NBLK + 2], scope) for n in ("st_re", "st_im"))
            par = sb("s5_par", [P, 24, PAIRS], scope)
            (lr, li, dt, mag, th, nn, red, co, si, ar, ai, den, zr, zi, x1, x2, c8, s8, rho, ab, ph) = (par[:, n, :] for n in range(21))
            pw = sb("s5_pow", [P, 2, BLK + 1, PAIRS], scope)
            bb = sb("s5_b", [P, 4, PAIRS, GH], scope)
            cc = sb("s5_c", [P, 2, PAIRS, GH], scope)
            c_rows = ssm_y[:, 3, :].rearrange("p (x t g s) -> p x t g s", x=2, t=ST, g=2)
            d16 = sb("s5_d", [GH, 2, PAIRS], scope)
            half_pi = sb("half_pi", [P, 1], scope)
            par_loaded, c_loaded, d_loaded, u_loaded = sem("par_loaded"), sem("c_loaded"), sem("d_loaded"), sem("u_loaded")
            K_placed, y_stored, y_loaded = sem("K_placed"), sem("y_stored"), sem("y_loaded")
            pe_s = Steps(sem("s5_pe"), ["c_flip", "kernel", "B_flip"] + [f"{n}{h}" for h in range(2) for n in ("w", "y")])
            act_s = Steps(sem("s5_act"), ["dt", "mag", "rho", "sin", "cos_abs", "cos", "kernel", "B", "y0", "y1"]
                          + [f"gelu{n}" for n in range(ST)])
            dve_s = Steps(sem("s5_dve"), ["rates", "reduced", "c", "b", "C", "lift", "kernel", "s0", "s1"])
            pool_s = Steps(sem("s5_pool"), ["zero"])
            chain = sem("s5_chain")
            with nc.Block() as block:
                @block.sync
                def _(sp):
                    for g in range(2):
                        half = slice(g * NS, (g + 1) * NS)
                        sp.dma_start(lr[half], a["ssm_lambda_re_2"][0].rearrange("(j g) p -> g p j", g=2)[g], allow_slow_non_contiguous=True).then_inc(par_loaded, 16)
                        sp.dma_start(li[half], a["ssm_lambda_im_2"][0].rearrange("(j g) p -> g p j", g=2)[g], allow_slow_non_contiguous=True).then_inc(par_loaded, 16)
                        sp.dma_start(dt[half], a["ssm_log_dt_2"][0].rearrange("(j g) -> g j", g=2)[g].partition_broadcast(NS), allow_slow_non_contiguous=True).then_inc(par_loaded, 16)
                        for x, n in enumerate(("ssm_b_re_2", "ssm_b_im_2")):
                            sp.dma_start(bb[half, x], a[n][0].rearrange("(j g) p h -> g p j h", g=2)[g]).then_inc(par_loaded, 16)
                        for x, n in enumerate(("ssm_c_re_2", "ssm_c_im_2")):
                            sp.dma_start(c_rows[:, x, :, g, :], a[n][0].rearrange("(t r) h p -> (r h) t p", t=ST)).then_inc(c_loaded, 16)
                        sp.dma_start(d16[:, g, :], a["ssm_d_2"][0].rearrange("(j g) h -> g h j", g=2)[g],
                                     allow_slow_non_contiguous=True).then_inc(d_loaded, 16)
                    dve_s.wait(sp, "kernel")
                    pool_s.wait(sp, "zero")
                    for r in range(BLK):
                        sp.dma_start(K_lift[r * GH:(r + 1) * GH, :, (BLK - 1 - r) * GH:], kernel16[:, :, 0:(r + 1) * GH]).then_inc(K_placed, 16)
                    pe_s.wait(sp, "B_flip")
                    for t in range(BLK):
                        sp.dma_start(u_blk[(BLK - 1 - t) * GH:(BLK - t) * GH, :, :],
                                     u_dram.rearrange("(g h) t k -> t h g k", h=GH)[t]).then_inc(u_loaded, 16)
                    for h in range(2):
                        act_s.wait(sp, f"y{h}")
                        for t in range(BLK):
                            for g in range(2):
                                sp.dma_start(y_dram.rearrange("(j g h) t k -> t g h j k", h=GH, g=2)[t, g][:, h * HP:(h + 1) * HP, :],
                                             y_blk[t * GH:(t + 1) * GH, g * HP:(g + 1) * HP, :]).then_inc(y_stored, 16)
                        sp.wait_ge(y_stored, (h + 1) * 2 * BLK * 16)
                    sp.dma_start(flat[:, 4096:8192].rearrange("p (c x) -> p c x", c=ST),
                                 y_dram.rearrange("(c p) t k -> p c (t k)", p=P)).then_inc(y_loaded, 16)
                    sp.wait_ge(y_loaded, 16)

                @block.gpsimd
                def _(g):
                    pool_s.ready(g)
                    g.memset(half_pi[:, :], math.pi / 2)
                    g.memset(st_re[:, :, 0:1], 0.0)
                    g.memset(st_im[:, :, 0:1], 0.0)
                    pool_s.mark(g.memset(K_lift[:, :, :], 0.0), "zero")

                @block.tensor
                def _(pe):
                    pe_s.ready(pe)
                    pe.wait_ge(c_loaded, 64)
                    for x in range(2):
                        for t in range(ST):
                            last = nc.tensor.transpose(bank[:, x, t * P:(t + 1) * P], c_rows[:, x, t, :, :].rearrange("p g s -> p (g s)"), ident[:, :])
                    pe_s.mark(last, "c_flip")
                    dve_s.wait(pe, "C")
                    dve_s.wait(pe, "b")
                    for n in range(GROUPS):
                        g, j = n % 2, n // 2
                        half = slice(g * NS, (g + 1) * NS)
                        dst = bank[0:GH, 4 * g + j // 4, (j % 4) * P:(j % 4 + 1) * P]
                        for x in range(2):
                            last = nc.tensor.matmul(dst, bb[half, 2 + x, j, :], C_pow[half, x, j, 0:BLK, :].rearrange("p t h -> p (t h)"),
                                                    start=(x == 0), stop=(x == 1))
                    pe_s.mark(last, "kernel")
                    dve_s.wait(pe, "lift")
                    act_s.wait(pe, "kernel")
                    for x in range(2):
                        for j in range(PAIRS):
                            last = nc.tensor.transpose(bank[:, 4 * x + j // 4, (j % 4) * P:(j % 4 + 1) * P],
                                                       lift[:, x, j].rearrange("p t h -> p (t h)"), ident[:, :])
                    pe_s.mark(last, "B_flip")
                    act_s.wait(pe, "B")
                    pe.wait_ge(u_loaded, BLK * 16)
                    pe.wait_ge(K_placed, BLK * 16)
                    for h in range(2):
                        if h:
                            dve_s.wait(pe, "s0")
                        for x in range(2):
                            for jl in range(HP):
                                for g in range(2):
                                    j = h * HP + jl
                                    last = nc.tensor.matmul(bank[g * NS:(g + 1) * NS, 2 * x + jl // 4, (jl % 4) * P:(jl % 4 + 1) * P],
                                                            B_lift[:, x, j, g * NS:(g + 1) * NS], u_blk[:, 2 * j + g, :], start=True, stop=True)
                        pe_s.mark(last, f"w{h}")
                        dve_s.wait(pe, f"s{h}")
                        if h:
                            act_s.wait(pe, "y0")
                        for n in range(2 * HP):
                            g, jl = n % 2, n // 2
                            half, j = slice(g * NS, (g + 1) * NS), h * HP + jl
                            dst = bank[:, 4 + 2 * g + jl // 4, (jl % 4) * P:(jl % 4 + 1) * P]
                            nc.tensor.matmul(dst, K_lift[:, g * PAIRS + j, :], u_blk[:, 2 * j + g, :], start=True, stop=False)
                            nc.tensor.matmul(dst, C_pow[half, 0, j, 1:, :].rearrange("p t h -> p (t h)"), st_re[half, jl, 0:NBLK], start=False, stop=False)
                            last = nc.tensor.matmul(dst, C_pow[half, 1, j, 1:, :].rearrange("p t h -> p (t h)"), st_im[half, jl, 0:NBLK],
                                                    start=False, stop=True)
                        pe_s.mark(last, f"y{h}")

                @block.scalar
                def _(act):
                    act_s.ready(act)
                    act.wait_ge(par_loaded, 160)
                    act_s.mark(act.activation(dt, dt, ACT.Exp), "dt")
                    dve_s.wait(act, "rates")
                    act_s.mark(act.activation(mag, x1, ACT.Exp), "mag")
                    act_s.mark(act.activation(rho, x1, ACT.Exp, scale=float(BLK)), "rho")
                    pool_s.wait(act, "zero")
                    dve_s.wait(act, "reduced")
                    act_s.mark(act.activation(si, red, ACT.Sin), "sin")
                    act_s.mark(act.activation(ab, red, ACT.Abs), "cos_abs")
                    act_s.wait(act, "cos_abs")
                    act_s.mark(act.activation(co, ab, ACT.Sin, scale=-1.0, bias=half_pi[:, 0:1]), "cos")
                    pe_s.wait(act, "kernel")
                    dve_s.wait(act, "lift")
                    act_s.mark(act.activation(kernel16.rearrange("p g c -> p (g c)"), bank[0:GH, :, :].rearrange("p b c -> p (b c)"), ACT.Copy), "kernel")
                    pe_s.wait(act, "B_flip")
                    act_s.mark(act.activation(B_lift[:, :, :, :].rearrange("p x j c -> p (x j c)"), bank[:, :, :].rearrange("p b c -> p (b c)"), ACT.Copy), "B")
                    for h in range(2):
                        pe_s.wait(act, f"y{h}")
                        if h:
                            act.wait_ge(y_stored, 2 * BLK * 16)
                        act_s.mark(act.activation(y_blk[:, :, :].rearrange("p g k -> p (g k)"), bank[:, 4:8, :].rearrange("p b c -> p (b c)"), ACT.Copy), f"y{h}")
                    act.wait_ge(y_loaded, 16)
                    for n in range(ST):
                        act_s.mark(act.activation(ssm_y[:, n, :].rearrange("p (k t) -> p t k", t=BLK),
                                                  flat[:, 4096 + n * S:4096 + (n + 1) * S].rearrange("p (t k) -> p t k", t=BLK),
                                                  ACT.Gelu_apprx_tanh), f"gelu{n}")

                @block.vector
                def _(dve):
                    dve_s.ready(dve)
                    link = linker(dve, chain)
                    TT_, TS, STT = dve.tensor_tensor, dve.tensor_scalar, dve.scalar_tensor_tensor

                    def cmul(out_re, out_im, xr, xi, yr, yi, t):
                        TT_(t[0], xr, yr, ALU.mult)
                        link(TT_(t[1], xi, yi, ALU.mult))
                        link(TT_(out_re, t[0], t[1], ALU.subtract))
                        TT_(t[0], xr, yi, ALU.mult)
                        link(TT_(t[1], xi, yr, ALU.mult))
                        link(TT_(out_im, t[0], t[1], ALU.add))

                    act_s.wait(dve, "dt")
                    link(TT_(th, li, dt, ALU.mult))
                    dve_s.mark(TT_(x1, lr, dt, ALU.mult), "rates")
                    MAGIC = 1.5 * 2.0 ** 23
                    link(TS(nn, th, 1.0 / (2 * math.pi), MAGIC, ALU.mult, ALU.add))
                    link(TS(nn, nn, -MAGIC, None, ALU.add))
                    two_pi = [6.28125, float(np.float32(2 * math.pi - 6.28125) - np.float32(2 * math.pi - 6.28125) % np.float32(2.0 ** -21))]
                    two_pi.append(2 * math.pi - sum(two_pi))
                    link(STT(out=red, in0=nn, scalar=-two_pi[0], in1=th, op0=ALU.mult, op1=ALU.add))
                    link(STT(out=red, in0=nn, scalar=-two_pi[1], in1=red, op0=ALU.mult, op1=ALU.add))
                    link(STT(out=red, in0=nn, scalar=-two_pi[2], in1=red, op0=ALU.mult, op1=ALU.add))
                    dve_s.mark(TS(red, red, 3.1415925, -3.1415925, ALU.min, ALU.max), "reduced")
                    pe_s.wait(dve, "c_flip")
                    for g in range(2):
                        half = slice(g * NS, (g + 1) * NS)
                        ins = dve.tensor_copy(cc[half, :, :, :].rearrange("p x (t j) h -> p (x t) j h", t=ST),
                                              bank[half, 0:2, :].rearrange("p x (t j g h) -> p (x t) j g h", t=ST, g=2, h=GH)[:, :, :, g, :])
                    dve_s.mark(ins, "c")
                    act_s.wait(dve, "cos")
                    TT_(ar, mag, co, ALU.mult)
                    TT_(ai, mag, si, ALU.mult)
                    TT_(x2, lr, lr, ALU.mult)
                    link(TT_(den, li, li, ALU.mult))
                    link(TT_(den, den, x2, ALU.add))
                    link(dve.reciprocal(den, den))
                    link(TS(x2, ar, -1.0, None, ALU.add))
                    TT_(zr, x2, lr, ALU.mult)
                    TT_(zi, ai, lr, ALU.mult)
                    link(TT_(nn, ai, li, ALU.mult))
                    link(TT_(zr, zr, nn, ALU.add))
                    link(TT_(nn, x2, li, ALU.mult))
                    link(TT_(zi, zi, nn, ALU.subtract))
                    link(TT_(zr, zr, den, ALU.mult))
                    link(TT_(zi, zi, den, ALU.mult))
                    wide = [P, PAIRS, GH]
                    f1, f2 = (w.rearrange("p j k -> p (j k)") for w in (w1, w2))
                    by_h = lambda v: v.unsqueeze(2).broadcast_to(wide)
                    small = [f[:, 0:256].rearrange("p (j h) -> p j h", j=PAIRS) for f in (f1, f2)]
                    cmul(bb[:, 2], bb[:, 3], bb[:, 0], bb[:, 1], by_h(zr), by_h(zi), small)
                    TS(pw[:, 0, 0, :], lr, 0.0, 1.0, ALU.mult, ALU.add)
                    TS(pw[:, 1, 0, :], lr, 0.0, None, ALU.mult)
                    dve.tensor_copy(pw[:, 0, 1, :], ar)
                    dve_s.mark(dve.tensor_copy(pw[:, 1, 1, :], ai), "b")
                    dve_s.wait(dve, "b")
                    for n in (1, 2, 4):
                        shape = [P, n, PAIRS]
                        t = [f[:, 0:n * PAIRS].rearrange("p (n j) -> p n j", n=n) for f in (f1, f2)]
                        cmul(pw[:, 0, n + 1:2 * n + 1, :], pw[:, 1, n + 1:2 * n + 1, :], pw[:, 0, 1:n + 1, :], pw[:, 1, 1:n + 1, :],
                             pw[:, 0, n:n + 1, :].broadcast_to(shape), pw[:, 1, n:n + 1, :].broadcast_to(shape), t)
                    for n in range(BLK + 1):
                        pr, pi = by_h(pw[:, 0, n, :]), by_h(pw[:, 1, n, :])
                        TT_(small[0], cc[:, 0], pr, ALU.mult)
                        link(TT_(small[1], cc[:, 1], pi, ALU.mult))
                        link(TT_(C_pow[:, 0, :, n, :], small[0], small[1], ALU.subtract))
                        TT_(small[0], cc[:, 0], pi, ALU.mult)
                        link(TT_(small[1], cc[:, 1], pr, ALU.mult))
                        ins = STT(out=C_pow[:, 1, :, n, :], in0=small[0], scalar=-1.0, in1=small[1], op0=ALU.mult, op1=ALU.subtract)
                        if n < BLK:
                            link(ins)
                    dve_s.mark(ins, "C")
                    dve_s.wait(dve, "C")
                    for n in range(BLK):
                        cmul(lift[:, 0, :, n, :], lift[:, 1, :, n, :], bb[:, 2], bb[:, 3], by_h(pw[:, 0, n, :]), by_h(pw[:, 1, n, :]), small)
                    dve_s.mark(TS(c8, co, 1.0, None, ALU.mult), "lift")
                    act_s.wait(dve, "kernel")
                    dve.wait_ge(d_loaded, 32)
                    diag = [GH, GROUPS, GH]
                    dI = bb[0:GH, 0:2, :, :].rearrange("p x j h -> p (x j) h")
                    link(TT_(dI, d16[:, :, :].rearrange("p g j -> p (g j)").unsqueeze(2).broadcast_to(diag), ident[0:GH, 0:GH].unsqueeze(1).broadcast_to(diag), ALU.mult))
                    dve_s.mark(TT_(kernel16[:, :, 0:GH], kernel16[:, :, 0:GH], dI, ALU.add), "kernel")
                    link(dve.tensor_copy(s8, si))
                    t = [ab, ph]
                    for _ in range(3):
                        cmul(x2, nn, c8, s8, c8, s8, t)
                        dve.tensor_copy(c8, x2)
                        link(dve.tensor_copy(s8, nn))
                    for r in range(1):
                        dve.wait_ge(K_placed, BLK * 16)
                    TS(turn_re[:, :, 0:1], lr.unsqueeze(2), 0.0, 1.0, ALU.mult, ALU.add)
                    link(TS(turn_im[:, :, 0:1], lr.unsqueeze(2), 0.0, None, ALU.mult))
                    n = 1
                    while n < NBLK:
                        shape = [P, PAIRS, n]
                        t = [f.rearrange("p (j k) -> p j k", j=PAIRS)[:, :, 0:n] for f in (f1, f2)]
                        cmul(turn_re[:, :, n:2 * n], turn_im[:, :, n:2 * n], turn_re[:, :, 0:n], turn_im[:, :, 0:n],
                             c8.unsqueeze(2).broadcast_to(shape), s8.unsqueeze(2).broadcast_to(shape), t)
                        n *= 2
                        if n < NBLK:
                            cmul(x2, nn, c8, s8, c8, s8, [ab, ph])
                            dve.tensor_copy(c8, x2)
                            link(dve.tensor_copy(s8, nn))
                    act_s.wait(dve, "rho")
                    link(dve.tensor_copy(shrink[:, :, :], rho.unsqueeze(2).broadcast_to([P, PAIRS, NBLK])))
                    link(dve.memset(shrink[:, :, 0:1], 0.0))
                    pool_s.wait(dve, "zero")
                    for h in range(2):
                        rows_ = slice(h * HP, (h + 1) * HP)
                        tr, ti = turn_re[:, rows_, :], turn_im[:, rows_, :]
                        w_re, w_im = (bank[:, 2 * x:2 * x + 2, :].rearrange("p b (j k) -> p (b j) k", k=NBLK) for x in range(2))
                        one = lambda v: v.rearrange("p j k -> p (j k)")
                        if h:
                            pe_s.wait(dve, "y0")
                        pe_s.wait(dve, f"w{h}")
                        TT_(w1, w_re, tr, ALU.mult)
                        link(TT_(w2, w_im, ti, ALU.mult))
                        link(TT_(w1, w1, w2, ALU.add))
                        TT_(w3, w_re, ti, ALU.mult)
                        link(TT_(w2, w_im, tr, ALU.mult))
                        link(TT_(w2, w2, w3, ALU.subtract))
                        sh = one(shrink[:, rows_, :])
                        dve.tensor_tensor_scan(one(z_re), sh, one(w1), 0.0, ALU.mult, ALU.add)
                        link(dve.tensor_tensor_scan(one(z_im[:, :, :]), sh, one(w2), 0.0, ALU.mult, ALU.add))
                        TT_(w1, z_re, tr, ALU.mult)
                        link(TT_(w2, z_im[:, :, :], ti, ALU.mult))
                        link(TT_(st_re[:, :, 1:NBLK + 1], w1, w2, ALU.subtract))
                        TT_(w1, z_re, ti, ALU.mult)
                        link(TT_(w2, z_im[:, :, :], tr, ALU.mult))
                        dve_s.mark(TT_(st_im[:, :, 1:NBLK + 1], w1, w2, ALU.add), f"s{h}")

        with ExitStack() as scope:
            sig = sb("glu_sig", [P, 2, S], scope)
            glu = sb("glu", [P, ST, S], scope)
            pe_g = Steps(sem("glu_pe"), [f"{n}{b}" for n in ("glu", "z") for b in range(4)])
            act_g = Steps(sem("glu_act"), [f"{n}{b}" for n in ("glu", "z") for b in range(4)])
            dve_g = Steps(sem("glu_dve"), [f"{n}{b}" for n in ("glu", "z") for b in range(4)])
            q0 = quads[0]
            quads[0] += 2
            with nc.Block() as block:
                @block.sync
                def _(sp):
                    for b in range(4):
                        sp.dma_start(ring[:, b, 0:ST, :], columns(a["w_ssm_glu_2"][0], b)).then_inc(w_loaded[b], 16)
                    for b in range(4):
                        pe_g.wait(sp, f"glu{b}")
                        sp.dma_start(ring[:, b, :, :], columns(w_in, ZS + b)).then_inc(w_loaded[b], 16)

                @block.tensor
                def _(pe):
                    pe_g.ready(pe)
                    for n, (name, src, kt) in enumerate((("glu", ssm_y, ST), ("z", hT, KT))):
                        for b in range(4):
                            pe.wait_ge(w_loaded[b], (q0 + n + 1) * 16)
                            if b >= 2:
                                act_g.wait(pe, f"{name}{b - 2}")
                            elif n:
                                act_g.wait(pe, f"glu{b + 2}")
                            pe_g.mark(project(b, src, kt), f"{name}{b}")

                @block.scalar
                def _(act):
                    act_g.ready(act)
                    for n, (name, f) in enumerate((("glu", ACT.Sigmoid), ("z", ACT.Silu))):
                        for b in range(4):
                            pe_g.wait(act, f"{name}{b}")
                            if b >= 2 or n:
                                dve_g.wait(act, f"{name}{b - 2}" if b >= 2 else f"glu{b + 2}")
                            act_g.mark(act.activation(sig[:, b % 2, :], pair(b % 2), f, bias=vec("glu_b", b) if n == 0 else 0.0), f"{name}{b}")

                @block.vector
                def _(dve):
                    dve_g.ready(dve)
                    for b in range(4):
                        act_g.wait(dve, f"glu{b}")
                        dve_g.mark(dve.tensor_tensor(glu[:, b, :], ssm_y[:, b, :], sig[:, b % 2, :], ALU.mult), f"glu{b}")
                    pe_g.wait(dve, "glu3")
                    for b in range(4):
                        act_g.wait(dve, f"z{b}")
                        dve_g.wait(dve, f"glu{b}")
                        dve_g.mark(dve.tensor_tensor(ssm_y[:, b, :], glu[:, b, :], sig[:, b % 2, :], ALU.mult), f"z{b}")

        silu_zc = sb("silu_zc", [P, KT, S])
        with ExitStack() as scope:
            PAD = TAPS31 - 1
            sig = sb("conv_sig", [P, 2, S], scope)
            padded = sb("conv_padded", [P, 2, PAD + S], scope)
            acc = sb("conv_acc", [P, 2, S], scope)
            taps = sb("conv_taps", [P, 2, 32], scope)
            z_ring = sb("conv_z_ring", [P, 2, KT, P], scope)
            pe_v, pe_z = Steps(sem("conv_pe"), ["a0", "b0", "a1", "b1"]), Steps(sem("conv_z_pe"), ["z0", "z1"])
            act_v, act_z = Steps(sem("conv_act"), ["sig0", "sig1"]), Steps(sem("conv_z_act"), ["z0", "z1"])
            dve_v = Steps(sem("conv_dve"), [s + str(p) for p in range(2) for s in ["taps", "cu"] + [f"t{j}_" for j in range(TAPS31)]])
            pad_zero = sem("conv_pad_zero")
            z_loaded = [sem("conv_z_loaded0"), sem("conv_z_loaded1")]
            q0 = quads[0]
            quads[0] += KT // 2
            with nc.Block() as block:
                @block.sync
                def _(sp):
                    with sp.Fori(0, KT // 2) as i:
                        load_quad(sp, pe_v, i, [(ring[:, 2 * p + x, :, :], columns(w_in, i * 2 + (p + (CA, CB)[x])))
                                                for p in range(2) for x in range(2)], names=("a0", "b0", "a1", "b1"))
                        for p in range(2):
                            pe_z.wait(sp, f"z{p}", i, back=1)
                            sp.dma_start(z_ring[:, p, :, :], columns(w_in, i * 2 + (p + ZC))).then_inc(z_loaded[p], 16)

                @block.gpsimd
                def _(g):
                    g.memset(padded[:, :, 0:PAD], 0.0).then_inc(pad_zero, 1)

                @block.tensor
                def _(pe):
                    pe_v.ready(pe)
                    pe_z.ready(pe)

                    def conv_tiles(i, p):
                        pe.wait_ge(w_loaded[2 * p], (i + (q0 + 1)) * 16)
                        dve_v.wait(pe, f"cu{p}", i, back=1)
                        pe_v.mark(project(3 * p, hT, w=ring[:, 2 * p]), f"a{p}")
                        pe.wait_ge(w_loaded[2 * p + 1], (i + (q0 + 1)) * 16)
                        act_v.wait(pe, f"sig{1 - p}", i, back=int(p == 0))
                        pe_v.mark(project(1, hT, w=ring[:, 2 * p + 1]), f"b{p}")

                    def z_tile(i, p):
                        pe.wait_ge(z_loaded[p], (i + 1) * 16)
                        act_z.wait(pe, f"z{1 - p}", i, back=int(p == 0))
                        pe_z.mark(project(2, hT, w=z_ring[:, p]), f"z{p}")

                    for p in range(2):
                        conv_tiles(0, p)
                    with pe.Fori(1, KT // 2) as i:
                        for p in range(2):
                            conv_tiles(i, p)
                            z_tile(i - 1, p)
                    for p in range(2):
                        z_tile(KT // 2 - 1, p)

                @block.scalar
                def _(act):
                    act_v.ready(act)
                    act_z.ready(act)

                    def sigmoid(i, p):
                        pe_v.wait(act, f"b{p}", i)
                        dve_v.wait(act, f"cu{p}", i, back=1)
                        act_v.mark(act.activation(sig[:, p, :], pair(1), ACT.Sigmoid), f"sig{p}")

                    def silu(i, p):
                        pe_z.wait(act, f"z{p}", i)
                        act_z.mark(act.activation(silu_zc[:, i * 2 + p, :], pair(2), ACT.Silu), f"z{p}")

                    for p in range(2):
                        sigmoid(0, p)
                    with act.Fori(1, KT // 2) as i:
                        for p in range(2):
                            sigmoid(i, p)
                            silu(i - 1, p)
                    for p in range(2):
                        silu(KT // 2 - 1, p)

                @block.vector
                def _(dve):
                    dve_v.ready(dve)
                    dve.wait_ge(pad_zero, 1)
                    with dve.Fori(0, KT // 2) as i:
                        for p in range(2):
                            n = i * 2 + p
                            dve.tensor_copy(taps[:, p, 0:16], vecs[:, 3, :].rearrange("p (j k) -> p k j", k=KT)[:, n, :])
                            dve_v.mark(dve.tensor_copy(taps[:, p, 16:TAPS31], vecs[:, 4, 0:15 * KT].rearrange("p (j k) -> p k j", k=KT)[:, n, :]), f"taps{p}")
                            act_v.wait(dve, f"sig{p}", i)
                            dve_v.mark(dve.tensor_tensor(padded[:, p, PAD:], pair(3 * p), sig[:, p, :], ALU.mult), f"cu{p}")
                            dve_v.wait(dve, f"cu{p}", i)
                            dve_v.mark(dve.tensor_scalar(acc[:, p, :], padded[:, p, 0:S], taps[:, p, 0:1], vec("conv_b2", n), ALU.mult, ALU.add), f"t0_{p}")
                            for j in range(1, TAPS31):
                                dve_v.wait(dve, f"t{j - 1}_{p}", i)
                                dst = acc[:, p, :] if j < TAPS31 - 1 else yT[:, n, :]
                                dve_v.mark(dve.scalar_tensor_tensor(out=dst, in0=padded[:, p, j:j + S], scalar=taps[:, p, j:j + 1],
                                                                    in1=acc[:, p, :], op0=ALU.mult, op1=ALU.add), f"t{j}_{p}")

        merged = sb("merged", [P, KT, S])
        with ExitStack() as scope:
            eps = sb("ln_eps", [P, 1], scope)
            sig = sb("ssm_sig", [P, 2, S], scope)
            sq, inv_std = merged[:, KT - 2:KT, :], merged[:, KT - 3, :]
            pe_n = Steps(sem("ln_pe"), ["sums"] + [f"sq{k}" for k in range(KT)])
            act_n = Steps(sem("ln_act"), [f"sq{k}" for k in range(KT)] + ["std"] + [f"silu{k}" for k in range(KT)])
            dve_n = Steps(sem("ln_dve"), [f"centred{k}" for k in range(KT)] + ["inv"] + [f"scaled{k}" for k in range(KT)])
            pool_n = Steps(sem("ln_pool"), ["eps"] + [f"z{k}" for k in range(KT)])
            pe_m = Steps(sem("ssm_pe"), [f"tile{b}" for b in range(4)])
            act_m = Steps(sem("ssm_act"), ["sig0", "sig1"])
            dve_m = Steps(sem("ssm_dve"), ["merged0", "merged1"])
            q0 = quads[0]
            quads[0] += KT // 2
            with nc.Block() as block:
                @block.sync
                def _(sp):
                    with sp.Fori(0, KT // 2) as i:
                        load_quad(sp, pe_m, i, [tile for p in range(2) for tile in (
                            (ring[:, 2 * p, :, :], columns(w_in, i * 2 + (p + GS))),
                            (ring[:, 2 * p + 1, 0:ST, :], columns(a["w_ssm_out_2"][0], i * 2 + p)))])

                @block.gpsimd
                def _(g):
                    pool_n.ready(g)
                    pool_n.mark(g.memset(eps[:, :], LN_EPS), "eps")
                    for k in range(KT):
                        act_n.wait(g, f"silu{k}")
                        pool_n.mark(g.tensor_tensor(yT[:, k, :], yT[:, k, :], silu_zc[:, k, :], ALU.mult), f"z{k}")

                @block.tensor
                def _(pe):
                    pe_n.ready(pe)
                    pe_m.ready(pe)

                    def gate_tile(i, p):
                        pe.wait_ge(w_loaded[2 * p], (i + (q0 + 1)) * 16)
                        act_m.wait(pe, f"sig{1 - p}", i, back=int(p == 0))
                        pe_m.mark(project(2, hT, w=ring[:, 2 * p]), f"tile{2 * p}")

                    def ssm_tile(i, p):
                        pe.wait_ge(w_loaded[2 * p + 1], (i + (q0 + 1)) * 16)
                        dve_m.wait(pe, f"merged{1 - p}", i, back=int(p == 0))
                        pe_m.mark(project(3, ssm_y, ST, w=ring[:, 2 * p + 1]), f"tile{2 * p + 1}")

                    for k in range(KT):
                        for h in range(2):
                            last = nc.tensor.matmul(bank[:, 2 + h, :], ones[:, :], yT[:, k, h * HALF:(h + 1) * HALF], start=(k == 0), stop=(k == KT - 1))
                    pe_n.mark(last, "sums")
                    gate_tile(0, 0)
                    ssm_tile(0, 0)
                    for k in range(KT):
                        act_n.wait(pe, f"sq{k}")
                        for h in range(2):
                            last = nc.tensor.matmul(bank[:, h, :], ones[:, :], sq[:, k % 2, h * HALF:(h + 1) * HALF], start=(k == 0), stop=(k == KT - 1))
                        pe_n.mark(last, f"sq{k}")
                    gate_tile(0, 1)
                    ssm_tile(0, 1)
                    with pe.Fori(1, KT // 2) as i:
                        for p in range(2):
                            gate_tile(i, p)
                            ssm_tile(i, p)

                @block.scalar
                def _(act):
                    act_n.ready(act)
                    act_m.ready(act)

                    def gate(i, p):
                        pe_m.wait(act, f"tile{2 * p}", i)
                        dve_m.wait(act, f"merged{p}", i, back=1)
                        act_m.mark(act.activation(sig[:, p, :], pair(2), ACT.Sigmoid), f"sig{p}")

                    for k in range(KT):
                        if k == 2:
                            gate(0, 0)
                        dve_n.wait(act, f"centred{k}")
                        if k >= 2:
                            pe_n.wait(act, f"sq{k - 2}")
                        act_n.mark(act.activation(sq[:, k % 2, :], yT[:, k, :], ACT.Square), f"sq{k}")
                    pool_n.wait(act, "eps")
                    pe_n.wait(act, f"sq{KT - 1}")
                    act_n.mark(act.activation(inv_std, pair(0), ACT.Sqrt, bias=eps[:, 0:1], scale=1.0 / D), "std")
                    gate(0, 1)
                    for k in range(KT):
                        dve_n.wait(act, f"scaled{k}")
                        act_n.mark(act.activation(yT[:, k, :], yT[:, k, :], ACT.Silu, scale=vec("ln_g", k), bias=vec("ln_b", k)), f"silu{k}")
                    with act.Fori(1, KT // 2) as i:
                        for p in range(2):
                            gate(i, p)

                @block.vector
                def _(dve):
                    dve_n.ready(dve)
                    dve_m.ready(dve)

                    def merge(i, p):
                        pe_m.wait(dve, f"tile{2 * p + 1}", i)
                        act_m.wait(dve, f"sig{p}", i)
                        dve_m.mark(dve.tensor_tensor(merged[:, i * 2 + p, :], pair(3), sig[:, p, :], ALU.mult), f"merged{p}")

                    pe_n.wait(dve, "sums")
                    for k in range(KT):
                        dve_n.mark(dve.scalar_tensor_tensor(out=yT[:, k, :], in0=pair(1), scalar=-1.0 / D, in1=yT[:, k, :],
                                                            op0=ALU.mult, op1=ALU.add), f"centred{k}")
                    merge(0, 0)
                    act_n.wait(dve, "std")
                    dve_n.mark(dve.reciprocal(inv_std, inv_std), "inv")
                    dve_n.wait(dve, "inv")
                    for k in range(KT):
                        dve_n.mark(dve.tensor_tensor(yT[:, k, :], yT[:, k, :], inv_std, ALU.mult), f"scaled{k}")
                    merge(0, 1)
                    dve_n.wait(dve, f"scaled{KT - 1}")
                    with dve.Fori(1, KT // 2) as i:
                        for p in range(2):
                            merge(i, p)

        post_w = silu_zc[:, :, :].rearrange("p k (c n) -> p k c n", c=2)
        post_w_loaded = [sem("post_w_loaded0"), sem("post_w_loaded1")]
        with ExitStack() as scope:
            sig, branch = ssm_y[:, 0:2, :], ssm_y[:, 2, :]
            pe_m = Steps(sem("merge_pe"), [f"tile{b}" for b in range(4)])
            act_m = Steps(sem("merge_act"), ["sig0", "sig1"])
            dve_m = Steps(sem("merge_dve"), ["gated0", "merged0", "gated1", "merged1"])
            q0 = quads[0]
            quads[0] += KT // 2
            with nc.Block() as block:
                @block.sync
                def _(sp):
                    with sp.Fori(0, KT // 2) as i:
                        load_quad(sp, pe_m, i, [tile for p in range(2) for tile in (
                            (ring[:, 2 * p, :, :], columns(w_in, i * 2 + (p + GC))),
                            (ring[:, 2 * p + 1, :, :], columns(a["w_conv_out_2"][0], i * 2 + p)))])
                    for c in range(2):
                        sp.dma_start(post_w[:, :, c, :], a["w_out_2"][0].rearrange("(k p) (c n) -> p k c n", p=P, c=2)[:, :, c, :]) \
                            .then_inc(post_w_loaded[c], 16)

                @block.tensor
                def _(pe):
                    pe_m.ready(pe)
                    with pe.Fori(0, KT // 2) as i:
                        for p in range(2):
                            pe.wait_ge(w_loaded[2 * p], (i + (q0 + 1)) * 16)
                            act_m.wait(pe, f"sig{p}", i, back=1)
                            pe_m.mark(project(2 * p, hT, w=ring[:, 2 * p]), f"tile{2 * p}")
                            pe.wait_ge(w_loaded[2 * p + 1], (i + (q0 + 1)) * 16)
                            dve_m.wait(pe, f"gated{p}", i, back=1)
                            pe_m.mark(project(2 * p + 1, yT, w=ring[:, 2 * p + 1]), f"tile{2 * p + 1}")

                @block.scalar
                def _(act):
                    act_m.ready(act)
                    with act.Fori(0, KT // 2) as i:
                        for p in range(2):
                            pe_m.wait(act, f"tile{2 * p}", i)
                            dve_m.wait(act, f"gated{p}", i, back=1)
                            act_m.mark(act.activation(sig[:, p, :], pair(2 * p), ACT.Sigmoid), f"sig{p}")

                @block.vector
                def _(dve):
                    dve_m.ready(dve)
                    with dve.Fori(0, KT // 2) as i:
                        for p in range(2):
                            m_n = merged[:, i * 2 + p, :]
                            pe_m.wait(dve, f"tile{2 * p + 1}", i)
                            act_m.wait(dve, f"sig{p}", i)
                            dve_m.wait(dve, f"merged{1 - p}", i, back=int(p == 0))
                            dve_m.mark(dve.tensor_tensor(branch, pair(2 * p + 1), sig[:, p, :], ALU.mult), f"gated{p}")
                            dve_m.wait(dve, f"gated{p}", i)
                            dve_m.mark(dve.tensor_tensor(m_n, m_n, branch, ALU.add), f"merged{p}")

        with ExitStack() as scope:
            gain = sb("post_gain", [P, D], scope)
            junk = sb("post_junk", [P, D], scope)
            stat = sb("post_stat", [P, 2, TT], scope)
            eps = sb("post_eps", [P, 1], scope)
            gain_loaded, out_stored = sem("post_gain_loaded"), sem("out_stored")
            pe_p = Steps(sem("post_pe"), [f"tok{t}" for t in range(TT)])
            act_p = Steps(sem("post_act"), [f"{s}{t}" for t in range(TT) for s in ("sq", "rms")])
            dve_p = Steps(sem("post_dve"), [f"{s}{t}" for t in range(TT) for s in ("inv", "scaled", "out")])
            pool_p = Steps(sem("post_pool"), ["eps"])
            with nc.Block() as block:
                @block.sync
                def _(sp):
                    sp.dma_start(gain[:, :], a["post_norm_gain_2"][0].partition_broadcast(P)).then_inc(gain_loaded, 16)
                    for t in range(TT):
                        dve_p.wait(sp, f"out{t}")
                        sp.dma_start(out[0, t * P:(t + 1) * P, :], hT[:, t, :]).then_inc(out_stored, 16)
                    sp.wait_ge(out_stored, 16 * TT)

                @block.gpsimd
                def _(g):
                    pool_p.ready(g)
                    pool_p.mark(g.memset(eps[:, :], EPS), "eps")

                @block.tensor
                def _(pe):
                    pe_p.ready(pe)
                    for c in range(2):
                        pe.wait_ge(post_w_loaded[c], 16)
                    for t in range(TT):
                        if t >= 4:
                            dve_p.wait(pe, f"scaled{t - 4}")
                        for c in range(2):
                            for k in range(KT):
                                last = nc.tensor.matmul(bank[:, 2 * (t % 4) + c, :], merged[:, k, t * P:(t + 1) * P], post_w[:, k, c, :],
                                                        start=(k == 0), stop=(k == KT - 1))
                        pe_p.mark(last, f"tok{t}")

                @block.scalar
                def _(act):
                    act_p.ready(act)
                    pool_p.wait(act, "eps")
                    for t in range(TT):
                        pe_p.wait(act, f"tok{t}")
                        act_p.mark(act.activation(junk[:, :], pair(t % 4), ACT.Square, accum_out=stat[:, 0, t:t + 1]), f"sq{t}")
                        act_p.wait(act, f"sq{t}")
                        act_p.mark(act.activation(stat[:, 1, t:t + 1], stat[:, 0, t:t + 1], ACT.Sqrt, bias=eps[:, 0:1], scale=1.0 / D), f"rms{t}")

                @block.vector
                def _(dve):
                    dve_p.ready(dve)
                    dve.wait_ge(gain_loaded, 16)
                    for t in range(TT):
                        act_p.wait(dve, f"rms{t}")
                        dve_p.mark(dve.reciprocal(stat[:, 1, t:t + 1], stat[:, 1, t:t + 1]), f"inv{t}")
                        dve_p.wait(dve, f"inv{t}")
                        dve_p.mark(dve.scalar_tensor_tensor(out=hT[:, t, :], in0=pair(t % 4), scalar=stat[:, 1, t:t + 1], in1=gain[:, :],
                                                            op0=ALU.mult, op1=ALU.mult), f"scaled{t}")
                        dve_p.wait(dve, f"scaled{t}")
                        dve_p.mark(dve.tensor_tensor(hT[:, t, :], hT[:, t, :], resid[:, t, :], ALU.add), f"out{t}")


_OUT_SHAPE = (1, S, D)


def kernel(**inputs):
    import concourse.bacc as bacc
    from concourse.bass_utils import run_bass_kernel_spmd

    nc = bacc.Bacc("TRN2", target_bir_lowering=False, num_devices=1)
    arrays, patterns = {}, {}
    for name, value in inputs.items():
        arrays[f"in_{name}"] = np.ascontiguousarray(value)
        patterns[name] = nc.dram_tensor(f"in_{name}", arrays[f"in_{name}"].shape, F32, kind="ExternalInput").ap()
    out = nc.dram_tensor("out", _OUT_SHAPE, F32, kind="ExternalOutput").ap()
    block_program(nc, patterns, out)
    return run_bass_kernel_spmd(nc, [arrays], core_ids=[0]).results[0]["out"]
```

```python
import math
from contextlib import ExitStack

import concourse.bass as bass
import numpy as np
from concourse import mybir
from concourse.alu_op_type import AluOpType as ALU

ACT = mybir.ActivationFunctionType
AX = mybir.AxisListType
F32 = mybir.dt.float32

P = 128
D = 1024
S = 1024
KT = D // P
TT = S // P
HALF = 512
HEADS = 8
CH = P
NCH = S // CH
TAPS4 = 4
TAPS31 = 31
EPS = 1e-6
LN_EPS = 1e-5
RG_C = 8.0
GDN_Z = 4 * D
GROUPS = 32
PAIRS = GROUPS // 2
NS = 64
GH = 16
BLK = P // GH
NBLK = S // BLK
MASKED = -1.0e30


class Steps:

    def __init__(self, sem, names):
        self.sem, self.names = sem, names
        self.at = {n: k + 1 for k, n in enumerate(names)}
        assert len(self.at) == len(names)
        self.next = 0

    def ready(self, eng):
        eng.sem_inc(self.sem, len(self.names))

    def mark(self, ins, name):
        assert self.names[self.next] == name, (name, self.names[self.next])
        self.next = (self.next + 1) % len(self.names)
        ins.then_inc(self.sem, 1)

    def wait(self, eng, name, body=0, back=0):
        eng.wait_ge(self.sem, (body + 1 - back) * len(self.names) + self.at[name])


def block_program(nc, a, out):
    ctx = ExitStack()

    with ctx:
        def sem(name):
            return ctx.enter_context(nc.semaphore(name))

        def sb(name, shape, scope=ctx):
            return scope.enter_context(nc.sbuf_tensor(name, shape, F32))

        bank = ctx.enter_context(nc.psum_tensor("bank", [P, 8, HALF], F32))
        ident = sb("ident", [P, P])
        ones = sb("ones", [P, P])
        resid = sb("resid", [P, TT, D])
        hT = sb("hT", [P, KT, S])
        yT = sb("yT", [P, KT, S])
        ring = sb("ring", [P, 4, KT, P])
        vecs = sb("vecs", [P, 5, P])
        cond = sb("cond", [P, 2, 2 * KT])
        inv_rms = sb("inv_rms", [P, TT])
        norm_eps = sb("norm_eps", [P, 1])
        layers = ctx.enter_context(ExitStack())
        gate_b = sb("gate_b", [P, 2, D], layers)
        w_loaded = [sem(f"w_loaded{b}") for b in range(4)]
        quads = [0]

        def pair(n):
            return bank[:, 2 * n:2 * n + 2, :].rearrange("p a c -> p (a c)")

        VEC = {}

        def vec(name, k, n=1):
            tile, at = VEC[name]
            return vecs[:, tile, bass.ds(at + k, n)]

        def load_quad(sp, pe, body, tiles, names=("tile0", "tile1", "tile2", "tile3")):
            for b, (dst, src) in enumerate(tiles):
                pe.wait(sp, names[b], body, back=1)
                sp.dma_start(dst, src).then_inc(w_loaded[b], 16)

        def load_ahead(sp, tiles, pe=None, body=0, names=None):
            for b, (dst, src) in enumerate(tiles):
                if pe:
                    pe.wait(sp, names[b], body)
                sp.dma_start(dst, src).then_inc(w_loaded[b], 16)

        def columns(w, n, kt=KT):
            return w.rearrange("(k p) c -> p k c", p=P)[:, :, bass.ts(n, P)]

        def project(b, src, kt=KT, w=None):
            to, w = (b % 2, ring[:, b]) if w is None else (b, w)
            for h in range(2):
                for k in range(kt):
                    last = nc.tensor.matmul(bank[:, 2 * to + h, :], w[:, k, :],
                                            src[:, k, h * HALF:(h + 1) * HALF],
                                            start=(k == 0), stop=(k == kt - 1))
            return last

        def log1p_steps(dve, link, p, e, z, z2):
            link(dve.tensor_scalar(z, e, 2.0, None, ALU.add))
            link(dve.reciprocal(z, z))
            link(dve.tensor_tensor(z, z, e, ALU.mult))
            link(dve.tensor_tensor(z2, z, z, ALU.mult))
            link(dve.tensor_scalar(p, z2, 1.0 / 19.0, None, ALU.mult))
            for n in range(17, 1, -2):
                link(dve.scalar_tensor_tensor(out=p, in0=p, scalar=1.0 / n, in1=z2, op0=ALU.add, op1=ALU.mult))
            link(dve.scalar_tensor_tensor(out=p, in0=p, scalar=1.0, in1=z, op0=ALU.add, op1=ALU.mult))
            link(dve.tensor_scalar(p, p, 2.0, None, ALU.mult))

        SQUARES = [f"sq{t}" for t in range(TT)] + ["rms"]

        def token_rms(act, steps, junk, rms, ready=None):
            for t in range(TT):
                if ready:
                    ready(t)
                if t >= 2:
                    steps.wait(act, f"sq{t - 2}")
                steps.mark(act.activation(junk[:, t % 2, :], resid[:, t, :], ACT.Square, accum_out=rms[:, t:t + 1]), f"sq{t}")
            steps.wait(act, f"sq{TT - 1}")
            steps.mark(act.activation(rms[:, :], rms[:, :], ACT.Sqrt, bias=norm_eps[:, 0:1], scale=1.0 / D), "rms")

        def linker(eng, s):
            count = [0]

            def link(ins):
                count[0] += 1
                ins.then_inc(s, 1)
                eng.wait_ge(s, count[0])
            return link

        def flat(v):
            return v.rearrange("(k p) -> k p", p=P) if len(v.shape) == 1 else v.rearrange("n (k p) -> (n k) p", p=P)

        rows = [
            [(["norm_g0", "norm_g1"], a["norm_g"]), (["conv_b"], a["lru_conv_b"][0]), (["gate_b0", "gate_b1"], a["lru_gate_b"][0]),
             (["lam"], a["lru_lambda"][0]), (["ada_b0"], a["ada_b"][0, 0:2 * D]), (["ada_b1"], a["ada_b"][1, 0:2 * D])],
            [(["c"], a["c"][0]), (["conv_b2"], a["conv_b_2"][0]), (["ln_g"], a["conv_ln_gain_2"][0]), (["ln_b"], a["conv_ln_bias_2"][0]),
             (["glu_b"], a["b_ssm_glu_2"][0]), (["pre_g"], a["pre_norm_gain_2"][0]), (["onorm"], a["gdn_onorm_g"][0]),
             ([f"lru_conv{j}" for j in range(TAPS4)], a["lru_conv_w"][0])],
            [([f"gdn_conv{j}" for j in range(TAPS4)], a["gdn_conv_w"][0])],
            [([f"conv31_{j}" for j in range(16)], a["conv_w_2"][0, 0:16])],
            [([f"conv31_{j}" for j in range(16, TAPS31)], a["conv_w_2"][0, 16:TAPS31])],
        ]
        with ExitStack() as scope:
            row_tiles = sb("row_tiles", [P, 5, P], scope)
            c_act = sb("c_act", [P, KT], scope)
            c_wide = sb("c_wide", [P, KT, P], scope)
            junk = sb("setup_junk", [P, 2, D], scope)
            diagonal = sb("cond_diagonal", [P, 2, 4, P], scope)
            weighted = sb("cond_weighted", [P, 2, HALF], scope)
            ada = sb("ada", [P, 3, KT, HALF], scope)
            gate_bias = sb("gate_bias", [P, 2, D], scope)
            rows_loaded, biases_loaded = sem("rows_loaded"), sem("biases_loaded")
            ada_loaded = [sem(f"ada_loaded{b}") for b in range(3)]
            x_loaded = sem("x_loaded")
            pool = Steps(sem("setup_pool"), ["ident0", "ident", "ones", "eps", "row0"])
            pe_s = Steps(sem("setup_pe"), ["rows_flipped"])
            act_s = Steps(sem("setup_act"), ["vecs", "c_act"] + SQUARES)
            dve_s = Steps(sem("setup_dve"), ["c_wide", "cond0"])
            pe_c = Steps(sem("cond_pe"), [f"chunk{q}" for q in range(6)])
            KH = KT // 2
            dve_w = Steps(sem("cond_weighted_dve"), [f"w{q}_{k}" for q in range(6) for k in range(KH)])
            dve_c = Steps(sem("cond_dve"), [f"{n}{q}" for q in range(4) for n in ("diagonal", "cond")] + ["gate4", "gate5"])

            loads = []
            for tile, vectors in enumerate(rows):
                at = 0
                for names, v in vectors:
                    v = flat(v)
                    for n, name in enumerate(names):
                        VEC[name] = (tile, at + n * (v.shape[0] // len(names)))
                    loads.append((at, tile, v))
                    at += v.shape[0]
                assert at <= P
            n_rows = len(loads)

            with nc.Block() as block:
                @block.sync
                def _(sp):
                    def chunk(layer, q):
                        pe_c.wait(sp, f"chunk{(q + 3) % 6}", layer, back=int(q < 3))
                        src = a["ada_w"][layer].rearrange("(k p) c -> p k c", p=P)
                        sp.dma_start(ada[:, q % 3, :, :], src[:, :, q * HALF:(q + 1) * HALF]).then_inc(ada_loaded[q % 3], 16)

                    chunk(0, 0)
                    sp.wait_ge(rows_loaded, 16 * n_rows)
                    for q in range(1, 6):
                        chunk(0, q)
                        if q == 1:
                            sp.dma_start(resid[:, :, :], a["x"][0].rearrange("(t p) c -> p t c", p=P)).then_inc(x_loaded, 16)
                    for q in range(6):
                        chunk(1, q)

                @block.gpsimd
                def _(g):
                    pool.ready(g)
                    pool.mark(g.memset(ident[:, :], 0.0), "ident0")
                    pool.wait(g, "ident0")
                    pool.mark(g.affine_select(out=ident[:, :], in_=ident[:, :], compare_op=ALU.not_equal, fill=1.0,
                                              base=0, pattern=[[-1, P]], channel_multiplier=1), "ident")
                    pool.mark(g.memset(ones[:, :], 1.0), "ones")
                    pool.mark(g.memset(norm_eps[:, :], EPS), "eps")
                    pool.mark(g.memset(row_tiles[:, :, :], 0.0), "row0")

                @block.scalar
                def _(act):
                    act_s.ready(act)
                    pool.wait(act, "row0")
                    for at, tile, v in loads:
                        act.dma_start(row_tiles[at:at + v.shape[0], tile, :], v).then_inc(rows_loaded, 16)
                    for layer in range(2):
                        act.dma_start(gate_bias[:, layer, :],
                                      a["ada_b"][layer, 2 * D:3 * D].partition_broadcast(P)).then_inc(biases_loaded, 16)
                    pe_s.wait(act, "rows_flipped")
                    act.activation(vecs[:, 4, :], bank[:, 1, 0:P], ACT.Copy)
                    act_s.mark(act.activation(vecs[:, 0:4, :].rearrange("p t c -> p (t c)"), bank[:, 0, :], ACT.Copy),
                               "vecs")
                    act_s.wait(act, "vecs")
                    act_s.mark(act.activation(c_act[:, :], vec("c", 0, KT), ACT.Silu), "c_act")
                    act.wait_ge(x_loaded, 16)
                    token_rms(act, act_s, junk, inv_rms)

                @block.tensor
                def _(pe):
                    pe_s.ready(pe)
                    pe_c.ready(pe)
                    pool.wait(pe, "row0")
                    pe.wait_ge(rows_loaded, 16 * n_rows)
                    for tile in range(5):
                        last = nc.tensor.transpose(bank[:, tile // 4, (tile % 4) * P:(tile % 4 + 1) * P],
                                                   row_tiles[:, tile, :], ident[:, :])
                    pe_s.mark(last, "rows_flipped")
                    dve_s.wait(pe, "c_wide")
                    with pe.Fori(0, 2) as layer:
                        for q in range(6):
                            pe.wait_ge(ada_loaded[q % 3], (layer * 2 + q // 3 + 1) * 16)
                            dve_c.wait(pe, f"cond{q}" if q < 4 else f"gate{q}", layer, back=1)
                            for k in range(KH, KT):
                                nc.tensor.matmul(bank[:, 2 + q, :], c_wide[:, k, :], ada[:, q % 3, k, :], start=(k == KH), stop=False)
                            dve_w.wait(pe, f"w{q}_{KH - 1}", layer)
                            last = nc.tensor.matmul(bank[:, 2 + q, :], ones[:, :], weighted[:, q % 2, :], start=False, stop=True)
                            pe_c.mark(last, f"chunk{q}")

                @block.vector
                def _(dve):
                    dve_s.ready(dve)
                    dve_c.ready(dve)
                    act_s.wait(dve, "c_act")
                    dve_s.mark(dve.tensor_copy(c_wide[:, :, :], c_act[:, :].unsqueeze(2).broadcast_to([P, KT, P])), "c_wide")
                    dve.wait_ge(biases_loaded, 32)
                    dve_w.ready(dve)

                    def weigh(layer, q):
                        dve.wait_ge(ada_loaded[q % 3], (layer * 2 + q // 3 + 1) * 16)
                        w = weighted[:, q % 2, :]
                        for k in range(KH):
                            if k == 0:
                                ins = dve.tensor_scalar(w, ada[:, q % 3, k, :], c_act[:, k:k + 1], None, ALU.mult)
                            else:
                                dve_w.wait(dve, f"w{q}_{k - 1}", layer)
                                ins = dve.scalar_tensor_tensor(out=w, in0=ada[:, q % 3, k, :], scalar=c_act[:, k:k + 1], in1=w,
                                                               op0=ALU.mult, op1=ALU.add)
                            dve_w.mark(ins, f"w{q}_{k}")

                    def finish(layer, q):
                        pe_c.wait(dve, f"chunk{q}", layer)
                        if q < 4:
                            dve_c.mark(dve.tensor_tensor(diagonal[:, q % 2, :, :], bank[:, 2 + q, :].rearrange("p (m c) -> p m c", c=P),
                                                         ident[:, :].unsqueeze(1).broadcast_to([P, 4, P]), ALU.mult), f"diagonal{q}")
                            dve_c.wait(dve, f"diagonal{q}", layer)
                            dve_c.mark(dve.tensor_reduce(out=cond[:, layer, 4 * q:4 * q + 4], in_=diagonal[:, q % 2, :, :], op=ALU.add, axis=AX.X),
                                       f"cond{q}")
                        else:
                            half = slice((q - 4) * HALF, (q - 3) * HALF)
                            dve_c.mark(dve.tensor_tensor(gate_b[:, layer, half], bank[:, 2 + q, :], gate_bias[:, layer, half], ALU.add), f"gate{q}")

                    chunks = [(layer, q) for layer in range(2) for q in range(6)]
                    for n, at in enumerate(chunks):
                        weigh(*at)
                        if n:
                            finish(*chunks[n - 1])
                    finish(*chunks[-1])
                    act_s.wait(dve, "rms")
                    dve.reciprocal(inv_rms[:, :], inv_rms[:, :])
                    dve_c.wait(dve, "cond3", 1)
                    for layer in range(2):
                        ins = dve.tensor_tensor(cond[:, layer, :], cond[:, layer, :], vec(f"ada_b{layer}", 0, 2 * KT), ALU.add)
                    dve_s.mark(ins, "cond0")
                    dve_s.wait(dve, "cond0")
                    for layer in range(2):
                        dve.scalar_tensor_tensor(out=cond[:, layer, KT:2 * KT], in0=cond[:, layer, KT:2 * KT], scalar=1.0,
                                                 in1=vec(f"norm_g{layer}", 0, KT), op0=ALU.add, op1=ALU.mult)

        def norm_transpose(name, scale, shift, tiles):
            with ExitStack() as scope:
                normed = sb(f"{name}_normed", [P, 4, D], scope)
                act_n = Steps(sem(f"{name}_act"), [f"low{p}" for p in range(4)])
                dve_n = Steps(sem(f"{name}_dve"), ["normed0"] + [n for p in range(4) for n in ([f"normed{p + 1}"] if p < 3 else []) + [f"high{p}"]])
                pe_n = Steps(sem(f"{name}_pe"), [f"flip{p}" for p in range(4)])
                with nc.Block() as block:
                    @block.sync
                    def _(sp):
                        load_ahead(sp, tiles)

                    @block.scalar
                    def _(act):
                        act_n.ready(act)
                        for i in range(TT // 4):
                            for p in range(4):
                                pe_n.wait(act, f"flip{p}", i)
                                for k in range(KT // 2):
                                    ins = act.activation(hT[:, k, bass.ts(i * 4 + p, P)], bank[:, 2 * p, k * P:(k + 1) * P],
                                                         ACT.Identity, scale=scale(k), bias=shift(k))
                                act_n.mark(ins, f"low{p}")

                    @block.vector
                    def _(dve):
                        dve_n.ready(dve)

                        def normalise(i, p):
                            t = i * 4 + p
                            pe_n.wait(dve, f"flip{p}", i, back=1)
                            dve_n.mark(dve.tensor_scalar(normed[:, p, :], resid[:, t, :], inv_rms[:, t:t + 1], None, ALU.mult), f"normed{p}")

                        for i in range(TT // 4):
                            normalise(i, 0)
                            for p in range(4):
                                if p < 3:
                                    normalise(i, p + 1)
                                pe_n.wait(dve, f"flip{p}", i)
                                for k in range(KT // 2):
                                    ins = dve.tensor_scalar(hT[:, KT // 2 + k, bass.ts(i * 4 + p, P)],
                                                            bank[:, 2 * p + 1, k * P:(k + 1) * P],
                                                            scale(KT // 2 + k), shift(KT // 2 + k), ALU.mult, ALU.add)
                                dve_n.mark(ins, f"high{p}")

                    @block.tensor
                    def _(pe):
                        pe_n.ready(pe)
                        for i in range(TT // 4):
                            for p in range(4):
                                dve_n.wait(pe, f"normed{p}", i)
                                act_n.wait(pe, f"low{p}", i, back=1)
                                dve_n.wait(pe, f"high{p}", i, back=1)
                                for k in range(KT):
                                    last = nc.tensor.transpose(bank[:, 2 * p + k // 4, (k % 4) * P:(k % 4 + 1) * P],
                                                               normed[:, p, k * P:(k + 1) * P], ident[:, :])
                                pe_n.mark(last, f"flip{p}")

        ring_half = ring[:, :, :, :].rearrange("p b k c -> p (b k c)").rearrange("p (k c) -> p k c", k=KT)
        half_loaded = [sem("out0_half_loaded"), sem("out1_half_loaded")]

        def out_half(w, c):
            return w.rearrange("(k p) c -> p k c", p=P)[:, :, c * HALF:(c + 1) * HALF]

        def load_first_half(sp, w, layer):
            sp.dma_start(ring_half, out_half(w, 0)).then_inc(half_loaded[layer], 16)

        def project_out(name, w, layer):
            with ExitStack() as scope:
                second_half = sb(f"{name}_w", [P, KT, HALF], scope)
                gated = sb(f"{name}_gated", [P, 2, HALF], scope)
                junk = sb(f"{name}_junk", [P, 2, D], scope)
                loaded = [half_loaded[layer], sem(f"{name}_second_loaded")]
                pe_o = Steps(sem(f"{name}_pe"), [f"tok{t}" for t in range(TT)])
                dve_o = Steps(sem(f"{name}_dve"), [f"{s}{t}" for t in range(TT) for s in ("gated", "added")])
                act_o = Steps(sem(f"{name}_act"), SQUARES)
                with nc.Block() as block:
                    @block.sync
                    def _(sp):
                        sp.dma_start(second_half[:, :, :], out_half(w, 1)).then_inc(loaded[1], 16)

                    @block.tensor
                    def _(pe):
                        pe_o.ready(pe)
                        for c in range(2):
                            pe.wait_ge(loaded[c], 16)
                            for t in range(TT):
                                dve_o.wait(pe, f"gated{t}", c, back=1)
                                for k in range(KT):
                                    last = nc.tensor.matmul(bank[:, t, :], yT[:, k, t * P:(t + 1) * P], (ring_half, second_half)[c][:, k, :],
                                                            start=(k == 0), stop=(k == KT - 1))
                                pe_o.mark(last, f"tok{t}")

                    @block.scalar
                    def _(act):
                        act_o.ready(act)
                        token_rms(act, act_o, junk, inv_rms, lambda t: dve_o.wait(act, f"added{t}", 1))

                    @block.vector
                    def _(dve):
                        dve_o.ready(dve)
                        for c in range(2):
                            half = slice(c * HALF, (c + 1) * HALF)
                            for t in range(TT):
                                pe_o.wait(dve, f"tok{t}", c)
                                x_t = resid[:, t, half]
                                dve_o.mark(dve.tensor_tensor(gated[:, t % 2, :], bank[:, t, :], gate_b[:, layer, half], ALU.mult), f"gated{t}")
                                dve_o.wait(dve, f"gated{t}", c)
                                dve_o.mark(dve.tensor_tensor(x_t, x_t, gated[:, t % 2, :], ALU.add), f"added{t}")
                        act_o.wait(dve, "rms")
                        dve.reciprocal(inv_rms[:, :], inv_rms[:, :])

        def lru_tiles(i):
            return [(ring[:, 2 * p + z, :, :], columns(a["lru_in_w"][0], i * 2 + (z * KT + p))) for p in range(2) for z in range(2)]

        norm_transpose("norm0", lambda k: cond[:, 0, KT + k:KT + k + 1], lambda k: cond[:, 0, k:k + 1], lru_tiles(0))

        with ExitStack() as scope:
            PAD = TAPS4 - 1
            rate = sb("rate", [P, KT], scope)
            nrate = sb("nrate", [P, KT], scope)
            small = sb("lru_small", [P, 5, KT], scope)
            padded = sb("padded", [P, 2, PAD + S], scope)
            conv = sb("conv", [P, 2, S], scope)
            gw = sb("gw", [P, 2, 2, P], scope)
            gate_r = sb("gate_r", [P, S], scope)
            gate_i = sb("gate_i", [P, S], scope)
            sig_z = sb("sig_z", [P, 2, S], scope)
            tau = sb("tau", [P, S], scope)
            decay = sb("decay", [P, S], scope)
            mult = sb("mult", [P, S], scope)
            inp = sb("inp", [P, S], scope)
            state = sb("state", [P, S], scope)
            gw_loaded = [sem("gw_loaded0"), sem("gw_loaded1")]
            pe_l = Steps(sem("lru_pe"), ["tile0", "tile1", "gates0", "tile2", "tile3", "gates1"])
            act_names = ["x_in", "sig_z", "gate_r", "gate_i", "tau", "decay", "decay2", "mult"]
            act_l = Steps(sem("lru_act"), [s + str(p) for p in range(2) for s in act_names])
            dve_names = ["c0_", "c1_", "c2_", "conv", "sz", "ix", "m2", "b", "scan", "y"]
            dve_l = Steps(sem("lru_dve"), [s + str(p) for p in range(2) for s in dve_names])
            chain, e_ready = sem("lru_chain"), sem("lru_e_ready")
            pad_zero = sem("lru_pad_zero")
            q0 = quads[0]
            quads[0] += KT // 2

            with nc.Block() as block:
                @block.sync
                def _(sp):
                    with sp.Fori(1, KT // 2) as i:
                        load_quad(sp, pe_l, i, lru_tiles(i))
                    pe_l.wait(sp, "tile3", KT // 2 - 1)
                    load_first_half(sp, a["lru_out_w"][0], 0)

                @block.gpsimd
                def _(g):
                    g.memset(padded[:, :, 0:PAD], 0.0).then_inc(pad_zero, 1)
                    with g.Fori(0, KT // 2) as i:
                        for p in range(2):
                            pe_l.wait(g, f"gates{p}", i, back=1)
                            g.dma_start(gw[:, p, :, :], a["lru_gate_w"][0].rearrange("g n i j -> n i g j")[i * 2 + p]) \
                                .then_inc(gw_loaded[p], 16)

                @block.tensor
                def _(pe):
                    pe_l.ready(pe)

                    def gates(i, p):
                        pe.wait_ge(gw_loaded[p], (i + 1) * 16)
                        dve_l.wait(pe, f"conv{p}", i)
                        act_l.wait(pe, f"gate_i{1 - p}", i, back=int(p == 0))
                        for g in range(2):
                            for h in range(2):
                                last = nc.tensor.matmul(bank[:, 4 + 2 * g + h, :], gw[:, p, g, :],
                                                        conv[:, p, h * HALF:(h + 1) * HALF], start=True, stop=True)
                        pe_l.mark(last, f"gates{p}")

                    with pe.Fori(0, KT // 2) as i:
                        for b in range(4):
                            pe.wait_ge(w_loaded[b], (i + (q0 + 1)) * 16)
                            if b % 2 == 0:
                                act_l.wait(pe, f"x_in{1 - b // 2}", i, back=int(b == 0))
                            else:
                                dve_l.wait(pe, f"sz{1 - b // 2}", i, back=int(b == 1))
                            pe_l.mark(project(b, hT), f"tile{b}")
                            if b % 2 == 1:
                                gates(i, b // 2)

                @block.scalar
                def _(act):
                    act_l.ready(act)
                    act.activation(small[:, 0, :], vec("lam", 0, KT), ACT.Abs).then_inc(e_ready, 1)
                    act.wait_ge(e_ready, 1)
                    act.activation(small[:, 1, :], small[:, 0, :], ACT.Exp, scale=-1.0).then_inc(e_ready, 1)
                    act.wait_ge(pad_zero, 1)
                    act.wait_ge(chain, 17)
                    with act.Fori(0, KT // 2) as i:
                        for p in range(2):
                            n = i * 2 + p
                            pe_l.wait(act, f"tile{2 * p}", i)
                            dve_l.wait(act, f"conv{p}", i, back=1)
                            act_l.mark(act.activation(padded[:, p, PAD:], pair(0), ACT.Copy), f"x_in{p}")
                            pe_l.wait(act, f"tile{2 * p + 1}", i)
                            act_l.mark(act.activation(sig_z[:, p, :], pair(1), ACT.Sigmoid), f"sig_z{p}")
                            pe_l.wait(act, f"gates{p}", i)
                            act_l.mark(act.activation(gate_r[:, :], pair(2), ACT.Sigmoid, bias=vec("gate_b0", n)), f"gate_r{p}")
                            dve_l.wait(act, f"ix{1 - p}", i, back=int(p == 0))
                            act_l.mark(act.activation(gate_i[:, :], pair(3), ACT.Sigmoid, bias=vec("gate_b1", n)), f"gate_i{p}")
                            act_l.wait(act, f"gate_r{p}", i)
                            dve_l.wait(act, f"m2{1 - p}", i, back=int(p == 0))
                            act_l.mark(act.activation(tau[:, :], gate_r[:, :], ACT.Tanh, scale=nrate[:, bass.ds(n, 1)]), f"tau{p}")
                            dve_l.wait(act, f"scan{1 - p}", i, back=int(p == 0))
                            act_l.mark(act.activation(decay[:, :], gate_r[:, :], ACT.Exp, scale=rate[:, bass.ds(n, 1)]), f"decay{p}")
                            act_l.wait(act, f"decay{p}", i)
                            act_l.mark(act.activation(mult[:, :], decay[:, :], ACT.Square), f"decay2{p}")
                            dve_l.wait(act, f"m2{p}", i)
                            act_l.mark(act.activation(mult[:, :], mult[:, :], ACT.Sqrt), f"mult{p}")

                @block.vector
                def _(dve):
                    dve_l.ready(dve)
                    link = linker(dve, chain)
                    dve.wait_ge(e_ready, 2)
                    log1p_steps(dve, link, small[:, 2, :], small[:, 1, :], small[:, 3, :], small[:, 4, :])
                    link(dve.tensor_scalar(small[:, 0, :], vec("lam", 0, KT), -1.0, 0.0, ALU.mult, ALU.max))
                    link(dve.tensor_tensor(small[:, 2, :], small[:, 2, :], small[:, 0, :], ALU.add))
                    dve.tensor_scalar(rate[:, :], small[:, 2, :], -RG_C, None, ALU.mult)
                    link(dve.tensor_scalar(nrate[:, :], small[:, 2, :], RG_C, None, ALU.mult))
                    with dve.Fori(0, KT // 2) as i:
                        for p in range(2):
                            n = i * 2 + p
                            acc = conv[:, p, :]
                            act_l.wait(dve, f"x_in{p}", i)
                            pe_l.wait(dve, f"gates{p}", i, back=1)
                            dve_l.mark(dve.tensor_scalar(acc, padded[:, p, 0:S], vec("lru_conv0", n), vec("conv_b", n),
                                                         ALU.mult, ALU.add), f"c0_{p}")
                            for j in range(1, TAPS4):
                                dve_l.wait(dve, f"c{j - 1}_{p}", i)
                                dve_l.mark(dve.scalar_tensor_tensor(out=acc, in0=padded[:, p, j:j + S], scalar=vec(f"lru_conv{j}", n),
                                                                    in1=acc, op0=ALU.mult, op1=ALU.add),
                                           f"c{j}_{p}" if j < TAPS4 - 1 else f"conv{p}")
                            act_l.wait(dve, f"sig_z{p}", i)
                            dve_l.mark(dve.tensor_tensor(sig_z[:, p, :], pair(1), sig_z[:, p, :], ALU.mult), f"sz{p}")
                            act_l.wait(dve, f"gate_i{p}", i)
                            dve_l.mark(dve.tensor_tensor(inp[:, :], gate_i[:, :], acc, ALU.mult), f"ix{p}")
                            act_l.wait(dve, f"decay2{p}", i)
                            dve_l.mark(dve.scalar_tensor_tensor(out=mult[:, :], in0=mult[:, :], scalar=1.0, in1=tau[:, :],
                                                                op0=ALU.add, op1=ALU.mult), f"m2{p}")
                            act_l.wait(dve, f"mult{p}", i)
                            dve_l.mark(dve.tensor_tensor(inp[:, :], inp[:, :], mult[:, :], ALU.mult), f"b{p}")
                            dve_l.wait(dve, f"b{p}", i)
                            dve_l.mark(dve.tensor_tensor_scan(state[:, :], decay[:, :], inp[:, :], 0.0, ALU.mult, ALU.add), f"scan{p}")
                            dve_l.wait(dve, f"scan{p}", i)
                            dve_l.mark(dve.tensor_tensor(yT[:, n, :], state[:, :], sig_z[:, p, :], ALU.mult), f"y{p}")
        project_out("out0", a["lru_out_w"][0], 0)
        def gdn_tiles(h):
            w = a["gdn_in_w"][0].rearrange("(k p) c -> p k c", p=P)
            return [(ring[:, b, :, :], w[:, :, bass.ts(h + b * HEADS, P)]) for b in range(4)]

        norm_transpose("norm1", lambda k: cond[:, 1, KT + k:KT + k + 1], lambda k: cond[:, 1, k:k + 1], gdn_tiles(0))

        with ExitStack() as scope:
            levels = [1 << s for s in range(7)]
            cols = {n: sb(f"col_{n}", [P, HEADS, NCH], scope)
                    for n in ("g", "beta", "exp_g", "exp_rest", "exp_last", "neg_beta_exp_g")}
            level_mask = sb("level_mask", [P, len(levels), P], scope)
            causal = sb("causal", [P, P], scope)

            w_ab = sb("w_ab", [P, KT, 2 * HEADS], scope)
            tri = sb("tri", [P, P], scope)
            last_row = sb("last_row", [P, P], scope)
            dt_bias = sb("dt_bias", [P, HEADS], scope)
            neg_a = sb("neg_a", [P, HEADS], scope)
            a_in = sb("a_in", [P, HEADS, NCH], scope)
            step = sb("step", [P, HEADS, NCH], scope)
            tmp = [sb(f"ab_tmp{n}", [P, HEADS, NCH], scope) for n in range(5)]
            ab_loaded, row_loaded = sem("ab_loaded"), sem("ab_row_loaded")
            pe_a = Steps(sem("ab_pe"), ["rows", "ab", "cum", "last"])
            act_a = Steps(sem("ab_act"), ["neg_a", "rows", "beta", "abs", "exp", "exp_g", "exp_last", "exp_rest"])
            dve_a = Steps(sem("ab_dve"), ["a_in", "g_step", "g", "rest", "neg"])
            pool_a = Steps(sem("ab_pool"), ["fill", "masks"])
            chain = sem("ab_chain")
            pool_chain = sem("ab_pool_chain")

            PAD = TAPS4 - 1
            padded = sb("qkv_padded", [P, 3, PAD + S], scope)
            tok_shape = [P, NCH, P]
            cq, ck, cv = (sb(n, [P, S], scope) for n in ("cq", "ck", "cv"))
            silu_z = sb("silu_z", [P, S], scope)
            k_tok, k_rest, v_tok, buf_a, buf_b, buf_c = (sb(n, tok_shape, scope) for n in ("k_tok", "k_rest", "v_tok", "buf_a", "buf_b", "buf_c"))
            kT, kbT, part0 = (sb(n, tok_shape, scope) for n in ("kT", "kbT", "part0"))
            decayT, attnT = (sb(n, tok_shape, scope) for n in ("decayT", "attnT"))
            kb_tok = ck[:, :].rearrange("p (c d) -> p c d", c=NCH)
            qT = cq[:, :].rearrange("p (c d) -> p c d", c=NCH)
            AT, inv, invT = buf_a, buf_b, buf_c
            part = [part0, k_tok]
            prod = kbT
            o_tok, o_normed = part0[:, :, :], AT
            memory = sb("memory", [P, P], scope)
            delta = sb("delta", [P, 2, P], scope)
            g_col = sb("g_col", [P, NCH], scope)
            stat = sb("gdn_stat", [P, 4, NCH], scope)
            eps2 = sb("gdn_eps", [P, 2], scope)
            ab_rows = silu_z[0:2 * HEADS, :]
            pj_pe = Steps(sem("gdn_proj_pe"), ["q", "k", "v", "z"])
            pj_act = Steps(sem("gdn_proj_act"), ["q_in", "k_in", "v_in", "z"])
            def halves(*names):
                return [n + x for n in names for x in "ab"]

            hd_pe = Steps(sem("gdn_pe"), ["g_row", "k_flip", "q_ss", "kT", "kbT", "qk", "kk"] + halves("Y1")
                          + [n for s in levels[1:] for n in (halves(f"Y{s}", f"TY{s}", f"YT{s}") if s < 64 else ["v_flip"] + halves(f"Y{s}", f"YT{s}"))]
                          + [f"{n}{c}" for c in range(NCH) for n in ("read", "new", "mem", "o")] + ["o_flip"])
            hd_act = Steps(sem("gdn_act"), ["k_sq", "k_rms", "q_silu", "q_sq", "q_rms", "kT", "kbT", "decay"]
                           + [n for s in levels[1:] for n in halves(f"prod{s}") + (["v_silu"] if s == 32 else [])]
                           + [n for c in range(NCH) for n in [f"new{c}", f"o{c}"] + ([f"o_sq{c - 1}"] if c else [])] + [f"o_sq{NCH - 1}", "o_rms"])
            dve_k, act_k = Steps(sem("gdn_keys_dve"), [f"kc{j}" for j in range(TAPS4)]), Steps(sem("gdn_keys_act"), ["k_silu"])
            hd_dve = Steps(sem("gdn_dve"), ["rel"] + [f"qc{j}" for j in range(TAPS4)]
                           + ["k_ss", "k_inv", "k_tok", "q_inv", "q_dec", "attn", "AT"] + halves("inv1", "invT1") + ["vc0"]
                           + [n for k, s in enumerate(levels[1:]) for n in (halves(f"inv{s}", f"invT{s}") if s < 64 else ["v_tok"] + halves(f"invT{s}"))
                              + ([f"vc{k + 1}"] if k + 1 < TAPS4 else [])]
                           + ["mem_zero"] + [f"{n}{c}" for c in range(NCH) for n in ("delta", "mem", "o")]
                           + ["g_col", "o_inv", "o_tok", "y"])
            hd_pool = Steps(sem("gdn_pool"), ["rel", "kb_tok", "k_rest"] + [f"part{s}" for s in levels])
            gdn_zero, g_first = sem("gdn_zero"), sem("gdn_g_first")
            q0 = quads[0]
            quads[0] += HEADS
            R4, R5 = pair(2).rearrange("p (c d) -> p c d", c=NCH), pair(3).rearrange("p (c d) -> p c d", c=NCH)

            def per_tok(name, h):
                return cols[name][:, h, :].unsqueeze(2).broadcast_to(tok_shape)

            def along(m):
                return m.unsqueeze(1).broadcast_to(tok_shape)

            def for_heads(eng, body):
                with eng.Fori(0, HEADS - 1) as h:
                    body(h, h + 1)
                body(HEADS - 1, None)

            with nc.Block() as block:
                @block.sync
                def _(sp):
                    sp.dma_start(w_ab[:, :, :], a["gdn_in_w"][0].rearrange("(k p) c -> p k c", p=P)[:, :, GDN_Z:]) \
                        .then_inc(ab_loaded, 16)
                    sp.dma_start(dt_bias[:, :], a["gdn_dt_bias"][0].partition_broadcast(P)).then_inc(row_loaded, 16)
                    sp.dma_start(neg_a[:, :], a["gdn_a_log"][0].partition_broadcast(P)).then_inc(row_loaded, 16)
                    with sp.Fori(1, HEADS) as h:
                        load_quad(sp, pj_pe, h, gdn_tiles(h), names=("q", "k", "v", "z"))
                    pj_pe.wait(sp, "z", HEADS - 1)
                    load_first_half(sp, a["gdn_out_w"][0], 1)

                @block.gpsimd
                def _(g):
                    hd_pool.ready(g)
                    g.memset(padded[:, :, 0:PAD], 0.0).then_inc(gdn_zero, 1)
                    g.memset(eps2[:, 0:1], EPS).then_inc(gdn_zero, 1)
                    g.memset(eps2[:, 1:2], EPS * P).then_inc(gdn_zero, 1)
                    pool_a.ready(g)
                    link = linker(g, pool_chain)

                    def select(m, pattern, base, mult, fill, op=ALU.is_ge):
                        link(g.affine_select(out=m, in_=m, compare_op=op, fill=fill, base=base, pattern=pattern,
                                             channel_multiplier=mult))

                    g.memset(tri[:, :], 1.0)
                    g.memset(causal[:, :], 0.0)
                    g.memset(last_row[:, :], 1.0)
                    pool_a.mark(g.memset(level_mask[:, :, :], 1.0), "fill")
                    pool_a.wait(g, "fill")
                    select(tri[:, :], [[1, P]], 0, -1, 0.0)
                    select(causal[:, :], [[1, P]], 0, -1, MASKED)
                    select(last_row[:, :], [[0, P]], -(P - 1), 1, 0.0)
                    for n, s in enumerate(levels):
                        nb = P // (2 * s)
                        m = level_mask[:, n, :].rearrange("p (b r e) -> p b r e", r=2, e=s)
                        select(m, [[0, nb], [1, 2], [0, s]], -1, 0, 0.0)
                        select(m, [[-2 * s, nb], [0, 2], [0, s]], 0, 1, 0.0)
                        select(m, [[2 * s, nb], [0, 2], [0, s]], s - 1, -1, 0.0)
                    pool_a.mark(g.memset(a_in[:, :, :], 0.0), "masks")
                    act_a.wait(g, "exp_rest")

                    def body(h, _):
                        hd_dve.wait(g, "rel", h)
                        hd_pool.mark(g.tensor_tensor(decayT[:, :, :], decayT[:, :, :], along(causal[:, :]), ALU.add), "rel")
                        hd_dve.wait(g, "k_tok", h)
                        hd_pe.wait(g, "k_flip", h)
                        hd_pool.mark(g.tensor_tensor(kb_tok, k_tok[:, :, :], per_tok("beta", h), ALU.mult), "kb_tok")
                        hd_pool.mark(g.tensor_tensor(k_rest[:, :, :], k_tok[:, :, :], per_tok("exp_rest", h), ALU.mult), "k_rest")
                        hd_dve.wait(g, "AT", h)
                        hd_pe.wait(g, "kT", h)
                        hd_pool.wait(g, "k_rest", h)
                        for n, s in enumerate(levels):
                            if n >= 2:
                                hd_pe.wait(g, f"Y{levels[n - 2]}b", h)
                            if n == 2:
                                hd_dve.wait(g, "invT1b", h)
                            hd_pool.mark(g.tensor_tensor(part[n % 2][:, :, :], AT[:, :, :], along(level_mask[:, n, :]), ALU.mult), f"part{s}")
                    for_heads(g, body)

                @block.tensor
                def _(pe):
                    pe_a.ready(pe)
                    pe.wait_ge(ab_loaded, 16)
                    for h in range(2):
                        for k in range(KT):
                            last = nc.tensor.matmul(bank[0:2 * HEADS, 6 + h, :], w_ab[:, k, :], hT[:, k, h * HALF:(h + 1) * HALF],
                                                    start=(k == 0), stop=(k == KT - 1))
                    pe_a.mark(last, "rows")
                    act_a.wait(pe, "rows")
                    pool_a.wait(pe, "masks")
                    for t in range(TT):
                        last = nc.tensor.transpose(bank[:, 4, t * 2 * HEADS:(t + 1) * 2 * HEADS], ab_rows[:, t * P:(t + 1) * P],
                                                   ident[0:2 * HEADS, 0:2 * HEADS])
                    pe_a.mark(last, "ab")
                    hd_pe.ready(pe)
                    pj_pe.ready(pe)

                    def project_head(head):
                        for b, name in enumerate(("q", "k", "v", "z")):
                            pe.wait_ge(w_loaded[b], (head + (q0 + 1)) * 16)
                            if b < 2:
                                pj_act.wait(pe, ("v_in", "z")[b], head, back=1)
                            else:
                                pj_act.wait(pe, ("q_in", "k_in")[b - 2], head)
                            for n in range(2):
                                for k in range(KT):
                                    last = nc.tensor.matmul(bank[:, 2 * (b % 2) + n, :], ring[:, b, k, :], hT[:, k, n * HALF:(n + 1) * HALF],
                                                            start=(k == 0), stop=(k == KT - 1))
                                    if (n, k) == (1, KT - 1):
                                        pj_pe.mark(last, name)
                                    yield

                    def each(dst, lhs, rhs, name):
                        for c in range(NCH):
                            last = nc.tensor.matmul(dst[:, c, :], lhs(c), rhs(c), start=True, stop=True)
                        hd_pe.mark(last, name)

                    def each_half(dst, lhs, rhs, name, before=lambda x: None):
                        for n, x in enumerate("ab"):
                            before(x)
                            for c in range(n * NCH // 2, (n + 1) * NCH // 2):
                                last = nc.tensor.matmul(dst[:, c, :], lhs(c), rhs(c), start=True, stop=True)
                            hd_pe.mark(last, name + x)

                    def flip(dst, src, name):
                        for c in range(NCH):
                            last = nc.tensor.transpose(dst[:, c, :], src(c), ident[:, :])
                        hd_pe.mark(last, name)

                    def body(h, after):
                        coming = project_head(after) if after is not None else iter(())

                        def fill(n):
                            for _ in range(n):
                                next(coming, None)

                        hd_dve.wait(pe, "g_col", h, back=1)
                        hd_dve.wait(pe, f"o{NCH - 1}", h, back=1)
                        for c in range(NCH):
                            last = nc.tensor.matmul(R5[:, c, :], g_col[:, c:c + 1].broadcast_to([P, P]), ident[:, :], start=True, stop=True)
                        hd_pe.mark(last, "g_row")
                        fill(3)
                        act_k.wait(pe, "k_silu", h)
                        hd_dve.wait(pe, "y", h, back=1)
                        flip(R4, lambda c: ck[:, c * P:(c + 1) * P], "k_flip")
                        fill(8)
                        hd_act.wait(pe, "q_sq", h)
                        hd_dve.wait(pe, "rel", h)
                        for c in range(NCH):
                            last = nc.tensor.matmul(R5[:, 0, c:c + 1], prod[:, c, :], ones[:, 0:1], start=True, stop=True)
                        hd_pe.mark(last, "q_ss")
                        hd_dve.wait(pe, "k_tok", h)
                        hd_act.wait(pe, "q_rms", h)
                        flip(R5, lambda c: k_tok[:, c, :], "kT")
                        fill(3)
                        hd_pool.wait(pe, "kb_tok", h)
                        hd_act.wait(pe, "k_sq", h)
                        flip(R4, lambda c: kb_tok[:, c, :], "kbT")
                        fill(1)
                        hd_act.wait(pe, "kT", h)
                        each(R5, lambda c: kT[:, c, :], lambda c: qT[:, c, :], "qk")
                        hd_act.wait(pe, "kbT", h)
                        each(R4, lambda c: kT[:, c, :], lambda c: kbT[:, c, :], "kk")
                        fill(4)
                        hd_dve.wait(pe, "AT", h)
                        hd_pool.wait(pe, "part1", h)
                        each_half(R4, lambda c: part[0][:, c, :], lambda c: ident[:, :], "Y1")
                        for n, s in enumerate(levels):
                            if n == 0:
                                continue
                            fill(1)
                            hd_pool.wait(pe, f"part{s}", h)
                            if s == 64:
                                hd_dve.wait(pe, f"inv{levels[n - 1]}b", h)
                                hd_act.wait(pe, "v_silu", h)
                                flip(R5, lambda c: cv[:, c * P:(c + 1) * P], "v_flip")
                            each_half(R4, lambda c: part[n % 2][:, c, :], lambda c: inv[:, c, :], f"Y{s}",
                                      lambda x: hd_dve.wait(pe, f"invT{levels[n - 1]}{x}", h))
                            fill(1)
                            if n == 1:
                                hd_dve.wait(pe, "attn", h)
                            if s < 64:
                                each_half(R5, lambda c: invT[:, c, :], lambda c: prod[:, c, :], f"TY{s}",
                                          lambda x: hd_act.wait(pe, f"prod{s}{x}", h))
                            each_half(R4, lambda c: prod[:, c, :], lambda c: invT[:, c, :], f"YT{s}",
                                      lambda x: hd_act.wait(pe, f"prod{s}{x}", h))
                        for c in range(NCH):
                            fill(c % 2 if c else 4)
                            if c == 0:
                                hd_dve.wait(pe, "invT64b", h)
                                hd_dve.wait(pe, "mem_zero", h)
                                hd_dve.wait(pe, "v_tok", h)
                            else:
                                hd_dve.wait(pe, f"mem{c - 1}", h)
                            hd_pe.mark(nc.tensor.matmul(R4[:, 0, :], kT[:, c, :], memory[:, :], start=True, stop=True), f"read{c}")
                            if c:
                                hd_dve.wait(pe, f"o{c - 1}", h)
                                hd_act.wait(pe, f"o{c - 1}", h)
                            nc.tensor.matmul(R5[:, 4, :], qT[:, c, :], memory[:, :], start=True, stop=True)
                            fill(1)
                            hd_dve.wait(pe, f"delta{c}", h)
                            hd_pe.mark(nc.tensor.matmul(R4[:, 4, :], invT[:, c, :], delta[:, 0, :], start=True, stop=True), f"new{c}")
                            fill(1)
                            hd_act.wait(pe, f"new{c}", h)
                            hd_pool.wait(pe, "k_rest", h)
                            hd_pe.mark(nc.tensor.matmul(R5[:, 0, :], k_rest[:, c, :], delta[:, 1, :], start=True, stop=True), f"mem{c}")
                            hd_pe.mark(nc.tensor.matmul(R4[:, 4, :], attnT[:, c, :], delta[:, 1, :], start=True, stop=True), f"o{c}")
                        fill(64)
                        hd_dve.wait(pe, "o_tok", h)
                        flip(R4, lambda c: o_normed[:, c, :], "o_flip")

                    first = project_head(0)
                    for _ in range(4 * KT):
                        next(first)
                    pool_a.wait(pe, "masks")
                    dve_a.wait(pe, "g_step")
                    pe_a.mark(nc.tensor.matmul(bank[:, 5, 0:HEADS * NCH], tri[:, :], step[:, :, :].rearrange("p h c -> p (h c)"),
                                               start=True, stop=True), "cum")
                    for _ in range(2 * KT):
                        next(first)
                    dve_a.wait(pe, "g")
                    pe_a.mark(nc.tensor.matmul(bank[:, 6, 0:HEADS * NCH], last_row[:, :],
                                               cols["g"][:, :, :].rearrange("p h c -> p (h c)"), start=True, stop=True), "last")
                    for _ in first:
                        pass
                    pe.wait_ge(g_first, 1)
                    act_a.wait(pe, "exp_rest")
                    for_heads(pe, body)

                @block.scalar
                def _(act):
                    hd_act.ready(act)
                    pj_act.ready(act)
                    act_k.ready(act)
                    act.wait_ge(gdn_zero, 3)

                    def take(head, n, name):
                        pj_pe.wait(act, name, head)
                        (dve_k if name == "k" else hd_dve).wait(act, f"{name}c{TAPS4 - 1}", head, back=1)
                        pj_act.mark(act.activation(padded[:, n, PAD:], pair(n % 2), ACT.Copy), f"{name}_in")

                    def take_z(head):
                        pj_pe.wait(act, "z", head)
                        hd_dve.wait(act, "y", head, back=1)
                        pj_act.mark(act.activation(silu_z[:, :], pair(1), ACT.Silu), "z")

                    def key_silu(head):
                        dve_k.wait(act, f"kc{TAPS4 - 1}", head)
                        act_k.mark(act.activation(ck[:, :], ck[:, :], ACT.Silu), "k_silu")

                    def output_square(h, c):
                        hd_dve.wait(act, f"o{c}", h)
                        hd_act.mark(act.activation(inv[:, c, :], o_tok[:, c, :], ACT.Square, accum_out=stat[:, 2, c:c + 1]), f"o_sq{c}")

                    def body(h, after):
                        hd_pe.wait(act, "k_flip", h)
                        hd_act.mark(act.activation(inv[:, :, :], R4, ACT.Square), "k_sq")
                        hd_dve.wait(act, f"qc{TAPS4 - 1}", h)
                        hd_dve.wait(act, "k_ss", h)
                        hd_act.mark(act.activation(stat[:, 0, :], stat[:, 0, :], ACT.Sqrt, bias=eps2[:, 0:1]), "k_rms")
                        hd_act.mark(act.activation(cq[:, :], cq[:, :], ACT.Silu), "q_silu")
                        hd_act.wait(act, "q_silu", h)
                        hd_act.mark(act.activation(prod[:, :, :], qT, ACT.Square), "q_sq")
                        hd_pe.wait(act, "q_ss", h)
                        hd_act.mark(act.activation(stat[:, 1, :], R5[:, 0, 0:NCH], ACT.Sqrt, bias=eps2[:, 1:2], scale=float(P)), "q_rms")
                        for name, r, dst in (("kT", R5, kT), ("kbT", R4, kbT)):
                            hd_pe.wait(act, name, h)
                            hd_act.mark(act.activation(dst[:, :, :], r, ACT.Copy), name)
                        hd_pool.wait(act, "rel", h)
                        hd_act.mark(act.activation(decayT[:, :, :], decayT[:, :, :], ACT.Exp), "decay")
                        for s in levels[1:]:
                            for n, x in enumerate("ab"):
                                half = slice(n * NCH // 2, (n + 1) * NCH // 2)
                                hd_pe.wait(act, f"Y{s}{x}", h)
                                hd_act.mark(act.activation(prod[:, half, :], R4[:, half, :], ACT.Copy), f"prod{s}{x}")
                            if s == 4 and after is not None:
                                take(after, 0, "q")
                            if s == 32:
                                hd_dve.wait(act, f"vc{TAPS4 - 1}", h)
                                hd_act.mark(act.activation(cv[:, :], cv[:, :], ACT.Silu), "v_silu")
                        if after is not None:
                            take(after, 1, "k")
                        for c in range(NCH):
                            hd_pe.wait(act, f"new{c}", h)
                            hd_act.mark(act.activation(delta[:, 1, :], R4[:, 4, :], ACT.Copy), f"new{c}")
                            hd_dve.wait(act, "q_inv", h)
                            hd_pe.wait(act, f"o{c}", h)
                            hd_act.mark(act.activation(o_tok[:, c, :], R4[:, 4, :], ACT.Copy, scale=stat[:, 1, c:c + 1]), f"o{c}")
                            if c:
                                output_square(h, c - 1)
                            if c == 6 and after is not None:
                                take(after, 2, "v")
                        output_square(h, NCH - 1)
                        hd_act.wait(act, f"o_sq{NCH - 1}", h)
                        hd_act.mark(act.activation(stat[:, 2, :], stat[:, 2, :], ACT.Sqrt, bias=eps2[:, 0:1], scale=1.0 / P), "o_rms")
                        if after is not None:
                            key_silu(after)
                            take_z(after)

                    act_a.ready(act)
                    ab = bank[:, 4, 0:P].rearrange("p (t x h) -> p x h t", x=2, h=HEADS)
                    act.wait_ge(row_loaded, 32)
                    act_a.mark(act.activation(neg_a[:, :], neg_a[:, :], ACT.Exp), "neg_a")
                    pe_a.wait(act, "rows")
                    act_a.mark(act.activation(ab_rows, pair(3)[0:2 * HEADS], ACT.Copy), "rows")
                    pe_a.wait(act, "ab")
                    act_a.mark(act.activation(cols["beta"][:, :, :], ab[:, 1], ACT.Sigmoid), "beta")
                    dve_a.wait(act, "a_in")
                    act_a.mark(act.activation(tmp[0][:, :, :], a_in[:, :, :], ACT.Abs), "abs")
                    act_a.wait(act, "abs")
                    act_a.mark(act.activation(tmp[1][:, :, :], tmp[0][:, :, :], ACT.Exp, scale=-1.0), "exp")
                    take(0, 0, "q")
                    take(0, 1, "k")
                    dve_a.wait(act, "g")
                    act_a.mark(act.activation(cols["exp_g"][:, :, :], cols["g"][:, :, :], ACT.Exp), "exp_g")
                    take(0, 2, "v")
                    pe_a.wait(act, "last")
                    act_a.mark(act.activation(cols["exp_last"][:, :, :],
                                              bank[:, 6, 0:HEADS * NCH].rearrange("p (h c) -> p h c", h=HEADS), ACT.Exp), "exp_last")
                    dve_a.wait(act, "rest")
                    act_a.mark(act.activation(cols["exp_rest"][:, :, :], tmp[2][:, :, :], ACT.Exp), "exp_rest")
                    key_silu(0)
                    take_z(0)
                    for_heads(act, body)

                @block.vector
                def _(dve):
                    hd_dve.ready(dve)
                    dve_k.ready(dve)
                    dve.wait_ge(gdn_zero, 3)

                    def tap(h, n, j, name, dst):
                        w = vec(f"gdn_conv{j}", h + n * HEADS)
                        steps = dve_k if name == "k" else hd_dve
                        if j == 0:
                            pj_act.wait(dve, f"{name}_in", h)
                            steps.mark(dve.tensor_scalar(dst[:, :], padded[:, n, 0:S], w, None, ALU.mult), f"{name}c0")
                        else:
                            steps.wait(dve, f"{name}c{j - 1}", h)
                            steps.mark(dve.scalar_tensor_tensor(out=dst[:, :], in0=padded[:, n, j:j + S], scalar=w, in1=dst[:, :],
                                                                 op0=ALU.mult, op1=ALU.add), f"{name}c{j}")

                    def inverse_root(h, n, name, source=None):
                        if source is not None:
                            hd_act.wait(dve, f"{name}_sq", h)
                            hd_dve.mark(dve.tensor_reduce(out=stat[:, n, :], in_=source, op=ALU.add, axis=AX.X), f"{name}_ss")
                        hd_act.wait(dve, f"{name}_rms", h)
                        hd_dve.mark(dve.reciprocal(stat[:, n, :], stat[:, n, :]), f"{name}_inv")
                        hd_dve.wait(dve, f"{name}_inv", h)
                        return stat[:, n, :].unsqueeze(2).broadcast_to(tok_shape)

                    dve_a.ready(dve)
                    link = linker(dve, chain)
                    ab = bank[:, 4, 0:P].rearrange("p (t x h) -> p x h t", x=2, h=HEADS)
                    dve.wait_ge(row_loaded, 32)
                    pool_a.wait(dve, "masks")
                    pe_a.wait(dve, "ab")
                    act_a.wait(dve, "beta")
                    dve_a.mark(dve.tensor_tensor(a_in[:, :, :], ab[:, 0], dt_bias[:, :].unsqueeze(2).broadcast_to([P, HEADS, NCH]),
                                                 ALU.add), "a_in")
                    act_a.wait(dve, "exp")
                    log1p_steps(dve, link, tmp[2][:, :, :], tmp[1][:, :, :], tmp[3][:, :, :], tmp[4][:, :, :])
                    link(dve.scalar_tensor_tensor(out=tmp[2][:, :, :], in0=a_in[:, :, :], scalar=0.0, in1=tmp[2][:, :, :],
                                                  op0=ALU.max, op1=ALU.add))
                    act_a.wait(dve, "neg_a")
                    dve_a.mark(dve.scalar_tensor_tensor(out=step[:, :, :], in0=tmp[2][:, :, :], scalar=-1.0,
                                                        in1=neg_a[:, :].unsqueeze(2).broadcast_to([P, HEADS, NCH]),
                                                        op0=ALU.mult, op1=ALU.mult), "g_step")
                    pe_a.wait(dve, "cum")
                    dve_a.mark(dve.tensor_copy(cols["g"][:, :, :], bank[:, 5, 0:HEADS * NCH].rearrange("p (h c) -> p h c", h=HEADS)), "g")
                    pe_a.wait(dve, "last")
                    act_a.wait(dve, "exp_last")
                    dve_a.wait(dve, "g")
                    dve_a.mark(dve.tensor_tensor(tmp[2][:, :, :], bank[:, 6, 0:HEADS * NCH].rearrange("p (h c) -> p h c", h=HEADS),
                                                 cols["g"][:, :, :], ALU.subtract), "rest")
                    act_a.wait(dve, "exp_g")
                    dve_a.mark(dve.scalar_tensor_tensor(out=cols["neg_beta_exp_g"][:, :, :], in0=cols["beta"][:, :, :], scalar=-1.0,
                                                        in1=cols["exp_g"][:, :, :], op0=ALU.mult, op1=ALU.mult), "neg")
                    act_a.wait(dve, "exp_rest")
                    dve_a.wait(dve, "neg")
                    dve.tensor_copy(g_col[:, :], cols["g"][:, 0, :]).then_inc(g_first, 1)
                    for j in range(TAPS4):
                        tap(0, 1, j, "k", ck)

                    def body(h, after):
                        hd_pe.wait(dve, "g_row", h)
                        hd_dve.mark(dve.tensor_tensor(decayT[:, :, :], R5, per_tok("g", h), ALU.subtract), "rel")
                        for j in range(TAPS4):
                            tap(h, 0, j, "q", cq)
                        by = inverse_root(h, 0, "k", inv[:, :, :])
                        hd_dve.mark(dve.tensor_tensor(k_tok[:, :, :], R4, by, ALU.mult), "k_tok")
                        hd_act.wait(dve, "q_rms", h)
                        hd_dve.mark(dve.reciprocal(stat[:, 1, :], stat[:, 1, :]), "q_inv")
                        hd_dve.wait(dve, "q_inv", h)
                        hd_dve.mark(dve.tensor_tensor(stat[:, 3, :], stat[:, 1, :], cols["exp_g"][:, h, :], ALU.mult), "q_dec")
                        hd_act.wait(dve, "decay", h)
                        hd_pe.wait(dve, "qk", h)
                        hd_dve.mark(dve.tensor_tensor(attnT[:, :, :], R5, decayT[:, :, :], ALU.mult), "attn")
                        hd_pe.wait(dve, "kk", h)
                        hd_dve.mark(dve.tensor_tensor(AT[:, :, :], R4, decayT[:, :, :], ALU.mult), "AT")
                        def half_step(dst, first, second, name, before, **ops):
                            for n, x in enumerate("ab"):
                                half = slice(n * NCH // 2, (n + 1) * NCH // 2)
                                before(x)
                                hd_dve.mark(dve.scalar_tensor_tensor(out=dst[:, half, :], in0=first(half), scalar=-1.0, in1=second(half),
                                                                     op0=ALU.mult, op1=ALU.add), name + x)

                        eye = lambda half: ident[:, :].unsqueeze(1).broadcast_to([P, NCH // 2, P])
                        half_step(inv, lambda half: R4[:, half, :], eye, "inv1", lambda x: hd_pe.wait(dve, f"Y1{x}", h))
                        half_step(invT, lambda half: part[0][:, half, :], eye, "invT1", lambda x: None)
                        tap(h, 2, 0, "v", cv)
                        for n, s in enumerate(levels):
                            if n == 0:
                                continue
                            before = levels[n - 1]

                            def ready(dst, steps):
                                def wait(x):
                                    hd_pe.wait(dve, f"{steps}{s}{x}", h)
                                    hd_dve.wait(dve, f"{dst}{before}{x}", h)
                                return wait

                            if s < 64:
                                half_step(inv, lambda half: R5[:, half, :], lambda half: inv[:, half, :], f"inv{s}", ready("inv", "TY"))
                            else:
                                hd_pe.wait(dve, "v_flip", h)
                                hd_dve.mark(dve.tensor_tensor(v_tok[:, :, :], R5, per_tok("beta", h), ALU.mult), "v_tok")
                            half_step(invT, lambda half: R4[:, half, :], lambda half: invT[:, half, :], f"invT{s}", ready("invT", "YT"))
                            if n < TAPS4:
                                tap(h, 2, n, "v", cv)
                        hd_pe.wait(dve, f"o{NCH - 1}", h, back=1)
                        hd_dve.mark(dve.memset(memory[:, :], 0.0), "mem_zero")
                        for c in range(NCH):
                            hd_pe.wait(dve, f"read{c}", h)
                            hd_dve.mark(dve.scalar_tensor_tensor(out=delta[:, 0, :], in0=R4[:, 0, :],
                                                                 scalar=cols["neg_beta_exp_g"][:, h, c:c + 1],
                                                                 in1=v_tok[:, c, :], op0=ALU.mult, op1=ALU.add), f"delta{c}")
                            hd_pe.wait(dve, f"mem{c}", h)
                            hd_dve.mark(dve.scalar_tensor_tensor(out=memory[:, :], in0=memory[:, :], scalar=cols["exp_last"][:, h, c:c + 1],
                                                                 in1=R5[:, 0, :], op0=ALU.mult, op1=ALU.add), f"mem{c}")
                            hd_act.wait(dve, f"o{c}", h)
                            hd_dve.mark(dve.scalar_tensor_tensor(out=o_tok[:, c, :], in0=R5[:, 4, :], scalar=stat[:, 3, c:c + 1],
                                                                 in1=o_tok[:, c, :], op0=ALU.mult, op1=ALU.add), f"o{c}")
                        hd_dve.mark(dve.tensor_copy(g_col[:, :], cols["g"][:, h if after is None else after, :]), "g_col")
                        if after is not None:
                            for j in range(TAPS4):
                                tap(after, 1, j, "k", ck)
                        by = inverse_root(h, 2, "o")
                        hd_dve.mark(dve.tensor_tensor(o_normed[:, :, :], o_tok, by, ALU.mult), "o_tok")
                        hd_pe.wait(dve, "o_flip", h)
                        hd_dve.mark(dve.scalar_tensor_tensor(out=yT[:, h, :], in0=pair(2), scalar=vec("onorm", 0), in1=silu_z[:, :],
                                                             op0=ALU.mult, op1=ALU.mult), "y")
                    for_heads(dve, body)
        project_out("out1", a["gdn_out_w"][0], 1)

        layers.close()
        with ExitStack() as scope:
            gain = sb("final_gain", [P, D], scope)
            junk = sb("final_junk", [P, 2, D], scope)
            sums = sb("final_sums", [P, TT], scope)
            gain_loaded = sem("final_gain_loaded")
            act_f = Steps(sem("final_act"), SQUARES)
            dve_f = Steps(sem("final_dve"), [f"tok{t}" for t in range(TT)])
            with nc.Block() as block:
                @block.sync
                def _(sp):
                    sp.dma_start(gain[:, :], a["final_g"].partition_broadcast(P)).then_inc(gain_loaded, 16)

                @block.vector
                def _(dve):
                    dve_f.ready(dve)
                    dve.wait_ge(gain_loaded, 16)
                    for t in range(TT):
                        dve_f.mark(dve.scalar_tensor_tensor(out=resid[:, t, :], in0=resid[:, t, :], scalar=inv_rms[:, t:t + 1], in1=gain[:, :],
                                                            op0=ALU.mult, op1=ALU.mult), f"tok{t}")
                    act_f.wait(dve, "rms")
                    dve_f.wait(dve, f"tok{TT - 1}")
                    dve.reciprocal(inv_rms[:, :], sums[:, :])

                @block.scalar
                def _(act):
                    act_f.ready(act)
                    token_rms(act, act_f, junk, sums, lambda t: dve_f.wait(act, f"tok{t}"))
        w_in = a["w_in_2"][0]
        CA, CB, ZC, US, ZS, GC, GS = (c // P for c in (0, D, 2 * D, 3 * D, 3 * D + 512, 4 * D, 5 * D))
        ST = GROUPS * GH // P
        norm_transpose("norm2", lambda k: vec("pre_g", k), lambda k: 0.0, [(ring[:, b, :, :], columns(w_in, US + b)) for b in range(ST)])

        def conv_tiles_of(i):
            return [(ring[:, 2 * p + x, :, :], columns(w_in, i * 2 + (p + (CA, CB)[x]))) for p in range(2) for x in range(2)]

        def ssm_tiles_of(i):
            return [tile for p in range(2) for tile in ((ring[:, 2 * p, :, :], columns(w_in, i * 2 + (p + GS))),
                                                        (ring[:, 2 * p + 1, 0:ST, :], columns(a["w_ssm_out_2"][0], i * 2 + p)))]

        def merge_tiles_of(i):
            return [tile for p in range(2) for tile in ((ring[:, 2 * p, :, :], columns(w_in, i * 2 + (p + GC))),
                                                        (ring[:, 2 * p + 1, :, :], columns(a["w_conv_out_2"][0], i * 2 + p)))]

        TILES = [f"tile{b}" for b in range(4)]
        u_dram = nc.dram_tensor("u_scratch", (ST * P, BLK, NBLK), F32, kind="Internal").ap()
        y_dram = nc.dram_tensor("y_scratch", (ST * P, BLK, NBLK), F32, kind="Internal").ap()
        ssm_y = sb("ssm_y", [P, ST, S])

        with ExitStack() as scope:
            flat = yT[:, :, :].rearrange("p k s -> p (k s)")
            lift = flat[:, 0:4096].rearrange("p (x j t h) -> p x j t h", x=2, j=PAIRS, t=BLK)
            kernel16 = flat[0:GH, 4096:8192].rearrange("p (g c) -> p g c", g=GROUPS)
            u_blk = flat[:, 0:4096].rearrange("p (g k) -> p g k", g=GROUPS)
            HP = PAIRS // 2
            w1, w2, w3, z_re = (flat[:, 4096 + n * 1024:5120 + n * 1024].rearrange("p (j k) -> p j k", j=HP) for n in range(4))
            turn = ring[:, :, :, :].rearrange("p b k c -> p (b k c)").rearrange("p (x j k) -> p x j k", x=2, j=PAIRS)
            turn_re, turn_im = turn[:, 0], turn[:, 1]
            B_lift = sb("B_lift", [P, 2, PAIRS, P], scope)
            C_pow = sb("C_pow", [P, 2, PAIRS, BLK + 1, GH], scope)
            K_lift = sb("K_lift", [P, GROUPS, P], scope)
            shrink = sb("shrink", [P, PAIRS, NBLK], scope)
            z_im = ssm_y[:, 2, :].rearrange("p (j k) -> p j k", j=HP)
            y_blk = ssm_y[:, 0:2, :].rearrange("p c (g k) -> p (c g) k", k=NBLK)
            st_re, st_im = (sb(n, [P, HP, NBLK + 2], scope) for n in ("st_re", "st_im"))
            par = sb("s5_par", [P, 24, PAIRS], scope)
            (lr, li, dt, mag, th, nn, red, co, si, ar, ai, den, zr, zi, x1, x2, c8, s8, rho, ab, ph) = (par[:, n, :] for n in range(21))
            pw = sb("s5_pow", [P, 2, BLK + 1, PAIRS], scope)
            bb = sb("s5_b", [P, 4, PAIRS, GH], scope)
            cc = sb("s5_c", [P, 2, PAIRS, GH], scope)
            c_rows = ssm_y[:, 3, :].rearrange("p (x t g s) -> p x t g s", x=2, t=ST, g=2)
            d16 = sb("s5_d", [GH, 2, PAIRS], scope)
            half_pi = sb("half_pi", [P, 1], scope)
            par_loaded, c_loaded, d_loaded, u_loaded = sem("par_loaded"), sem("c_loaded"), sem("d_loaded"), sem("u_loaded")
            K_placed, y_stored, y_loaded = sem("K_placed"), sem("y_stored"), sem("y_loaded")
            u_perm = shrink[:, :, :].rearrange("p j k -> p (j k)").rearrange("p (b t k) -> p b t k", b=2, t=BLK)
            silu_zs = B_lift[:, :, :, :].rearrange("p x j c -> p (x j c)").rearrange("p (n s) -> p n s", n=ST)
            u_stored = [sem("u_stored0"), sem("u_stored1")]
            q0 = quads[0]
            quads[0] += 3
            pe_s = Steps(sem("s5_pe"), ["u0", "c_flip"] + [f"u{b}" for b in range(1, ST)] + ["kernel", "B_flip"]
                         + [f"{n}{h}" for h in range(2) for n in ("w", "y")] + [f"z{b}" for b in range(ST)])
            act_s = Steps(sem("s5_act"), ["dt", "mag", "rho", "sin", "cos_abs", "cos"] + [f"u{b}" for b in range(ST)]
                          + ["kernel", "B", "y0", "y1", "z0"] + [f"gelu{n}" for n in range(ST)] + [f"z{b}" for b in range(1, ST)])
            dve_s = Steps(sem("s5_dve"), ["rates", "reduced", "c", "b", "C", "lift", "kernel", "s0", "s1"])
            pool_s = Steps(sem("s5_pool"), ["zero"])
            chain = sem("s5_chain")
            with nc.Block() as block:
                @block.sync
                def _(sp):
                    for g in range(2):
                        half = slice(g * NS, (g + 1) * NS)
                        sp.dma_start(lr[half], a["ssm_lambda_re_2"][0].rearrange("(j g) p -> g p j", g=2)[g], allow_slow_non_contiguous=True).then_inc(par_loaded, 16)
                        sp.dma_start(li[half], a["ssm_lambda_im_2"][0].rearrange("(j g) p -> g p j", g=2)[g], allow_slow_non_contiguous=True).then_inc(par_loaded, 16)
                        sp.dma_start(dt[half], a["ssm_log_dt_2"][0].rearrange("(j g) -> g j", g=2)[g].partition_broadcast(NS), allow_slow_non_contiguous=True).then_inc(par_loaded, 16)
                        for x, n in enumerate(("ssm_b_re_2", "ssm_b_im_2")):
                            sp.dma_start(bb[half, x], a[n][0].rearrange("(j g) p h -> g p j h", g=2)[g]).then_inc(par_loaded, 16)
                        for x, n in enumerate(("ssm_c_re_2", "ssm_c_im_2")):
                            sp.dma_start(c_rows[:, x, :, g, :], a[n][0].rearrange("(t r) h p -> (r h) t p", t=ST)).then_inc(c_loaded, 16)
                        sp.dma_start(d16[:, g, :], a["ssm_d_2"][0].rearrange("(j g) h -> g h j", g=2)[g],
                                     allow_slow_non_contiguous=True).then_inc(d_loaded, 16)
                    for b in range(ST):
                        act_s.wait(sp, f"u{b}")
                        sp.dma_start(u_dram[b * P:(b + 1) * P], u_perm[:, b % 2, :, :]).then_inc(u_stored[b % 2], 16)
                    dve_s.wait(sp, "kernel")
                    pool_s.wait(sp, "zero")
                    for r in range(BLK):
                        sp.dma_start(K_lift[r * GH:(r + 1) * GH, :, (BLK - 1 - r) * GH:], kernel16[:, :, 0:(r + 1) * GH]).then_inc(K_placed, 16)
                    pe_s.wait(sp, "B_flip")
                    for p in range(2):
                        sp.wait_ge(u_stored[p], 32)
                    for t in range(BLK):
                        sp.dma_start(u_blk[(BLK - 1 - t) * GH:(BLK - t) * GH, :, :],
                                     u_dram.rearrange("(g h) t k -> t h g k", h=GH)[t]).then_inc(u_loaded, 16)
                    for h in range(2):
                        if h:
                            dve_s.wait(sp, "s1")
                            for b in range(ST):
                                sp.dma_start(ring[:, b, :, :], columns(w_in, ZS + b)).then_inc(w_loaded[b], 16)
                        act_s.wait(sp, f"y{h}")
                        for t in range(BLK):
                            for g in range(2):
                                sp.dma_start(y_dram.rearrange("(j g h) t k -> t g h j k", h=GH, g=2)[t, g][:, h * HP:(h + 1) * HP, :],
                                             y_blk[t * GH:(t + 1) * GH, g * HP:(g + 1) * HP, :]).then_inc(y_stored, 16)
                    sp.wait_ge(y_stored, 2 * 2 * BLK * 16)
                    sp.dma_start(flat[:, 4096:8192].rearrange("p (c x) -> p c x", c=ST),
                                 y_dram.rearrange("(c p) t k -> p c (t k)", p=P)).then_inc(y_loaded, 16)
                    for b in range(ST):
                        pe_s.wait(sp, f"z{b}")
                        sp.dma_start(ring[:, b, 0:ST, :], columns(a["w_ssm_glu_2"][0], b)).then_inc(w_loaded[b], 16)

                @block.gpsimd
                def _(g):
                    pool_s.ready(g)
                    g.memset(half_pi[:, :], math.pi / 2)
                    g.memset(st_re[:, :, 0:1], 0.0)
                    g.memset(st_im[:, :, 0:1], 0.0)
                    pool_s.mark(g.memset(K_lift[:, :, :], 0.0), "zero")

                @block.tensor
                def _(pe):
                    pe_s.ready(pe)

                    def u_tile(b):
                        pe.wait_ge(w_loaded[b], (q0 + 1) * 16)
                        if b >= 2:
                            act_s.wait(pe, f"u{b - 2}")
                        pe_s.mark(project(b, hT), f"u{b}")

                    u_tile(0)
                    pe.wait_ge(c_loaded, 64)
                    for x in range(2):
                        for t in range(ST):
                            last = nc.tensor.transpose(bank[:, 4 + x, t * P:(t + 1) * P], c_rows[:, x, t, :, :].rearrange("p g s -> p (g s)"), ident[:, :])
                    pe_s.mark(last, "c_flip")
                    for b in range(1, ST):
                        u_tile(b)
                    dve_s.wait(pe, "C")
                    dve_s.wait(pe, "b")
                    act_s.wait(pe, f"u{ST - 1}")
                    for n in range(GROUPS):
                        g, j = n % 2, n // 2
                        half = slice(g * NS, (g + 1) * NS)
                        dst = bank[0:GH, 4 * g + j // 4, (j % 4) * P:(j % 4 + 1) * P]
                        for x in range(2):
                            last = nc.tensor.matmul(dst, bb[half, 2 + x, j, :], C_pow[half, x, j, 0:BLK, :].rearrange("p t h -> p (t h)"),
                                                    start=(x == 0), stop=(x == 1))
                    pe_s.mark(last, "kernel")
                    dve_s.wait(pe, "lift")
                    act_s.wait(pe, "kernel")
                    for x in range(2):
                        for j in range(PAIRS):
                            last = nc.tensor.transpose(bank[:, 4 * x + j // 4, (j % 4) * P:(j % 4 + 1) * P],
                                                       lift[:, x, j].rearrange("p t h -> p (t h)"), ident[:, :])
                    pe_s.mark(last, "B_flip")
                    act_s.wait(pe, "B")
                    pe.wait_ge(u_loaded, BLK * 16)
                    pe.wait_ge(K_placed, BLK * 16)
                    for h in range(2):
                        if h:
                            dve_s.wait(pe, "s0")
                        for x in range(2):
                            for jl in range(HP):
                                for g in range(2):
                                    j = h * HP + jl
                                    last = nc.tensor.matmul(bank[g * NS:(g + 1) * NS, 2 * x + jl // 4, (jl % 4) * P:(jl % 4 + 1) * P],
                                                            B_lift[:, x, j, g * NS:(g + 1) * NS], u_blk[:, 2 * j + g, :], start=True, stop=True)
                        pe_s.mark(last, f"w{h}")
                        dve_s.wait(pe, f"s{h}")
                        if h:
                            act_s.wait(pe, "y0")
                        for n in range(2 * HP):
                            g, jl = n % 2, n // 2
                            half, j = slice(g * NS, (g + 1) * NS), h * HP + jl
                            dst = bank[:, 4 + 2 * g + jl // 4, (jl % 4) * P:(jl % 4 + 1) * P]
                            nc.tensor.matmul(dst, K_lift[:, g * PAIRS + j, :], u_blk[:, 2 * j + g, :], start=True, stop=False)
                            nc.tensor.matmul(dst, C_pow[half, 0, j, 1:, :].rearrange("p t h -> p (t h)"), st_re[half, jl, 0:NBLK], start=False, stop=False)
                            last = nc.tensor.matmul(dst, C_pow[half, 1, j, 1:, :].rearrange("p t h -> p (t h)"), st_im[half, jl, 0:NBLK],
                                                    start=False, stop=True)
                        pe_s.mark(last, f"y{h}")
                    for b in range(ST):
                        pe.wait_ge(w_loaded[b], (q0 + 2) * 16)
                        if b >= 2:
                            act_s.wait(pe, f"z{b - 2}")
                        pe_s.mark(project(b, hT), f"z{b}")

                @block.scalar
                def _(act):
                    act_s.ready(act)
                    act.wait_ge(par_loaded, 160)
                    act_s.mark(act.activation(dt, dt, ACT.Exp), "dt")
                    dve_s.wait(act, "rates")
                    act_s.mark(act.activation(mag, x1, ACT.Exp), "mag")
                    act_s.mark(act.activation(rho, x1, ACT.Exp, scale=float(BLK)), "rho")
                    pool_s.wait(act, "zero")
                    dve_s.wait(act, "reduced")
                    act_s.mark(act.activation(si, red, ACT.Sin), "sin")
                    act_s.mark(act.activation(ab, red, ACT.Abs), "cos_abs")
                    act_s.wait(act, "cos_abs")
                    act_s.mark(act.activation(co, ab, ACT.Sin, scale=-1.0, bias=half_pi[:, 0:1]), "cos")
                    for b in range(ST):
                        pe_s.wait(act, f"u{b}")
                        if b >= 2:
                            act.wait_ge(u_stored[b % 2], 16)
                        act_s.mark(act.activation(u_perm[:, b % 2, :, :], pair(b % 2).rearrange("p (k t) -> p t k", t=BLK), ACT.Copy), f"u{b}")
                    pe_s.wait(act, "kernel")
                    dve_s.wait(act, "lift")
                    act_s.mark(act.activation(kernel16.rearrange("p g c -> p (g c)"), bank[0:GH, :, :].rearrange("p b c -> p (b c)"), ACT.Copy), "kernel")
                    pe_s.wait(act, "B_flip")
                    act_s.mark(act.activation(B_lift[:, :, :, :].rearrange("p x j c -> p (x j c)"), bank[:, :, :].rearrange("p b c -> p (b c)"), ACT.Copy), "B")
                    for h in range(2):
                        pe_s.wait(act, f"y{h}")
                        if h:
                            act.wait_ge(y_stored, 2 * BLK * 16)
                        act_s.mark(act.activation(y_blk[:, :, :].rearrange("p g k -> p (g k)"), bank[:, 4:8, :].rearrange("p b c -> p (b c)"), ACT.Copy), f"y{h}")

                    def silu(b):
                        pe_s.wait(act, f"z{b}")
                        act_s.mark(act.activation(silu_zs[:, b, :], pair(b % 2), ACT.Silu), f"z{b}")

                    silu(0)
                    act.wait_ge(y_loaded, 16)
                    for n in range(ST):
                        act_s.mark(act.activation(ssm_y[:, n, :].rearrange("p (k t) -> p t k", t=BLK),
                                                  flat[:, 4096 + n * S:4096 + (n + 1) * S].rearrange("p (t k) -> p t k", t=BLK),
                                                  ACT.Gelu_apprx_tanh), f"gelu{n}")
                    for b in range(1, ST):
                        silu(b)

                @block.vector
                def _(dve):
                    dve_s.ready(dve)
                    link = linker(dve, chain)
                    TT_, TS, STT = dve.tensor_tensor, dve.tensor_scalar, dve.scalar_tensor_tensor

                    def cmul(out_re, out_im, xr, xi, yr, yi, t):
                        TT_(t[0], xr, yr, ALU.mult)
                        link(TT_(t[1], xi, yi, ALU.mult))
                        link(TT_(out_re, t[0], t[1], ALU.subtract))
                        TT_(t[0], xr, yi, ALU.mult)
                        link(TT_(t[1], xi, yr, ALU.mult))
                        link(TT_(out_im, t[0], t[1], ALU.add))

                    act_s.wait(dve, "dt")
                    link(TT_(th, li, dt, ALU.mult))
                    dve_s.mark(TT_(x1, lr, dt, ALU.mult), "rates")
                    MAGIC = 1.5 * 2.0 ** 23
                    link(TS(nn, th, 1.0 / (2 * math.pi), MAGIC, ALU.mult, ALU.add))
                    link(TS(nn, nn, -MAGIC, None, ALU.add))
                    two_pi = [6.28125, float(np.float32(2 * math.pi - 6.28125) - np.float32(2 * math.pi - 6.28125) % np.float32(2.0 ** -21))]
                    two_pi.append(2 * math.pi - sum(two_pi))
                    link(STT(out=red, in0=nn, scalar=-two_pi[0], in1=th, op0=ALU.mult, op1=ALU.add))
                    link(STT(out=red, in0=nn, scalar=-two_pi[1], in1=red, op0=ALU.mult, op1=ALU.add))
                    link(STT(out=red, in0=nn, scalar=-two_pi[2], in1=red, op0=ALU.mult, op1=ALU.add))
                    dve_s.mark(TS(red, red, 3.1415925, -3.1415925, ALU.min, ALU.max), "reduced")
                    pe_s.wait(dve, "c_flip")
                    for g in range(2):
                        half = slice(g * NS, (g + 1) * NS)
                        ins = dve.tensor_copy(cc[half, :, :, :].rearrange("p x (t j) h -> p (x t) j h", t=ST),
                                              bank[half, 4:6, :].rearrange("p x (t j g h) -> p (x t) j g h", t=ST, g=2, h=GH)[:, :, :, g, :])
                    dve_s.mark(ins, "c")
                    act_s.wait(dve, "cos")
                    TT_(ar, mag, co, ALU.mult)
                    TT_(ai, mag, si, ALU.mult)
                    TT_(x2, lr, lr, ALU.mult)
                    link(TT_(den, li, li, ALU.mult))
                    link(TT_(den, den, x2, ALU.add))
                    link(dve.reciprocal(den, den))
                    link(TS(x2, ar, -1.0, None, ALU.add))
                    TT_(zr, x2, lr, ALU.mult)
                    TT_(zi, ai, lr, ALU.mult)
                    link(TT_(nn, ai, li, ALU.mult))
                    link(TT_(zr, zr, nn, ALU.add))
                    link(TT_(nn, x2, li, ALU.mult))
                    link(TT_(zi, zi, nn, ALU.subtract))
                    link(TT_(zr, zr, den, ALU.mult))
                    link(TT_(zi, zi, den, ALU.mult))
                    wide = [P, PAIRS, GH]
                    f1, f2 = (w.rearrange("p j k -> p (j k)") for w in (w1, w2))
                    by_h = lambda v: v.unsqueeze(2).broadcast_to(wide)
                    small = [f[:, 0:256].rearrange("p (j h) -> p j h", j=PAIRS) for f in (f1, f2)]
                    cmul(bb[:, 2], bb[:, 3], bb[:, 0], bb[:, 1], by_h(zr), by_h(zi), small)
                    TS(pw[:, 0, 0, :], lr, 0.0, 1.0, ALU.mult, ALU.add)
                    TS(pw[:, 1, 0, :], lr, 0.0, None, ALU.mult)
                    dve.tensor_copy(pw[:, 0, 1, :], ar)
                    dve_s.mark(dve.tensor_copy(pw[:, 1, 1, :], ai), "b")
                    dve_s.wait(dve, "b")
                    for n in (1, 2, 4):
                        shape = [P, n, PAIRS]
                        t = [f[:, 0:n * PAIRS].rearrange("p (n j) -> p n j", n=n) for f in (f1, f2)]
                        cmul(pw[:, 0, n + 1:2 * n + 1, :], pw[:, 1, n + 1:2 * n + 1, :], pw[:, 0, 1:n + 1, :], pw[:, 1, 1:n + 1, :],
                             pw[:, 0, n:n + 1, :].broadcast_to(shape), pw[:, 1, n:n + 1, :].broadcast_to(shape), t)
                    for n in range(BLK + 1):
                        pr, pi = by_h(pw[:, 0, n, :]), by_h(pw[:, 1, n, :])
                        TT_(small[0], cc[:, 0], pr, ALU.mult)
                        link(TT_(small[1], cc[:, 1], pi, ALU.mult))
                        link(TT_(C_pow[:, 0, :, n, :], small[0], small[1], ALU.subtract))
                        TT_(small[0], cc[:, 0], pi, ALU.mult)
                        link(TT_(small[1], cc[:, 1], pr, ALU.mult))
                        ins = STT(out=C_pow[:, 1, :, n, :], in0=small[0], scalar=-1.0, in1=small[1], op0=ALU.mult, op1=ALU.subtract)
                        if n < BLK:
                            link(ins)
                    dve_s.mark(ins, "C")
                    dve_s.wait(dve, "C")
                    for n in range(BLK):
                        cmul(lift[:, 0, :, n, :], lift[:, 1, :, n, :], bb[:, 2], bb[:, 3], by_h(pw[:, 0, n, :]), by_h(pw[:, 1, n, :]), small)
                    dve_s.mark(TS(c8, co, 1.0, None, ALU.mult), "lift")
                    act_s.wait(dve, "kernel")
                    dve.wait_ge(d_loaded, 32)
                    diag = [GH, GROUPS, GH]
                    dI = bb[0:GH, 0:2, :, :].rearrange("p x j h -> p (x j) h")
                    link(TT_(dI, d16[:, :, :].rearrange("p g j -> p (g j)").unsqueeze(2).broadcast_to(diag), ident[0:GH, 0:GH].unsqueeze(1).broadcast_to(diag), ALU.mult))
                    dve_s.mark(TT_(kernel16[:, :, 0:GH], kernel16[:, :, 0:GH], dI, ALU.add), "kernel")
                    link(dve.tensor_copy(s8, si))
                    t = [ab, ph]
                    for _ in range(3):
                        cmul(x2, nn, c8, s8, c8, s8, t)
                        dve.tensor_copy(c8, x2)
                        link(dve.tensor_copy(s8, nn))
                    for r in range(1):
                        dve.wait_ge(K_placed, BLK * 16)
                    TS(turn_re[:, :, 0:1], lr.unsqueeze(2), 0.0, 1.0, ALU.mult, ALU.add)
                    link(TS(turn_im[:, :, 0:1], lr.unsqueeze(2), 0.0, None, ALU.mult))
                    n = 1
                    while n < NBLK:
                        shape = [P, PAIRS, n]
                        t = [f.rearrange("p (j k) -> p j k", j=PAIRS)[:, :, 0:n] for f in (f1, f2)]
                        cmul(turn_re[:, :, n:2 * n], turn_im[:, :, n:2 * n], turn_re[:, :, 0:n], turn_im[:, :, 0:n],
                             c8.unsqueeze(2).broadcast_to(shape), s8.unsqueeze(2).broadcast_to(shape), t)
                        n *= 2
                        if n < NBLK:
                            cmul(x2, nn, c8, s8, c8, s8, [ab, ph])
                            dve.tensor_copy(c8, x2)
                            link(dve.tensor_copy(s8, nn))
                    act_s.wait(dve, "rho")
                    for p in range(2):
                        dve.wait_ge(u_stored[p], 32)
                    link(dve.tensor_copy(shrink[:, :, :], rho.unsqueeze(2).broadcast_to([P, PAIRS, NBLK])))
                    link(dve.memset(shrink[:, :, 0:1], 0.0))
                    pool_s.wait(dve, "zero")
                    for h in range(2):
                        rows_ = slice(h * HP, (h + 1) * HP)
                        tr, ti = turn_re[:, rows_, :], turn_im[:, rows_, :]
                        w_re, w_im = (bank[:, 2 * x:2 * x + 2, :].rearrange("p b (j k) -> p (b j) k", k=NBLK) for x in range(2))
                        one = lambda v: v.rearrange("p j k -> p (j k)")
                        if h:
                            pe_s.wait(dve, "y0")
                        pe_s.wait(dve, f"w{h}")
                        TT_(w1, w_re, tr, ALU.mult)
                        link(TT_(w2, w_im, ti, ALU.mult))
                        link(TT_(w1, w1, w2, ALU.add))
                        TT_(w3, w_re, ti, ALU.mult)
                        link(TT_(w2, w_im, tr, ALU.mult))
                        link(TT_(w2, w2, w3, ALU.subtract))
                        sh = one(shrink[:, rows_, :])
                        dve.tensor_tensor_scan(one(z_re), sh, one(w1), 0.0, ALU.mult, ALU.add)
                        link(dve.tensor_tensor_scan(one(z_im[:, :, :]), sh, one(w2), 0.0, ALU.mult, ALU.add))
                        TT_(w1, z_re, tr, ALU.mult)
                        link(TT_(w2, z_im[:, :, :], ti, ALU.mult))
                        link(TT_(st_re[:, :, 1:NBLK + 1], w1, w2, ALU.subtract))
                        TT_(w1, z_re, ti, ALU.mult)
                        link(TT_(w2, z_im[:, :, :], tr, ALU.mult))
                        dve_s.mark(TT_(st_im[:, :, 1:NBLK + 1], w1, w2, ALU.add), f"s{h}")

            sig = shrink[:, :, :].rearrange("p j k -> p (j k)").rearrange("p (b s) -> p b s", b=2)
            glu = K_lift[:, :, :].rearrange("p g c -> p (g c)").rearrange("p (n s) -> p n s", n=ST)
            pe_g, act_g = Steps(sem("glu_pe"), [f"glu{b}" for b in range(ST)]), Steps(sem("glu_act"), [f"glu{b}" for b in range(ST)])
            dve_g = Steps(sem("glu_dve"), [f"{n}{b}" for n in ("glu", "z") for b in range(ST)])
            with nc.Block() as block:
                @block.sync
                def _(sp):
                    load_ahead(sp, conv_tiles_of(0), pe_g, 0, [f"glu{b}" for b in range(ST)])

                @block.tensor
                def _(pe):
                    pe_g.ready(pe)
                    for b in range(ST):
                        pe.wait_ge(w_loaded[b], (q0 + 3) * 16)
                        if b >= 2:
                            act_g.wait(pe, f"glu{b - 2}")
                        pe_g.mark(project(b, ssm_y, ST), f"glu{b}")

                @block.scalar
                def _(act):
                    act_g.ready(act)
                    for b in range(ST):
                        pe_g.wait(act, f"glu{b}")
                        if b >= 2:
                            dve_g.wait(act, f"glu{b - 2}")
                        act_g.mark(act.activation(sig[:, b % 2, :], pair(b % 2), ACT.Sigmoid, bias=vec("glu_b", b)), f"glu{b}")

                @block.vector
                def _(dve):
                    dve_g.ready(dve)
                    for b in range(ST):
                        act_g.wait(dve, f"glu{b}")
                        dve_g.mark(dve.tensor_tensor(glu[:, b, :], ssm_y[:, b, :], sig[:, b % 2, :], ALU.mult), f"glu{b}")
                    pe_g.wait(dve, f"glu{ST - 1}")
                    for b in range(ST):
                        dve_g.wait(dve, f"glu{b}")
                        dve_g.mark(dve.tensor_tensor(ssm_y[:, b, :], glu[:, b, :], silu_zs[:, b, :], ALU.mult), f"z{b}")

        silu_zc = sb("silu_zc", [P, KT, S])
        with ExitStack() as scope:
            PAD = TAPS31 - 1
            sig = sb("conv_sig", [P, 2, S], scope)
            padded = sb("conv_padded", [P, 2, PAD + S], scope)
            SIDE = 6
            product = sb("conv_product", [P, 2, S], scope)
            side = sb("conv_side", [P, S], scope)
            taps = sb("conv_taps", [P, 2, 32], scope)
            z_ring = sb("conv_z_ring", [P, 2, KT, P], scope)
            pe_v, pe_z = Steps(sem("conv_pe"), ["a0", "b0", "a1", "b1"]), Steps(sem("conv_z_pe"), ["z0", "z1"])
            act_v = Steps(sem("conv_act"), [n for p in range(2) for n in [f"sig{p}"] + [f"m{j}_{p}" for j in range(SIDE)]])
            act_z = Steps(sem("conv_z_act"), ["z0", "z1"])
            pool_v = Steps(sem("conv_pool"), [f"s{j}_{p}" for p in range(2) for j in range(1, SIDE)])
            dve_v = Steps(sem("conv_dve"), [s + str(p) for p in range(2) for s in ["taps", "cu"] + [f"t{j}_" for j in range(SIDE, TAPS31)] + ["side"]])
            CONV = ("a0", "b0", "a1", "b1")
            pad_zero = sem("conv_pad_zero")
            z_loaded = [sem("conv_z_loaded0"), sem("conv_z_loaded1")]
            q0 = quads[0]
            quads[0] += KT // 2
            with nc.Block() as block:
                @block.sync
                def _(sp):
                    for p in range(2):
                        sp.dma_start(z_ring[:, p, :, :], columns(w_in, ZC + p)).then_inc(z_loaded[p], 16)
                    def z_load(i, p):
                        pe_z.wait(sp, f"z{p}", i, back=1)
                        sp.dma_start(z_ring[:, p, :, :], columns(w_in, i * 2 + (p + ZC))).then_inc(z_loaded[p], 16)

                    load_quad(sp, pe_v, 1, conv_tiles_of(1), names=CONV)
                    with sp.Fori(1, KT // 2 - 1) as i:
                        tiles = conv_tiles_of(i + 1)
                        for p in range(2):
                            for x in range(2):
                                pe_v.wait(sp, CONV[2 * p + x], i)
                                sp.dma_start(*tiles[2 * p + x]).then_inc(w_loaded[2 * p + x], 16)
                            z_load(i, p)
                    for p in range(2):
                        z_load(KT // 2 - 1, p)
                    load_ahead(sp, ssm_tiles_of(0), pe_v, KT // 2 - 1, CONV)

                @block.gpsimd
                def _(g):
                    g.memset(padded[:, :, 0:PAD], 0.0).then_inc(pad_zero, 1)
                    pool_v.ready(g)
                    with g.Fori(0, KT // 2) as i:
                        for p in range(2):
                            dve_v.wait(g, f"side{1 - p}", i, back=int(p == 0))
                            for j in range(1, SIDE):
                                act_v.wait(g, f"m{j}_{p}", i)
                                if j > 1:
                                    pool_v.wait(g, f"s{j - 1}_{p}", i)
                                pool_v.mark(g.tensor_tensor(side[:, :], product[:, 0, :] if j == 1 else side[:, :], product[:, j % 2, :], ALU.add), f"s{j}_{p}")

                @block.tensor
                def _(pe):
                    pe_v.ready(pe)
                    pe_z.ready(pe)

                    def conv_tiles(i, p):
                        pe.wait_ge(w_loaded[2 * p], (i + (q0 + 1)) * 16)
                        dve_v.wait(pe, f"cu{p}", i, back=1)
                        pe_v.mark(project(3 * p, hT, w=ring[:, 2 * p]), f"a{p}")
                        pe.wait_ge(w_loaded[2 * p + 1], (i + (q0 + 1)) * 16)
                        act_v.wait(pe, f"sig{1 - p}", i, back=int(p == 0))
                        pe_v.mark(project(1, hT, w=ring[:, 2 * p + 1]), f"b{p}")

                    def z_tile(i, p):
                        pe.wait_ge(z_loaded[p], (i + 1) * 16)
                        act_z.wait(pe, f"z{1 - p}", i, back=int(p == 0))
                        pe_z.mark(project(2, hT, w=z_ring[:, p]), f"z{p}")

                    for p in range(2):
                        conv_tiles(0, p)
                    with pe.Fori(1, KT // 2) as i:
                        for p in range(2):
                            conv_tiles(i, p)
                            z_tile(i - 1, p)
                    for p in range(2):
                        z_tile(KT // 2 - 1, p)

                @block.scalar
                def _(act):
                    act_v.ready(act)
                    act_z.ready(act)

                    def sigmoid(i, p):
                        pe_v.wait(act, f"b{p}", i)
                        dve_v.wait(act, f"cu{p}", i, back=1)
                        act_v.mark(act.activation(sig[:, p, :], pair(1), ACT.Sigmoid), f"sig{p}")
                        dve_v.wait(act, f"cu{p}", i)
                        for j in range(SIDE):
                            if j == 2:
                                pool_v.wait(act, f"s1_{p}", i)
                            elif j > 2:
                                pool_v.wait(act, f"s{j - 2}_{p}", i)
                            else:
                                pool_v.wait(act, f"s{SIDE - 1}_{1 - p}", i, back=int(p == 0))
                            act_v.mark(act.activation(product[:, j % 2, :], padded[:, p, j:j + S], ACT.Copy, scale=taps[:, p, j:j + 1]), f"m{j}_{p}")

                    def silu(i, p):
                        pe_z.wait(act, f"z{p}", i)
                        act_z.mark(act.activation(silu_zc[:, i * 2 + p, :], pair(2), ACT.Silu), f"z{p}")

                    for p in range(2):
                        sigmoid(0, p)
                    with act.Fori(1, KT // 2) as i:
                        for p in range(2):
                            sigmoid(i, p)
                            silu(i - 1, p)
                    for p in range(2):
                        silu(KT // 2 - 1, p)

                @block.vector
                def _(dve):
                    dve_v.ready(dve)
                    dve.wait_ge(pad_zero, 1)
                    with dve.Fori(0, KT // 2) as i:
                        for p in range(2):
                            n = i * 2 + p
                            act_v.wait(dve, f"m{SIDE - 1}_{p}", i, back=1)
                            dve.tensor_copy(taps[:, p, 0:16], vecs[:, 3, :].rearrange("p (j k) -> p k j", k=KT)[:, n, :])
                            dve_v.mark(dve.tensor_copy(taps[:, p, 16:TAPS31], vecs[:, 4, 0:15 * KT].rearrange("p (j k) -> p k j", k=KT)[:, n, :]), f"taps{p}")
                            act_v.wait(dve, f"sig{p}", i)
                            dve_v.mark(dve.tensor_tensor(padded[:, p, PAD:], pair(3 * p), sig[:, p, :], ALU.mult), f"cu{p}")
                            dve_v.wait(dve, f"cu{p}", i)
                            dve_v.mark(dve.tensor_scalar(yT[:, n, :], padded[:, p, SIDE:SIDE + S], taps[:, p, SIDE:SIDE + 1], vec("conv_b2", n),
                                                         ALU.mult, ALU.add), f"t{SIDE}_{p}")
                            for j in range(SIDE + 1, TAPS31):
                                dve_v.wait(dve, f"t{j - 1}_{p}", i)
                                dve_v.mark(dve.scalar_tensor_tensor(out=yT[:, n, :], in0=padded[:, p, j:j + S], scalar=taps[:, p, j:j + 1],
                                                                    in1=yT[:, n, :], op0=ALU.mult, op1=ALU.add), f"t{j}_{p}")
                            dve_v.wait(dve, f"t{TAPS31 - 1}_{p}", i)
                            pool_v.wait(dve, f"s{SIDE - 1}_{p}", i)
                            dve_v.mark(dve.tensor_tensor(yT[:, n, :], yT[:, n, :], side[:, :], ALU.add), f"side{p}")

        merged = sb("merged", [P, KT, S])
        with ExitStack() as scope:
            eps = sb("ln_eps", [P, 1], scope)
            sig = sb("ssm_sig", [P, 2, S], scope)
            sq, inv_std = merged[:, KT - 2:KT, :], merged[:, KT - 3, :]
            pe_n = Steps(sem("ln_pe"), ["sums"] + [f"sq{k}" for k in range(KT)])
            act_n = Steps(sem("ln_act"), [f"sq{k}" for k in range(KT)] + ["std"] + [f"silu{k}" for k in range(KT)])
            dve_n = Steps(sem("ln_dve"), [f"centred{k}" for k in range(KT)] + ["inv"] + [f"scaled{k}" for k in range(KT)])
            pool_n = Steps(sem("ln_pool"), ["eps"] + [f"z{k}" for k in range(KT)])
            pe_m = Steps(sem("ssm_pe"), [f"tile{b}" for b in range(4)])
            act_m = Steps(sem("ssm_act"), ["sig0", "sig1"])
            dve_m = Steps(sem("ssm_dve"), ["merged0", "merged1"])
            q0 = quads[0]
            quads[0] += KT // 2
            with nc.Block() as block:
                @block.sync
                def _(sp):
                    with sp.Fori(1, KT // 2) as i:
                        load_quad(sp, pe_m, i, ssm_tiles_of(i))
                    load_ahead(sp, merge_tiles_of(0), pe_m, KT // 2 - 1, TILES)

                @block.gpsimd
                def _(g):
                    pool_n.ready(g)
                    pool_n.mark(g.memset(eps[:, :], LN_EPS), "eps")
                    for k in range(KT):
                        act_n.wait(g, f"silu{k}")
                        pool_n.mark(g.tensor_tensor(yT[:, k, :], yT[:, k, :], silu_zc[:, k, :], ALU.mult), f"z{k}")

                @block.tensor
                def _(pe):
                    pe_n.ready(pe)
                    pe_m.ready(pe)

                    def gate_tile(i, p):
                        pe.wait_ge(w_loaded[2 * p], (i + (q0 + 1)) * 16)
                        act_m.wait(pe, f"sig{1 - p}", i, back=int(p == 0))
                        pe_m.mark(project(2, hT, w=ring[:, 2 * p]), f"tile{2 * p}")

                    def ssm_tile(i, p):
                        pe.wait_ge(w_loaded[2 * p + 1], (i + (q0 + 1)) * 16)
                        dve_m.wait(pe, f"merged{1 - p}", i, back=int(p == 0))
                        pe_m.mark(project(3, ssm_y, ST, w=ring[:, 2 * p + 1]), f"tile{2 * p + 1}")

                    for k in range(KT):
                        for h in range(2):
                            last = nc.tensor.matmul(bank[:, 2 + h, :], ones[:, :], yT[:, k, h * HALF:(h + 1) * HALF], start=(k == 0), stop=(k == KT - 1))
                    pe_n.mark(last, "sums")
                    gate_tile(0, 0)
                    ssm_tile(0, 0)
                    for k in range(KT):
                        act_n.wait(pe, f"sq{k}")
                        for h in range(2):
                            last = nc.tensor.matmul(bank[:, h, :], ones[:, :], sq[:, k % 2, h * HALF:(h + 1) * HALF], start=(k == 0), stop=(k == KT - 1))
                        pe_n.mark(last, f"sq{k}")
                    gate_tile(0, 1)
                    ssm_tile(0, 1)
                    with pe.Fori(1, KT // 2) as i:
                        for p in range(2):
                            gate_tile(i, p)
                            ssm_tile(i, p)

                @block.scalar
                def _(act):
                    act_n.ready(act)
                    act_m.ready(act)

                    def gate(i, p):
                        pe_m.wait(act, f"tile{2 * p}", i)
                        dve_m.wait(act, f"merged{p}", i, back=1)
                        act_m.mark(act.activation(sig[:, p, :], pair(2), ACT.Sigmoid), f"sig{p}")

                    for k in range(KT):
                        if k == 2:
                            gate(0, 0)
                        dve_n.wait(act, f"centred{k}")
                        if k >= 2:
                            pe_n.wait(act, f"sq{k - 2}")
                        act_n.mark(act.activation(sq[:, k % 2, :], yT[:, k, :], ACT.Square), f"sq{k}")
                    pool_n.wait(act, "eps")
                    pe_n.wait(act, f"sq{KT - 1}")
                    act_n.mark(act.activation(inv_std, pair(0), ACT.Sqrt, bias=eps[:, 0:1], scale=1.0 / D), "std")
                    gate(0, 1)
                    for k in range(KT):
                        dve_n.wait(act, f"scaled{k}")
                        act_n.mark(act.activation(yT[:, k, :], yT[:, k, :], ACT.Silu, scale=vec("ln_g", k), bias=vec("ln_b", k)), f"silu{k}")
                    with act.Fori(1, KT // 2) as i:
                        for p in range(2):
                            gate(i, p)

                @block.vector
                def _(dve):
                    dve_n.ready(dve)
                    dve_m.ready(dve)

                    def merge(i, p):
                        pe_m.wait(dve, f"tile{2 * p + 1}", i)
                        act_m.wait(dve, f"sig{p}", i)
                        dve_m.mark(dve.tensor_tensor(merged[:, i * 2 + p, :], pair(3), sig[:, p, :], ALU.mult), f"merged{p}")

                    pe_n.wait(dve, "sums")
                    for k in range(KT):
                        dve_n.mark(dve.scalar_tensor_tensor(out=yT[:, k, :], in0=pair(1), scalar=-1.0 / D, in1=yT[:, k, :],
                                                            op0=ALU.mult, op1=ALU.add), f"centred{k}")
                    merge(0, 0)
                    act_n.wait(dve, "std")
                    dve_n.mark(dve.reciprocal(inv_std, inv_std), "inv")
                    dve_n.wait(dve, "inv")
                    for k in range(KT):
                        dve_n.mark(dve.tensor_tensor(yT[:, k, :], yT[:, k, :], inv_std, ALU.mult), f"scaled{k}")
                    merge(0, 1)
                    dve_n.wait(dve, f"scaled{KT - 1}")
                    with dve.Fori(1, KT // 2) as i:
                        for p in range(2):
                            merge(i, p)

        post_w = silu_zc[:, :, :].rearrange("p k (c n) -> p k c n", c=2)
        post_w_loaded = [sem("post_w_loaded0"), sem("post_w_loaded1")]
        with ExitStack() as scope:
            sig, branch = ssm_y[:, 0:2, :], ssm_y[:, 2, :]
            pe_m = Steps(sem("merge_pe"), [f"tile{b}" for b in range(4)])
            act_m = Steps(sem("merge_act"), ["sig0", "sig1"])
            dve_m = Steps(sem("merge_dve"), ["gated0", "merged0", "gated1", "merged1"])
            q0 = quads[0]
            quads[0] += KT // 2
            with nc.Block() as block:
                @block.sync
                def _(sp):
                    with sp.Fori(1, KT // 2) as i:
                        load_quad(sp, pe_m, i, merge_tiles_of(i))
                    for c in range(2):
                        sp.dma_start(post_w[:, :, c, :], a["w_out_2"][0].rearrange("(k p) (c n) -> p k c n", p=P, c=2)[:, :, c, :]) \
                            .then_inc(post_w_loaded[c], 16)

                @block.tensor
                def _(pe):
                    pe_m.ready(pe)
                    with pe.Fori(0, KT // 2) as i:
                        for p in range(2):
                            pe.wait_ge(w_loaded[2 * p], (i + (q0 + 1)) * 16)
                            act_m.wait(pe, f"sig{p}", i, back=1)
                            pe_m.mark(project(2 * p, hT, w=ring[:, 2 * p]), f"tile{2 * p}")
                            pe.wait_ge(w_loaded[2 * p + 1], (i + (q0 + 1)) * 16)
                            dve_m.wait(pe, f"gated{p}", i, back=1)
                            pe_m.mark(project(2 * p + 1, yT, w=ring[:, 2 * p + 1]), f"tile{2 * p + 1}")

                @block.scalar
                def _(act):
                    act_m.ready(act)
                    with act.Fori(0, KT // 2) as i:
                        for p in range(2):
                            pe_m.wait(act, f"tile{2 * p}", i)
                            dve_m.wait(act, f"gated{p}", i, back=1)
                            act_m.mark(act.activation(sig[:, p, :], pair(2 * p), ACT.Sigmoid), f"sig{p}")

                @block.vector
                def _(dve):
                    dve_m.ready(dve)
                    with dve.Fori(0, KT // 2) as i:
                        for p in range(2):
                            m_n = merged[:, i * 2 + p, :]
                            pe_m.wait(dve, f"tile{2 * p + 1}", i)
                            act_m.wait(dve, f"sig{p}", i)
                            dve_m.wait(dve, f"merged{1 - p}", i, back=int(p == 0))
                            dve_m.mark(dve.tensor_tensor(branch, pair(2 * p + 1), sig[:, p, :], ALU.mult), f"gated{p}")
                            dve_m.wait(dve, f"gated{p}", i)
                            dve_m.mark(dve.tensor_tensor(m_n, m_n, branch, ALU.add), f"merged{p}")

        with ExitStack() as scope:
            gain = sb("post_gain", [P, D], scope)
            junk = sb("post_junk", [P, D], scope)
            stat = sb("post_stat", [P, 2, TT], scope)
            eps = sb("post_eps", [P, 1], scope)
            gain_loaded, out_stored = sem("post_gain_loaded"), sem("out_stored")
            pe_p = Steps(sem("post_pe"), [f"tok{t}" for t in range(TT)])
            act_p = Steps(sem("post_act"), [f"{s}{t}" for t in range(TT) for s in ("sq", "rms")])
            dve_p = Steps(sem("post_dve"), [f"{s}{t}" for t in range(TT) for s in ("inv", "scaled", "out")])
            pool_p = Steps(sem("post_pool"), ["eps"])
            with nc.Block() as block:
                @block.sync
                def _(sp):
                    sp.dma_start(gain[:, :], a["post_norm_gain_2"][0].partition_broadcast(P)).then_inc(gain_loaded, 16)
                    for t in range(TT):
                        dve_p.wait(sp, f"out{t}")
                        sp.dma_start(out[0, t * P:(t + 1) * P, :], hT[:, t, :]).then_inc(out_stored, 16)
                    sp.wait_ge(out_stored, 16 * TT)

                @block.gpsimd
                def _(g):
                    pool_p.ready(g)
                    pool_p.mark(g.memset(eps[:, :], EPS), "eps")

                @block.tensor
                def _(pe):
                    pe_p.ready(pe)
                    for c in range(2):
                        pe.wait_ge(post_w_loaded[c], 16)
                    for t in range(TT):
                        if t >= 4:
                            dve_p.wait(pe, f"scaled{t - 4}")
                        for c in range(2):
                            for k in range(KT):
                                last = nc.tensor.matmul(bank[:, 2 * (t % 4) + c, :], merged[:, k, t * P:(t + 1) * P], post_w[:, k, c, :],
                                                        start=(k == 0), stop=(k == KT - 1))
                        pe_p.mark(last, f"tok{t}")

                @block.scalar
                def _(act):
                    act_p.ready(act)
                    pool_p.wait(act, "eps")
                    for t in range(TT):
                        pe_p.wait(act, f"tok{t}")
                        act_p.mark(act.activation(junk[:, :], pair(t % 4), ACT.Square, accum_out=stat[:, 0, t:t + 1]), f"sq{t}")
                        act_p.wait(act, f"sq{t}")
                        act_p.mark(act.activation(stat[:, 1, t:t + 1], stat[:, 0, t:t + 1], ACT.Sqrt, bias=eps[:, 0:1], scale=1.0 / D), f"rms{t}")

                @block.vector
                def _(dve):
                    dve_p.ready(dve)
                    dve.wait_ge(gain_loaded, 16)
                    for t in range(TT):
                        act_p.wait(dve, f"rms{t}")
                        dve_p.mark(dve.reciprocal(stat[:, 1, t:t + 1], stat[:, 1, t:t + 1]), f"inv{t}")
                        dve_p.wait(dve, f"inv{t}")
                        dve_p.mark(dve.scalar_tensor_tensor(out=hT[:, t, :], in0=pair(t % 4), scalar=stat[:, 1, t:t + 1], in1=gain[:, :],
                                                            op0=ALU.mult, op1=ALU.mult), f"scaled{t}")
                        dve_p.wait(dve, f"scaled{t}")
                        dve_p.mark(dve.tensor_tensor(hT[:, t, :], hT[:, t, :], resid[:, t, :], ALU.add), f"out{t}")


_OUT_SHAPE = (1, S, D)


def kernel(**inputs):
    import concourse.bacc as bacc
    from concourse.bass_utils import run_bass_kernel_spmd

    nc = bacc.Bacc("TRN2", target_bir_lowering=False, num_devices=1)
    arrays, patterns = {}, {}
    for name, value in inputs.items():
        arrays[f"in_{name}"] = np.ascontiguousarray(value)
        patterns[name] = nc.dram_tensor(f"in_{name}", arrays[f"in_{name}"].shape, F32, kind="ExternalInput").ap()
    out = nc.dram_tensor("out", _OUT_SHAPE, F32, kind="ExternalOutput").ap()
    block_program(nc, patterns, out)
    return run_bass_kernel_spmd(nc, [arrays], core_ids=[0]).results[0]["out"]
```
